# Optimizing a Trainium2 kernel written in Bass

```python
import math
import jax, jax.numpy as jnp
from jax import lax
import numpy as np
import jax
import jax.numpy as jnp

D_MODEL = 1024
BATCH = 1
SEQ = 256
DEPTH = 2

GRID_W = 64
CTX_LEN = 256
N_MIXERS = 3
D_FF = 4 * D_MODEL
DEEPNORM_ALPHA = (2 * DEPTH) ** 0.25
DEEPNORM_BETA = (8 * DEPTH) ** -0.25
LN_EPS = 1e-5
RMS_EPS = 1e-6

GLA_HEADS = 4
GLA_DK = D_MODEL // 2
GLA_DV = D_MODEL
GLA_HK = GLA_DK // GLA_HEADS
GLA_HV = GLA_DV // GLA_HEADS
GLA_RANK = 16
GLA_GATE_NORM = 16.0
GLA_CHUNK = 64
GLA_IN = 2 * GLA_DK + 2 * GLA_DV + 2 * GLA_RANK

SSD_DI = 2 * D_MODEL
SSD_HEADDIM = 64
SSD_HEADS = SSD_DI // SSD_HEADDIM
SSD_GROUPS = 8
SSD_REP = SSD_HEADS // SSD_GROUPS
SSD_STATE = 128
SSD_CONV = 5
SSD_CHUNK = 64
SSD_GN = SSD_GROUPS * SSD_STATE
SSD_CONV_DIM = SSD_DI + 2 * SSD_GN
SSD_IN = SSD_DI + SSD_CONV_DIM + 2 * SSD_HEADS

HY_ORDER = 2
HY_SHORT = 3
HY_EMB = 33
HY_FW = 64
HY_DECAY_TARGET = 1e-2
HY_FAST_DECAY = 0.3
HY_SLOW_DECAY = 1.5
HY_FILTER_GAIN = 0.05


def layer_norm(h, g, b):
    hf = h.astype(jnp.float32)
    mu = jnp.mean(hf, -1, keepdims=True)
    var = jnp.mean(jnp.square(hf - mu), -1, keepdims=True)
    return ((hf - mu) * lax.rsqrt(var + LN_EPS) * g + b).astype(h.dtype)

def rms_norm(h, g):
    hf = h.astype(jnp.float32)
    return (hf * lax.rsqrt(jnp.mean(hf * hf, -1, keepdims=True) + RMS_EPS) * g).astype(h.dtype)

def modulate(h, shift, scale):
    return h * (1 + scale) + shift

def snake(h):
    b, l, ch = h.shape
    rows = l // GRID_W
    g = h.reshape(b, rows, GRID_W, ch)
    odd = (jnp.arange(rows) % 2 == 1)[None, :, None, None]
    return jnp.where(odd, g[:, :, ::-1], g).reshape(b, l, ch)

def dwconv(u, w, bias):
    k, ch = w.shape
    out = lax.conv_general_dilated(u, w.astype(u.dtype)[:, None, :], window_strides=(1,),
                                   padding=[(k // 2, k // 2)],
                                   dimension_numbers=('NWC', 'WIO', 'NWC'),
                                   feature_group_count=ch)
    return out + bias

def to_heads(t, dh):
    b, l, _ = t.shape
    return t.reshape(b, l, -1, dh).transpose(0, 2, 1, 3)

def sq_relu_mlp(h, w1, w2):
    return jnp.square(jax.nn.relu(h @ w1)) @ w2

def gla_chunk_scan(q, k, v, log_a, s0):
    b, h, l, _ = q.shape
    nc = l // GLA_CHUNK

    def chunks(t):
        return jnp.moveaxis(t.reshape(b, h, nc, GLA_CHUNK, t.shape[-1]), 2, 0)

    mask = jnp.tril(jnp.ones((GLA_CHUNK, GLA_CHUNK), dtype=bool))[:, :, None]

    def step(s, inp):
        qi, ki, vi, gi = inp
        cum = jnp.cumsum(gi, axis=2)
        diff = cum[:, :, :, None, :] - cum[:, :, None, :, :]
        decay = jnp.exp(jnp.where(mask, diff, -jnp.inf))
        attn = jnp.einsum('bhid,bhjd,bhijd->bhij', qi, ki, decay)
        o = jnp.einsum('bhij,bhjv->bhiv', attn, vi) + jnp.einsum('bhid,bhdv->bhiv', qi * jnp.exp(cum), s)
        last = cum[:, :, -1:, :]
        s_new = s * jnp.exp(last[:, :, 0, :, None]) + jnp.einsum('bhjd,bhjv->bhdv', ki * jnp.exp(last - cum), vi)
        return s_new, o

    s_fin, oc = lax.scan(step, s0, tuple(map(chunks, (q, k, v, log_a))))
    return jnp.moveaxis(oc, 0, 2).reshape(b, h, l, v.shape[-1]), s_fin

def gla_mixer(uc, ul, w_in, w_a2, b_a2, norm_g, w_out, need_ctx):
    split_at = [GLA_DK, 2 * GLA_DK, 2 * GLA_DK + GLA_DV, 2 * GLA_DK + 2 * GLA_DV]

    def run(h, s_init, need_y):
        b, l, _ = h.shape
        q, k, v, g, a = jnp.split(h @ w_in, split_at, axis=-1)
        q = to_heads(q, GLA_HK) * GLA_HK ** -0.5
        k = to_heads(k, GLA_HK)
        v = to_heads(v, GLA_HV)
        logit = jnp.einsum('blzr,zrd->zbld', a.reshape(b, l, 2, GLA_RANK), w_a2) + b_a2[:, None, None, :]
        log_a = jax.nn.log_sigmoid(logit.astype(jnp.float32)) / GLA_GATE_NORM
        o_f, s_f = gla_chunk_scan(q, k, v, to_heads(log_a[0], GLA_HK), s_init[0])
        o_b, s_b = gla_chunk_scan(q[:, :, ::-1], k[:, :, ::-1], v[:, :, ::-1],
                                  to_heads(log_a[1], GLA_HK)[:, :, ::-1], s_init[1])
        if not need_y:
            return None, (s_f, s_b)
        o = rms_norm(o_f + o_b[:, :, ::-1], norm_g)
        o = o.transpose(0, 2, 1, 3).reshape(b, l, GLA_DV)
        return (o * jax.nn.silu(g)) @ w_out, (s_f, s_b)

    zeros = jnp.zeros((uc.shape[0], GLA_HEADS, GLA_HK, GLA_HV), jnp.float32)
    yc, ctx_states = run(uc, (zeros, zeros), need_ctx)
    yl, _ = run(ul, ctx_states, True)
    return yc, yl

def ssd_chunk_scan(xs, dt, a, bm, cm, s0):
    b, l = xs.shape[:2]
    nc = l // SSD_CHUNK

    def chunks(t):
        return jnp.moveaxis(t.reshape(b, nc, SSD_CHUNK, *t.shape[2:]), 1, 0)

    mask = jnp.tril(jnp.ones((SSD_CHUNK, SSD_CHUNK), dtype=bool))[None, :, :, None, None]

    def step(s, inp):
        xi, dti, bi, ci = inp
        cum = jnp.cumsum(dti * a, axis=1)
        seg = cum[:, :, None] - cum[:, None, :]
        decay = jnp.exp(jnp.where(mask, seg, -jnp.inf))
        xdt = xi * dti[..., None]
        cb = jnp.einsum('bign,bjgn->bijg', ci, bi)
        y = jnp.einsum('bijg,bijgr,bjgrp->bigrp', cb, decay, xdt)
        y = y + jnp.einsum('bign,bigr,bgrpn->bigrp', ci, jnp.exp(cum), s)
        last = cum[:, -1]
        s_new = s * jnp.exp(last)[..., None, None] + jnp.einsum(
            'bjgn,bjgr,bjgrp->bgrpn', bi, jnp.exp(last[:, None] - cum), xdt)
        return s_new, y

    s_fin, ys = lax.scan(step, s0, tuple(map(chunks, (xs, dt, bm, cm))))
    return jnp.moveaxis(ys, 0, 1).reshape(xs.shape), s_fin

def ssd_mixer(uc, ul, w_in, conv_w, conv_b, dt_bias, a_log, d_skip, norm_g, w_out, need_ctx):
    a = (-jnp.exp(a_log.astype(jnp.float32))).reshape(2, SSD_GROUPS, SSD_REP)
    d_gr = d_skip.reshape(SSD_GROUPS, SSD_REP, 1)

    def run(h, s_init, need_y):
        b, l, _ = h.shape
        z, xbc, dt = jnp.split(h @ w_in, [SSD_DI, SSD_DI + SSD_CONV_DIM], axis=-1)
        xbc = jax.nn.silu(dwconv(xbc, conv_w, conv_b))
        xs, bm, cm = jnp.split(xbc, [SSD_DI, SSD_DI + SSD_GN], axis=-1)
        xs = xs.reshape(b, l, SSD_GROUPS, SSD_REP, SSD_HEADDIM)
        bm = bm.reshape(b, l, SSD_GROUPS, SSD_STATE)
        cm = cm.reshape(b, l, SSD_GROUPS, SSD_STATE)
        dt = jax.nn.softplus(dt.astype(jnp.float32).reshape(b, l, 2, SSD_GROUPS, SSD_REP)
                             + dt_bias.reshape(2, SSD_GROUPS, SSD_REP))
        y_f, s_f = ssd_chunk_scan(xs, dt[:, :, 0], a[0], bm, cm, s_init[0])
        y_b, s_b = ssd_chunk_scan(xs[:, ::-1], dt[:, ::-1, 1], a[1], bm[:, ::-1], cm[:, ::-1], s_init[1])
        if not need_y:
            return None, (s_f, s_b)
        y = (y_f + y_b[:, ::-1] + xs * d_gr).reshape(b, l, SSD_DI)
        return rms_norm(y * jax.nn.silu(z), norm_g) @ w_out, (s_f, s_b)

    zeros = jnp.zeros((uc.shape[0], SSD_GROUPS, SSD_REP, SSD_HEADDIM, SSD_STATE), jnp.float32)
    yc, ctx_states = run(uc, (zeros, zeros), need_ctx)
    yl, _ = run(ul, ctx_states, True)
    return yc, yl

def hyena_pos_emb(l):
    bands = (HY_EMB - 1) // 2
    t = jnp.linspace(0.0, 1.0, l)[:, None]
    w = 2 * math.pi * jnp.arange(l, dtype=jnp.float32)[:, None] / l
    ang = jnp.linspace(1e-4, bands - 1, bands)[None, :] * w
    return jnp.concatenate([t, jnp.cos(ang), -jnp.sin(ang)], axis=-1)

def hyena_filters(l, f_w1, f_b1, f_w2, f_b2, f_w3, f_b3, f_w4, f_freq):
    act = lambda t: jnp.sin(f_freq * t)
    hh = act(hyena_pos_emb(l) @ f_w1 + f_b1)
    hh = act(hh @ f_w2 + f_b2)
    hh = act(hh @ f_w3 + f_b3)
    hh = (hh @ f_w4).reshape(l, HY_ORDER, 2, D_MODEL)
    t = jnp.linspace(0.0, 1.0, l)[:, None]
    deltas = jnp.abs(jnp.linspace(math.log(HY_DECAY_TARGET) / HY_FAST_DECAY,
                                  math.log(HY_DECAY_TARGET) / HY_SLOW_DECAY, D_MODEL))
    hh = hh * jnp.exp(-t * deltas)[:, None, None, :]
    fwd, bwd = hh[:, :, 0], hh[:, :, 1]
    return jnp.concatenate([fwd, jnp.zeros_like(fwd[:1]), bwd[:0:-1]], axis=0)

def fft_long_conv(u, h2l, bias):
    l = u.shape[1]
    uf = jnp.fft.rfft(u.astype(jnp.float32), n=2 * l, axis=1)
    hf = jnp.fft.rfft(h2l.astype(jnp.float32), n=2 * l, axis=0)
    y = jnp.fft.irfft(uf * hf, n=2 * l, axis=1)[:, :l]
    return (y + u * bias).astype(u.dtype)

def hyena_mixer(uc, ul, w_in, conv_w, conv_b, f_w1, f_b1, f_w2, f_b2, f_w3, f_b3, f_w4, f_freq,
                h_bias, w_out, need_ctx):
    def run(h):
        l = h.shape[1]
        v, x1, x2 = jnp.split(dwconv(h @ w_in, conv_w, conv_b), 3, axis=-1)
        filt = hyena_filters(l, f_w1, f_b1, f_w2, f_b2, f_w3, f_b3, f_w4, f_freq)
        z = x1 * fft_long_conv(v, filt[:, 0], h_bias[0])
        return (x2 * fft_long_conv(z, filt[:, 1], h_bias[1])) @ w_out

    yc = run(uc) if need_ctx else None
    return yc, run(ul)

def first_inputs(seed: int = 0) -> dict:
    key = jax.random.key(seed)
    ks = iter(jax.random.split(key, 40))
    nrm = lambda shape, s: jax.random.normal(next(ks), shape, jnp.float32) * s
    uni = lambda shape, lo, hi: jax.random.uniform(next(ks), shape, jnp.float32, minval=lo, maxval=hi)
    inv_softplus = lambda y: y + jnp.log(-jnp.expm1(-y))
    D = D_MODEL
    ng, ns, nh = (len(range(m, DEPTH, N_MIXERS)) for m in range(N_MIXERS))
    return {
        'x': nrm((BATCH, SEQ, D), 1.0),
        'c': nrm((BATCH, D), 1.0),
        'ctx': nrm((BATCH, CTX_LEN, D), 1.0),
        'c_ctx': nrm((D,), 1.0),
        'ada_w': nrm((DEPTH, D, 6 * D), D ** -0.5),
        'ada_b': nrm((DEPTH, 6 * D), 0.02),
        'ln_g': 1.0 + nrm((DEPTH, 2, D), 0.02),
        'ln_b': nrm((DEPTH, 2, D), 0.02),
        'ffn_w1': nrm((DEPTH, D, D_FF), D ** -0.5),
        'ffn_w2': nrm((DEPTH, D_FF, D), D_FF ** -0.5 * DEEPNORM_BETA),
        'gla_w_in': nrm((ng, D, GLA_IN), D ** -0.5),
        'gla_w_a2': nrm((ng, 2, GLA_RANK, GLA_DK), GLA_RANK ** -0.5),
        'gla_b_a2': nrm((ng, 2, GLA_DK), 0.1),
        'gla_norm': 1.0 + nrm((ng, GLA_HV), 0.02),
        'gla_w_out': nrm((ng, GLA_DV, D), GLA_DV ** -0.5 * DEEPNORM_BETA),
        'ssd_w_in': nrm((ns, D, SSD_IN), D ** -0.5),
        'ssd_conv_w': nrm((ns, SSD_CONV, SSD_CONV_DIM), SSD_CONV ** -0.5),
        'ssd_conv_b': nrm((ns, SSD_CONV_DIM), 0.02),
        'ssd_dt_bias': inv_softplus(jnp.exp(uni((ns, 2, SSD_HEADS), math.log(1e-3), math.log(1e-1)))),
        'ssd_a_log': jnp.log(uni((ns, 2, SSD_HEADS), 1.0, 16.0)),
        'ssd_d': 1.0 + nrm((ns, SSD_HEADS), 0.1),
        'ssd_norm': 1.0 + nrm((ns, SSD_DI), 0.02),
        'ssd_w_out': nrm((ns, SSD_DI, D), SSD_DI ** -0.5 * DEEPNORM_BETA),
        'hy_w_in': nrm((nh, D, 3 * D), D ** -0.5),
        'hy_conv_w': nrm((nh, HY_SHORT, 3 * D), HY_SHORT ** -0.5),
        'hy_conv_b': nrm((nh, 3 * D), 0.02),
        'hy_f_w1': nrm((nh, HY_EMB, HY_FW), HY_EMB ** -0.5),
        'hy_f_b1': nrm((nh, HY_FW), 0.1),
        'hy_f_w2': nrm((nh, HY_FW, HY_FW), HY_FW ** -0.5),
        'hy_f_b2': nrm((nh, HY_FW), 0.1),
        'hy_f_w3': nrm((nh, HY_FW, HY_FW), HY_FW ** -0.5),
        'hy_f_b3': nrm((nh, HY_FW), 0.1),
        'hy_f_w4': nrm((nh, HY_FW, HY_ORDER * 2 * D), HY_FW ** -0.5 * HY_FILTER_GAIN),
        'hy_f_freq': 1.0 + nrm((nh, HY_FW), 0.1),
        'hy_bias': nrm((nh, HY_ORDER, D), 1.0),
        'hy_w_out': nrm((nh, D, D), D ** -0.5 * DEEPNORM_BETA),
    }

def first_block(x, c, ctx, c_ctx, ada_w, ada_b, ln_g, ln_b, ffn_w1, ffn_w2,
              gla_w_in, gla_w_a2, gla_b_a2, gla_norm, gla_w_out,
              ssd_w_in, ssd_conv_w, ssd_conv_b, ssd_dt_bias, ssd_a_log, ssd_d, ssd_norm, ssd_w_out,
              hy_w_in, hy_conv_w, hy_conv_b, hy_f_w1, hy_f_b1, hy_f_w2, hy_f_b2, hy_f_w3, hy_f_b3,
              hy_f_w4, hy_f_freq, hy_bias, hy_w_out):
    hl, hc = x, ctx
    s_lat = jax.nn.silu(c)
    s_ctx = jax.nn.silu(c_ctx)
    for i in range(DEPTH):
        kind, j = i % N_MIXERS, i // N_MIXERS
        need_ctx = i < DEPTH - 1
        m_l = jnp.split((s_lat @ ada_w[i] + ada_b[i])[:, None, :], 6, axis=-1)
        m_c = jnp.split(s_ctx @ ada_w[i] + ada_b[i], 6, axis=-1)
        ul = snake(modulate(hl, m_l[0], m_l[1]))
        uc = modulate(hc, m_c[0], m_c[1])
        if kind == 0:
            yc, yl = gla_mixer(uc, ul, gla_w_in[j], gla_w_a2[j], gla_b_a2[j], gla_norm[j], gla_w_out[j], need_ctx)
        elif kind == 1:
            yc, yl = ssd_mixer(uc, ul, ssd_w_in[j], ssd_conv_w[j], ssd_conv_b[j], ssd_dt_bias[j],
                               ssd_a_log[j], ssd_d[j], ssd_norm[j], ssd_w_out[j], need_ctx)
        else:
            yc, yl = hyena_mixer(uc, ul, hy_w_in[j], hy_conv_w[j], hy_conv_b[j], hy_f_w1[j], hy_f_b1[j],
                                 hy_f_w2[j], hy_f_b2[j], hy_f_w3[j], hy_f_b3[j], hy_f_w4[j], hy_f_freq[j],
                                 hy_bias[j], hy_w_out[j], need_ctx)
        hl = layer_norm(DEEPNORM_ALPHA * hl + m_l[2] * snake(yl), ln_g[i, 0], ln_b[i, 0])
        hl = layer_norm(DEEPNORM_ALPHA * hl + m_l[5] * sq_relu_mlp(modulate(hl, m_l[3], m_l[4]), ffn_w1[i], ffn_w2[i]),
                        ln_g[i, 1], ln_b[i, 1])
        if need_ctx:
            hc = layer_norm(DEEPNORM_ALPHA * hc + m_c[2] * yc, ln_g[i, 0], ln_b[i, 0])
            hc = layer_norm(DEEPNORM_ALPHA * hc + m_c[5] * sq_relu_mlp(modulate(hc, m_c[3], m_c[4]), ffn_w1[i], ffn_w2[i]),
                            ln_g[i, 1], ln_b[i, 1])
    return hl


HEAD_DIM = 64
N_SLOTS = D_MODEL // HEAD_DIM
CONV_CH = D_MODEL // 2
CONV_W = 3
NA_HEADS = N_SLOTS // 2
NA_ROWS = 8
NA_COLS = 16
SWA_HEADS = N_SLOTS // 2
SWA_KV_HEADS = max(1, SWA_HEADS // 4)
SWA_WINDOW = 128
BLOCK = 128
DIFF_HEADS = N_SLOTS // 4
D_FF_2 = 256 * math.ceil(8 * D_MODEL / 3 / 256)
N_EXPERTS = 8
TOP_K = 2
D_FF_EXPERT = D_FF_2 // 2
ROPE_THETA = 10000.0
EPS = 1e-6
NEG = -1e30
N_EVEN = (DEPTH + 1) // 2
N_ODD = DEPTH // 2
NA_W = NA_HEADS * HEAD_DIM
EV_Q = 3 * CONV_CH + NA_W
EV_KV = 2 * NA_W
EV_OUT = CONV_CH + NA_W
C_Q = SWA_HEADS * HEAD_DIM
C_KV = SWA_KV_HEADS * HEAD_DIM
D_QK = DIFF_HEADS * 2 * HEAD_DIM
D_V = DIFF_HEADS * 2 * HEAD_DIM
OD_Q = C_Q + D_QK
OD_KV = 2 * C_KV + D_QK + D_V
OD_OUT = C_Q + D_V


def rms_norm_2(x, g):
    xf = x.astype(jnp.float32)
    y = xf * lax.rsqrt(jnp.mean(xf * xf, -1, keepdims=True) + EPS)
    return (y * g.astype(jnp.float32)).astype(x.dtype)

def split_heads(t, h):
    b, n, _ = t.shape
    return t.reshape(b, n, h, -1).transpose(0, 2, 1, 3)

def merge_heads(t):
    b, h, n, d = t.shape
    return t.transpose(0, 2, 1, 3).reshape(b, n, h * d)

def rope_tables(n):
    t = jnp.arange(n)
    pos = jnp.stack([t // GRID_W, t % GRID_W], -1).astype(jnp.float32)
    nq = HEAD_DIM // 4
    inv = ROPE_THETA ** (-jnp.arange(nq, dtype=jnp.float32) / nq)
    ang = pos[:, :, None] * inv
    return jnp.cos(ang), jnp.sin(ang)

def apply_rope(x, cos, sin):
    shp = x.shape
    xr = x.reshape(shp[:-1] + (2, 2, HEAD_DIM // 4))
    a, b = xr[..., 0, :], xr[..., 1, :]
    cos = cos.astype(x.dtype)
    sin = sin.astype(x.dtype)
    return jnp.stack([a * cos - b * sin, b * cos + a * sin], -2).reshape(shp)

def joint_softmax(parts, extra=None):
    m = parts[0].max(-1, keepdims=True)
    for p in parts[1:]:
        m = jnp.maximum(m, p.max(-1, keepdims=True))
    if extra is not None:
        m = jnp.maximum(m, extra)
    es = [jnp.exp(p - m) for p in parts]
    den = es[0].sum(-1, keepdims=True)
    for e in es[1:]:
        den = den + e.sum(-1, keepdims=True)
    if extra is not None:
        den = den + jnp.exp(extra - m)
    return [e / den for e in es]

def dense_attention(q, k, v, sink=None):
    b, hq, lq, d = q.shape
    hkv = k.shape[1]
    g = hq // hkv
    qg = q.reshape(b, hkv, g, lq, d)
    s = jnp.einsum('bkgqd,bkld->bkgql', qg, k, preferred_element_type=jnp.float32) * d ** -0.5
    extra = None if sink is None else sink.astype(jnp.float32).reshape(1, hkv, g, 1, 1)
    (p,) = joint_softmax([s], extra)
    o = jnp.einsum('bkgql,bkld->bkgqd', p.astype(v.dtype), v)
    return o.reshape(b, hq, lq, d)

def dwconv3(u, w):
    return lax.conv_general_dilated(u, w[:, None, :].astype(u.dtype), window_strides=(1,),
                                    padding=[(1, 1)], dimension_numbers=('NWC', 'WIO', 'NWC'),
                                    feature_group_count=u.shape[-1])

def neighbourhood_attention(q, k, v, k_ctx, v_ctx, rpb):
    b, h, n, d = q.shape
    rows = n // GRID_W
    kh = min(NA_ROWS, rows)
    r = jnp.arange(rows)
    col = jnp.arange(GRID_W)
    r0 = jnp.clip(r - kh // 2, 0, rows - kh)
    row_idx = r0[:, None] + jnp.arange(kh)[None, :]
    c0 = jnp.clip(col - NA_COLS // 2, 0, GRID_W - NA_COLS)
    qg = q.reshape(b, h, rows, GRID_W, d)
    kg = k.reshape(b, h, rows, GRID_W, d)[:, :, row_idx]
    vg = v.reshape(b, h, rows, GRID_W, d)[:, :, row_idx]
    dr = row_idx - r[:, None] + NA_ROWS - 1
    dc = jnp.clip(col[None, :] - col[:, None] + NA_COLS - 1, 0, 2 * NA_COLS - 2)
    col_ok = (col[None, :] >= c0[:, None]) & (col[None, :] < c0[:, None] + NA_COLS)
    bias = rpb.astype(jnp.float32)[:, dr[:, None, :, None], dc[None, :, None, :]]
    bias = jnp.where(col_ok[None, None, :, None, :], bias, NEG)
    scale = d ** -0.5
    s_loc = jnp.einsum('bhrqd,bhrjkd->bhrqjk', qg, kg, preferred_element_type=jnp.float32) * scale + bias
    s_ctx = jnp.einsum('bhrqd,bhld->bhrql', qg, k_ctx, preferred_element_type=jnp.float32) * scale
    p_loc, p_ctx = joint_softmax([s_loc.reshape(b, h, rows, GRID_W, kh * GRID_W), s_ctx])
    p_loc = p_loc.reshape(b, h, rows, GRID_W, kh, GRID_W).astype(v.dtype)
    o = (jnp.einsum('bhrqjk,bhrjkd->bhrqd', p_loc, vg)
         + jnp.einsum('bhrql,bhld->bhrqd', p_ctx.astype(v.dtype), v_ctx))
    return o.reshape(b, h, n, d)

def window_gqa(q, k, v, k_ctx, v_ctx, sink):
    b, hq, n, d = q.shape
    hkv = k.shape[1]
    g = hq // hkv
    nb = n // BLOCK
    qb = q.reshape(b, hkv, g, nb, BLOCK, d)
    pad = ((0, 0), (0, 0), (BLOCK, BLOCK), (0, 0))
    band = (jnp.arange(nb) * BLOCK)[:, None] + jnp.arange(3 * BLOCK)[None, :]
    kb = jnp.pad(k, pad)[:, :, band]
    vb = jnp.pad(v, pad)[:, :, band]
    qpos = (jnp.arange(nb) * BLOCK)[:, None, None] + jnp.arange(BLOCK)[None, :, None]
    kpos = band[:, None, :] - BLOCK
    ok = (jnp.abs(kpos - qpos) <= SWA_WINDOW) & (kpos >= 0) & (kpos < n)
    scale = d ** -0.5
    s_loc = jnp.where(ok, jnp.einsum('bkgnqd,bknmd->bkgnqm', qb, kb, preferred_element_type=jnp.float32) * scale, NEG)
    s_ctx = jnp.einsum('bkgnqd,bkld->bkgnql', qb, k_ctx, preferred_element_type=jnp.float32) * scale
    extra = sink.astype(jnp.float32).reshape(1, hkv, g, 1, 1, 1)
    p_loc, p_ctx = joint_softmax([s_loc, s_ctx], extra)
    o = (jnp.einsum('bkgnqm,bknmd->bkgnqd', p_loc.astype(v.dtype), vb)
         + jnp.einsum('bkgnql,bkld->bkgnqd', p_ctx.astype(v.dtype), v_ctx))
    return o.reshape(b, hq, n, d)

def diff_attend(q, kvs, lam):
    scale = q.shape[-1] ** -0.5
    ss = [jnp.einsum('bhiqd,bhikd->bhiqk', q, k, preferred_element_type=jnp.float32) * scale for k, _ in kvs]
    ps = joint_softmax(ss)
    out = None
    for p, (_, v) in zip(ps, kvs):
        a = (p[:, :, 0] - lam * p[:, :, 1]).astype(v.dtype)
        o = jnp.einsum('bhqk,bhkd->bhqd', a, v)
        out = o if out is None else out + o
    return out

def diff_attention_latent(q, k, v, k_ctx, v_ctx, lam):
    b, h, _, n, d = q.shape
    nb = n // BLOCK
    qb = jnp.moveaxis(q.reshape(b, h, 2, nb, BLOCK, d), 3, 0)
    o = lax.map(lambda qi: diff_attend(qi, [(k, v), (k_ctx, v_ctx)], lam), qb)
    return jnp.moveaxis(o, 0, 2).reshape(b, h, n, v.shape[-1])

def swiglu(x, w1, w3, w2):
    return (jax.nn.silu(x @ w1) * (x @ w3)) @ w2

def moe_swiglu(x, router, w1, w3, w2):
    shp = x.shape
    xt = x.reshape(-1, shp[-1])
    logits = (xt @ router).astype(jnp.float32)
    top_v, top_i = lax.top_k(logits, TOP_K)
    top_w = jax.nn.softmax(top_v, axis=-1)
    gates = jnp.sum(jax.nn.one_hot(top_i, N_EXPERTS, dtype=jnp.float32) * top_w[..., None], axis=1)
    gates = gates.astype(x.dtype)
    out = gates[:, 0:1] * swiglu(xt, w1[0], w3[0], w2[0])
    for e in range(1, N_EXPERTS):
        out = out + gates[:, e:e + 1] * swiglu(xt, w1[e], w3[e], w2[e])
    return out.reshape(shp)

def even_mixer(h_lat, h_ctx, w_in, conv_w, q_g, k_g, rpb, w_out, need_ctx):
    def query_side(p):
        gb, gc, u, q = jnp.split(p, [CONV_CH, 2 * CONV_CH, 3 * CONV_CH], -1)
        y_conv = gb * dwconv3(gc * u, conv_w)
        return y_conv, rms_norm_2(split_heads(q, NA_HEADS), q_g)

    def kv_side(p):
        k, v = jnp.split(p, 2, -1)
        return rms_norm_2(split_heads(k, NA_HEADS), k_g), split_heads(v, NA_HEADS)

    p_lat = h_lat @ w_in
    yc_lat, q_lat = query_side(p_lat[..., :EV_Q])
    k_lat, v_lat = kv_side(p_lat[..., EV_Q:])
    p_ctx = h_ctx @ (w_in if need_ctx else w_in[:, EV_Q:])
    k_ctx, v_ctx = kv_side(p_ctx[..., -EV_KV:])
    y_na = merge_heads(neighbourhood_attention(q_lat, k_lat, v_lat, k_ctx, v_ctx, rpb))
    y_lat = jnp.concatenate([yc_lat, y_na], -1) @ w_out
    y_ctx = None
    if need_ctx:
        yc_ctx, q_ctx = query_side(p_ctx[..., :EV_Q])
        y_na_ctx = merge_heads(dense_attention(q_ctx, k_ctx, v_ctx))
        y_ctx = jnp.concatenate([yc_ctx, y_na_ctx], -1) @ w_out
    return y_lat, y_ctx

def odd_mixer(h_lat, h_ctx, w_in, cq_g, ck_g, sink, dq_g, dk_g, lam_q1, lam_k1, lam_q2, lam_k2,
              subln_g, w_out, lam_init, cos, sin, need_ctx):
    def diff_split(t):
        b, n, _ = t.shape
        return t.reshape(b, n, DIFF_HEADS, 2, HEAD_DIM).transpose(0, 2, 3, 1, 4)

    def query_side(p, rope):
        cq, dq = jnp.split(p, [C_Q], -1)
        cq = rms_norm_2(split_heads(cq, SWA_HEADS), cq_g)
        dq = rms_norm_2(diff_split(dq), dq_g)
        if rope:
            cq, dq = apply_rope(cq, cos, sin), apply_rope(dq, cos, sin)
        return cq, dq

    def kv_side(p, rope):
        ck, cv, dk, dv = jnp.split(p, [C_KV, 2 * C_KV, 2 * C_KV + D_QK], -1)
        ck = rms_norm_2(split_heads(ck, SWA_KV_HEADS), ck_g)
        dk = rms_norm_2(diff_split(dk), dk_g)
        if rope:
            ck, dk = apply_rope(ck, cos, sin), apply_rope(dk, cos, sin)
        return ck, split_heads(cv, SWA_KV_HEADS), dk, split_heads(dv, DIFF_HEADS)

    f32 = jnp.float32
    lam = (jnp.exp(jnp.sum(lam_q1.astype(f32) * lam_k1.astype(f32)))
           - jnp.exp(jnp.sum(lam_q2.astype(f32) * lam_k2.astype(f32))) + lam_init)

    def merge(yc, yd):
        yd = rms_norm_2(yd, subln_g) * (1.0 - lam_init)
        return jnp.concatenate([merge_heads(yc), merge_heads(yd)], -1) @ w_out

    p_lat = h_lat @ w_in
    cq_l, dq_l = query_side(p_lat[..., :OD_Q], True)
    ck_l, cv_l, dk_l, dv_l = kv_side(p_lat[..., OD_Q:], True)
    p_ctx = h_ctx @ (w_in if need_ctx else w_in[:, OD_Q:])
    ck_c, cv_c, dk_c, dv_c = kv_side(p_ctx[..., -OD_KV:], False)
    y_lat = merge(window_gqa(cq_l, ck_l, cv_l, ck_c, cv_c, sink),
                  diff_attention_latent(dq_l, dk_l, dv_l, dk_c, dv_c, lam))
    y_ctx = None
    if need_ctx:
        cq_c, dq_c = query_side(p_ctx[..., :OD_Q], False)
        y_ctx = merge(dense_attention(cq_c, ck_c, cv_c, sink), diff_attend(dq_c, [(dk_c, dv_c)], lam))
    return y_lat, y_ctx

def second_inputs(seed: int = 0) -> dict:
    key = jax.random.key(seed)
    ks = iter(jax.random.split(key, 40))
    D = D_MODEL

    def nrm(shape, scale=1.0):
        return jax.random.normal(next(ks), shape, jnp.float32) * scale

    def gain(shape):
        return 1.0 + nrm(shape, 0.05)

    return {
        'x': nrm((BATCH, SEQ, D)),
        'c': nrm((BATCH, D)),
        'ctx': nrm((BATCH, CTX_LEN, D)),
        'c_ctx': nrm((D,)),
        'ada_w': nrm((DEPTH, D, 6 * D), 0.5 * D ** -0.5),
        'ada_b': nrm((DEPTH, 6 * D), 0.02),
        'norm1_g': gain((DEPTH, D)),
        'norm2_g': gain((DEPTH, D)),
        'ev_w_in': nrm((N_EVEN, D, EV_Q + EV_KV), D ** -0.5),
        'ev_conv_w': nrm((N_EVEN, CONV_W, CONV_CH), CONV_W ** -0.5),
        'ev_q_g': gain((N_EVEN, HEAD_DIM)),
        'ev_k_g': gain((N_EVEN, HEAD_DIM)),
        'ev_rpb': nrm((N_EVEN, NA_HEADS, 2 * NA_ROWS - 1, 2 * NA_COLS - 1), 0.1),
        'ev_w_out': nrm((N_EVEN, EV_OUT, D), EV_OUT ** -0.5),
        'ffn_w1': nrm((N_EVEN, D, D_FF_2), D ** -0.5),
        'ffn_w3': nrm((N_EVEN, D, D_FF_2), D ** -0.5),
        'ffn_w2': nrm((N_EVEN, D_FF_2, D), D_FF_2 ** -0.5),
        'od_w_in': nrm((N_ODD, D, OD_Q + OD_KV), D ** -0.5),
        'od_cq_g': gain((N_ODD, HEAD_DIM)),
        'od_ck_g': gain((N_ODD, HEAD_DIM)),
        'od_sink': nrm((N_ODD, SWA_HEADS), 0.5),
        'od_dq_g': gain((N_ODD, HEAD_DIM)),
        'od_dk_g': gain((N_ODD, HEAD_DIM)),
        'od_lam_q1': nrm((N_ODD, HEAD_DIM), 0.1),
        'od_lam_k1': nrm((N_ODD, HEAD_DIM), 0.1),
        'od_lam_q2': nrm((N_ODD, HEAD_DIM), 0.1),
        'od_lam_k2': nrm((N_ODD, HEAD_DIM), 0.1),
        'od_subln_g': gain((N_ODD, 2 * HEAD_DIM)),
        'od_w_out': nrm((N_ODD, OD_OUT, D), OD_OUT ** -0.5),
        'moe_router': nrm((N_ODD, D, N_EXPERTS), D ** -0.5),
        'moe_w1': nrm((N_ODD, N_EXPERTS, D, D_FF_EXPERT), D ** -0.5),
        'moe_w3': nrm((N_ODD, N_EXPERTS, D, D_FF_EXPERT), D ** -0.5),
        'moe_w2': nrm((N_ODD, N_EXPERTS, D_FF_EXPERT, D), D_FF_EXPERT ** -0.5),
    }

def second_block(x, c, ctx, c_ctx, ada_w, ada_b, norm1_g, norm2_g, ev_w_in, ev_conv_w, ev_q_g, ev_k_g,
              ev_rpb, ev_w_out, ffn_w1, ffn_w3, ffn_w2, od_w_in, od_cq_g, od_ck_g, od_sink, od_dq_g,
              od_dk_g, od_lam_q1, od_lam_k1, od_lam_q2, od_lam_k2, od_subln_g, od_w_out, moe_router,
              moe_w1, moe_w3, moe_w2):
    n = x.shape[1]
    cos, sin = rope_tables(n)
    h, hc = x, ctx
    s_lat = jax.nn.silu(c)
    s_ctx = jax.nn.silu(c_ctx)
    for l in range(DEPTH):
        last = l == DEPTH - 1
        i = l // 2
        mod = (s_lat @ ada_w[l] + ada_b[l])[:, None, :]
        sh1, sc1, g1, sh2, sc2, g2 = jnp.split(mod, 6, -1)
        n_mod = 2 if last else 6
        modc = jnp.split(s_ctx @ ada_w[l][:, :n_mod * D_MODEL] + ada_b[l][:n_mod * D_MODEL], n_mod)
        a_lat = rms_norm_2(h, norm1_g[l]) * (1 + sc1) + sh1
        a_ctx = rms_norm_2(hc, norm1_g[l]) * (1 + modc[1]) + modc[0]
        if l % 2 == 0:
            y, yc = even_mixer(a_lat, a_ctx, ev_w_in[i], ev_conv_w[i], ev_q_g[i], ev_k_g[i], ev_rpb[i],
                               ev_w_out[i], not last)
            ffn = lambda t: swiglu(t, ffn_w1[i], ffn_w3[i], ffn_w2[i])
        else:
            lam_init = 0.8 - 0.6 * math.exp(-0.3 * l)
            y, yc = odd_mixer(a_lat, a_ctx, od_w_in[i], od_cq_g[i], od_ck_g[i], od_sink[i], od_dq_g[i],
                              od_dk_g[i], od_lam_q1[i], od_lam_k1[i], od_lam_q2[i], od_lam_k2[i],
                              od_subln_g[i], od_w_out[i], lam_init, cos, sin, not last)
            ffn = lambda t: moe_swiglu(t, moe_router[i], moe_w1[i], moe_w3[i], moe_w2[i])
        h = h + g1 * y
        h = h + g2 * ffn(rms_norm_2(h, norm2_g[l]) * (1 + sc2) + sh2)
        if not last:
            hc = hc + modc[2] * yc
            hc = hc + modc[5] * ffn(rms_norm_2(hc, norm2_g[l]) * (1 + modc[4]) + modc[3])
    return h


def setup_inputs(seed=0):
    out = dict(first_inputs(seed))
    for name, value in second_inputs(seed + 1).items():
        if name != "x":
            out[name + "_2"] = value
    return out


def reference(
    x, c, ctx, c_ctx, ada_w, ada_b, ln_g, ln_b, ffn_w1, ffn_w2, gla_w_in, gla_w_a2, gla_b_a2,
    gla_norm, gla_w_out, ssd_w_in, ssd_conv_w, ssd_conv_b, ssd_dt_bias, ssd_a_log, ssd_d,
    ssd_norm, ssd_w_out, hy_w_in, hy_conv_w, hy_conv_b, hy_f_w1, hy_f_b1, hy_f_w2, hy_f_b2,
    hy_f_w3, hy_f_b3, hy_f_w4, hy_f_freq, hy_bias, hy_w_out, c_2, ctx_2, c_ctx_2, ada_w_2,
    ada_b_2, norm1_g_2, norm2_g_2, ev_w_in_2, ev_conv_w_2, ev_q_g_2, ev_k_g_2, ev_rpb_2,
    ev_w_out_2, ffn_w1_2, ffn_w3_2, ffn_w2_2, od_w_in_2, od_cq_g_2, od_ck_g_2, od_sink_2,
    od_dq_g_2, od_dk_g_2, od_lam_q1_2, od_lam_k1_2, od_lam_q2_2, od_lam_k2_2, od_subln_g_2,
    od_w_out_2, moe_router_2, moe_w1_2, moe_w3_2, moe_w2_2,
):
    x = first_block(
        x, c, ctx, c_ctx, ada_w, ada_b, ln_g, ln_b, ffn_w1, ffn_w2, gla_w_in, gla_w_a2,
        gla_b_a2, gla_norm, gla_w_out, ssd_w_in, ssd_conv_w, ssd_conv_b, ssd_dt_bias, ssd_a_log,
        ssd_d, ssd_norm, ssd_w_out, hy_w_in, hy_conv_w, hy_conv_b, hy_f_w1, hy_f_b1, hy_f_w2,
        hy_f_b2, hy_f_w3, hy_f_b3, hy_f_w4, hy_f_freq, hy_bias, hy_w_out,
    )
    return second_block(
        x, c_2, ctx_2, c_ctx_2, ada_w_2, ada_b_2, norm1_g_2, norm2_g_2, ev_w_in_2, ev_conv_w_2,
        ev_q_g_2, ev_k_g_2, ev_rpb_2, ev_w_out_2, ffn_w1_2, ffn_w3_2, ffn_w2_2, od_w_in_2,
        od_cq_g_2, od_ck_g_2, od_sink_2, od_dq_g_2, od_dk_g_2, od_lam_q1_2, od_lam_k1_2,
        od_lam_q2_2, od_lam_k2_2, od_subln_g_2, od_w_out_2, moe_router_2, moe_w1_2, moe_w3_2,
        moe_w2_2,
    )


_drawn_inputs = setup_inputs


def setup_inputs(seed=0):
    import zlib

    import numpy as np

    out = dict(_drawn_inputs(seed))
    spreads = {}
    factors = {'gla_b_a2': 3.145,
     'gla_norm': 6.79,
     'ssd_conv_b': 6.527,
     'ssd_d': 5.824,
     'ssd_norm': 6.71,
     'ev_q_g_2': 8.0,
     'ev_k_g_2': 8.0,
     'ev_rpb_2': 8.0,
     'od_cq_g_2': 8.0,
     'od_ck_g_2': 8.0,
     'od_sink_2': 8.0,
     'od_dq_g_2': 8.0,
     'od_dk_g_2': 8.0,
     'od_lam_q2_2': 8.0,
     'od_lam_k2_2': 8.0,
     'od_subln_g_2': 4.792}
    for name, (base, spread) in spreads.items():
        noise = np.random.default_rng([zlib.crc32(name.encode()), seed]).standard_normal(out[name].shape)
        drawn = base * np.exp(spread * noise) if base else spread * noise
        out[name] = jnp.asarray(drawn.astype(out[name].dtype))
    for name, factor in factors.items():
        out[name] = (out[name] * factor).astype(out[name].dtype)
    return out
```

```python
from contextlib import ExitStack
import math

import numpy as np

import concourse.bass as bass
from concourse import mybir

F32 = mybir.dt.float32
ALU = mybir.AluOpType
ACT = mybir.ActivationFunctionType
AX = mybir.AxisListType

P = 128
D = 1024
KD = D // P
LAT = 256
CTX = 256
TOK = LAT + CTX
ROWS, GRID = 4, 64
ALPHA = 4 ** 0.25
LN_EPS, RMS_EPS = 1e-5, 1e-6
NBANK = 8
SLOTS = 4
SLOT = 4096
NEG = -1e30
ARENA = 23552

C_ID, C_TRIF, C_TRIB, C_ONE, C_HALF, C_ROT, C_DUP = 0, 128, 256, 384, 512, 640, 768
C_COL, C_SWA, C_COS, C_SIN, C_FLIP, C_END = 1024, 1088, 1600, 1856, 2112, 2240


def constants():
    c = np.zeros((P, C_END), np.float32)
    i = np.arange(P)
    c[:, C_ID:C_ID + P] = np.eye(P)
    c[:, C_TRIF:C_TRIF + P] = i[:, None] <= i[None, :]
    c[:, C_TRIB:C_TRIB + P] = i[:, None] >= i[None, :]
    c[:, C_ONE:C_ONE + P] = 1.0
    c[:, C_HALF:C_HALF + P] = (i[:, None] // 64) == (i[None, :] // 64)
    for f in range(P):
        if (f % 32) < 16:
            c[f + 16, C_ROT + f] = -1.0
        else:
            c[f - 16, C_ROT + f] = 1.0
    for g in range(2):
        for f in range(P):
            c[64 * g + f % 64, C_DUP + 128 * g + f] = 1.0
    c[i, C_FLIP + 64 * (i // 64) + 63 - i % 64] = 1.0
    col = np.arange(GRID)
    c0 = np.clip(col - 8, 0, GRID - 16)
    ok = (col[None, :] >= c0[:, None]) & (col[None, :] < c0[:, None] + 16)
    c[:, C_COL:C_COL + GRID] = np.where(np.tile(ok, (2, 1)), 0.0, NEG)
    k = np.arange(LAT)
    for t in range(2):
        q = t * P + i
        c[:, C_SWA + t * LAT:C_SWA + (t + 1) * LAT] = np.where(np.abs(k[None, :] - q[:, None]) <= 128, 0.0, NEG)
    inv = np.float32(10000.0) ** (-np.arange(16, dtype=np.float32) / np.float32(16))
    pos = np.stack([k // GRID, k % GRID]).astype(np.float32)
    f = i % 64
    ang = pos[f // 32] * inv[f % 16][:, None].astype(np.float32)
    c[:, C_COS:C_COS + LAT] = np.cos(ang)
    c[:, C_SIN:C_SIN + LAT] = np.sin(ang)
    return c


class Signal:

    def __init__(self, sem):
        self.sem, self.made, self.seen = sem, 0, {}

    def given(self):
        self.made += 1
        return self.sem, 1

    def taken(self, who, n=1):
        self.seen[who] = self.seen.get(who, 0) + n
        return self.sem, self.seen[who]


class Chain:

    def __init__(self, eng, sem):
        self.eng, self.sem, self.n = eng, sem, 0

    def __call__(self, ins):
        ins.then_inc(self.sem, 1)
        self.n += 1
        return self.n

    def wait(self, n=None):
        self.eng.wait_ge(self.sem, self.n if n is None else n)


class Banks:

    def __init__(self, banks, full, free):
        self.banks, self.full_sem, self.free_sem, self.base = banks, full, free, 0

    def __getitem__(self, i):
        return self.banks[(self.base + i) % NBANK]

    def empty(self, pe, i):
        g = self.base + i
        if g >= NBANK:
            pe.wait_ge(self.free_sem[g % NBANK], g // NBANK)
        return self.banks[g % NBANK]

    def full(self, eng, i):
        eng.wait_ge(self.full_sem, self.base + i + 1)
        return self.banks[(self.base + i) % NBANK]

    def freed(self, eng, i):
        g = self.base + i
        eng.wait_ge(self.free_sem[g % NBANK], g // NBANK + 1)

    def release(self, eng, i):
        eng.drain().then_inc(*self.free(i))

    def free(self, i):
        return self.free_sem[(self.base + i) % NBANK], 1


class Weights:

    def __init__(self, slots, landed):
        self.slots, self.landed, self.plan, self.at, self.done = slots, landed, [], 0, []

    def add(self, pieces, kt, cols):
        self.plan.append((pieces, kt, cols))

    def block(self, pe):
        n = self.at
        self.at += 1
        pieces, kt, cols = self.plan[n]
        s = n % SLOTS
        before = sum(len(self.plan[m][0]) for m in range(s, n, SLOTS))
        pe.wait_ge(self.landed[s], 16 * (before + len(pieces)))
        return self.view(n)

    def view(self, n):
        _, kt, cols = self.plan[n]
        return self.slots[n % SLOTS][:, 0:kt * cols].rearrange("p (k c) -> p k c", k=kt)

    def used(self, products):
        self.done.append(products)


def build(nc, I, out, stop=None):
    ctx = ExitStack()
    with ctx:
        def sb(name, shape):
            return ctx.enter_context(nc.sbuf_tensor(name, shape, F32))

        def sem(name):
            return ctx.enter_context(nc.semaphore(name))

        const = sb("const", [P, C_END])
        hT = sb("hT", [P, KD, TOK])
        uT = sb("uT", [P, KD, TOK])
        slots = [sb(f"slot{i}", [P, SLOT]) for i in range(SLOTS)]
        arena = sb("arena", [P, ARENA])
        mods = [sb(f"mod{i}", [P, 48, 2]) for i in range(4)]
        sT = sb("sT", [P, 2, KD, 2])
        rstd = sb("rstd", [P, TOK])
        small = sb("small", [P, 64])
        banks_t = [ctx.enter_context(nc.psum_tensor(f"bank{i}", [P, 512], F32)) for i in range(NBANK)]

        ident = const[:, C_ID:C_ID + P]
        tri = [const[:, C_TRIF:C_TRIF + P], const[:, C_TRIB:C_TRIB + P]]
        one = const[:, C_ONE:C_ONE + P]
        half = const[:, C_HALF:C_HALF + P]
        rot = const[:, C_ROT:C_ROT + P]

        full_sem = sem("products")
        free_sem = [sem(f"bank_free{i}") for i in range(NBANK)]
        W = Weights(slots, [sem(f"weights_landed{i}") for i in range(SLOTS)])
        signals = {}

        def S(name):
            if name not in signals:
                signals[name] = Signal(sem(name))
            return signals[name]

        ENG = ("pe", "act", "dve")
        stage_done = {e: sem(f"stage_done_{e}") for e in ENG}
        for n in ("loads", "setup_rows", "sil", "mod_lat", "mod_ready", "centred", "squares", "var", "root", "normed",
                  "evac_act", "evac_dve", "a_rows", "sg_exp", "lg", "gla_d", "gla_e", "gla_q", "gla_sm", "gla_kt",
                  "gla_s", "gla_sp", "gla_el", "res_done",
                  "raw", "conv", "feat", "xb", "dab", "seg", "segx", "mm", "cx", "xdt", "xw", "st", "lw", "lwx", "ecx", "cbm",
                  "s2", "nm", "pr", "pn", "pt", "gates", "hid", "tmp", "ot", "outrow", "stored", "dti", "dtx",
                  "free_a", "free_b", "free_c", "free_d", "bias_loads", "rope_in", "moe_loads", "da_done", "ready", "lam"):
            S(n)
        chain_sem = {e: sem(f"steps_{e}") for e in ENG}

        rows, col = [], {}

        def rowvec(name, ap, n):
            col[name] = sum(r[1] for r in rows)
            rows.append((ap, n))

        def flat(ap):
            k = len(ap.shape)
            names = " ".join(f"a{i}" for i in range(k))
            return ap.rearrange(f"{names} -> ({names})") if k > 1 else ap

        def r128(ap):
            return flat(ap).rearrange("(r p) -> r p", p=P)
        for b, s in enumerate(("", "_2")):
            rowvec(f"c{b}", r128(I["c" + s]), KD)
            rowvec(f"cc{b}", r128(I["c_ctx" + s]), KD)
            rowvec(f"ada_b{b}", r128(I["ada_b" + s]), 96)
        rowvec("ln_g", r128(I["ln_g"]), 32)
        rowvec("ln_b", r128(I["ln_b"]), 32)
        rowvec("gla_norm", r128(I["gla_norm"]), 2)
        rowvec("conv_w", r128(I["ssd_conv_w"]), 160)
        rowvec("conv_b", r128(I["ssd_conv_b"]), 32)
        rowvec("ssd_norm", r128(I["ssd_norm"]), 16)
        rowvec("norm1", r128(I["norm1_g_2"]), 16)
        rowvec("norm2", r128(I["norm2_g_2"]), 16)
        rowvec("ev_conv", r128(I["ev_conv_w_2"]), 12)
        rowvec("subln", r128(I["od_subln_g_2"]), 1)
        for nm in ("ev_q_g_2", "ev_k_g_2", "od_cq_g_2", "od_ck_g_2", "od_dq_g_2", "od_dk_g_2"):
            rowvec(nm, ("twice", I[nm]), 1)
        NR = sum(r[1] for r in rows)
        NT = -(-NR // P)
        VT = sb("vectors", [P, NR])

        def vc(name, i=0):
            return VT[:, col[name] + i:col[name] + i + 1]

        def arena_at(off, *dims):
            n = int(np.prod(dims))
            assert off + n <= ARENA, (off, dims)
            v = arena[:, off:off + n]
            if len(dims) == 2:
                v = v.rearrange("p (a b) -> p a b", a=dims[0])
            if len(dims) == 3:
                v = v.rearrange("p (a b c) -> p a b c", a=dims[0], b=dims[1])
            return v

        def bc(ap, n):
            return ap.unsqueeze(2).broadcast_to([ap.shape[0], ap.shape[1], n])

        def bcm(ap, n):
            return ap.unsqueeze(1).broadcast_to([ap.shape[0], n, ap.shape[1]])

        SEQ = {"lat": (0, LAT), "ctx": (LAT, TOK)}

        class Stage:
            products = 0

            def pe(self, pe, B):
                pass

            def act(self, act, B, ch):
                pass

            def dve(self, dve, B, ch):
                pass

        def dve_link(ch, ins):
            n = ch(ins)
            ch.wait(n)

        raw_rows = arena_at(0, NT, P)
        xrow = arena_at(NT * P, 4, D)
        dvec = sb("ssd_d_rows", [P, 32])
        dcol = sb("ssd_d", [P, 16])
        dtb = sb("dt_bias", [P, 64])
        alog = sb("a_log", [P, 64])
        halves = sb("halves", [P, 2, TOK])
        wa2 = halves
        rl = [halves[:, 0, :], halves[:, 1, :]]
        lamv = sb("lam_v", [P, 4])

        class Setup(Stage):
            products = NT + KD

            def act(self, act, B, ch):
                loads = S("loads")
                n = [0]

                def load(dst, src):
                    act.dma_start(dst, src).then_inc(loads.sem, 16)
                    n[0] += 16
                load(const[:, :], I["const"])
                at = 0
                for ap, k in rows:
                    if isinstance(ap, tuple):
                        for h in range(2):
                            load(raw_rows[at % P:at % P + 1, at // P, 64 * h:64 * h + 64],
                                 ap[1])
                        at += 1
                        continue
                    done = 0
                    while done < k:
                        m = min(k - done, P - at % P)
                        load(raw_rows[at % P:at % P + m, at // P, :], ap[done:done + m, :])
                        at += m
                        done += m
                for i, nm in enumerate(("x", "ctx")):
                    load(xrow[:, 2 * i:2 * i + 2, :], I[nm].rearrange("o (t p) d -> p (o t) d", p=P))
                load(dvec[:, :], flat(I["ssd_d"]).partition_broadcast(P))
                load(dtb[:, :], flat(I["ssd_dt_bias"]).partition_broadcast(P))
                load(alog[:, :], flat(I["ssd_a_log"]).partition_broadcast(P))
                for z in range(2):
                    load(wa2[0:16, z, :], I["gla_w_a2"][0, z])
                    load(wa2[16:17, z, :], I["gla_b_a2"][0:1, z])
                for j, nm in enumerate(("od_lam_q1_2", "od_lam_k1_2", "od_lam_q2_2", "od_lam_k2_2")):
                    load(lamv[0:64, j:j + 1], I[nm].rearrange("o p -> p o"))
                self.total = n[0]
                act.wait_ge(loads.sem, self.total)
                S("ready").given()
                act.drain().then_inc(S("ready").sem, 1)
                act.wait_ge(*S("setup_rows").taken("act"))
                for b in range(2):
                    for s, nm in enumerate(("c", "cc")):
                        c0 = col[f"{nm}{b}"]
                        ins = act.activation(sT[:, b, :, s], VT[:, c0:c0 + KD], ACT.Silu)
                ch(ins)

            def pe(self, pe, B):
                pe.wait_ge(*S("ready").taken("pe"))
                for t in range(NT):
                    r = min(P, NR - t * P)
                    bank = B.empty(pe, t)
                    pe.transpose(bank[:, 0:r], raw_rows[0:r, t, :], ident[0:r, 0:r]).then_inc(full_sem, 1)
                for k in range(KD):
                    bank = B.empty(pe, NT + k)
                    for t in range(4):
                        ins = pe.transpose(bank[:, t * P:t * P + P], xrow[:, t, k * P:k * P + P], ident)
                    ins.then_inc(full_sem, 1)

            def dve(self, dve, B, ch):
                for t in range(NT):
                    r = min(P, NR - t * P)
                    bank = B.full(dve, t)
                    dve.tensor_copy(VT[:, t * P:t * P + r], bank[:, 0:r]).then_inc(*B.free(t))
                dve.wait_ge(*S("ready").taken("dve"))
                S("setup_rows").given()
                dve.drain().then_inc(S("setup_rows").sem, 1)
                for k in range(KD):
                    bank = B.full(dve, NT + k)
                    dve.tensor_copy(hT[:, k, :], bank[:, :]).then_inc(*B.free(NT + k))
                d2 = dvec[:, :].rearrange("p (t a) -> p t a", a=2)
                dve.tensor_copy(dcol[0:64, :], d2[0:64, :, 0])
                dve_link(ch, dve.tensor_copy(dcol[64:P, :], d2[64:P, :, 1]))

        class Ada(Stage):
            products = 12

            def __init__(self, blk, layer):
                self.blk, self.layer = blk, layer
                self.w = I["ada_w" + ("_2" if blk else "")][layer]
                self.m = mods[2 * blk + layer]
                for c in range(12):
                    W.add([self.w[:, c * 512:c * 512 + 512]], KD, 512)

            def pe(self, pe, B):
                for c in range(12):
                    w = W.block(pe)
                    bank = B.empty(pe, c)
                    for j in range(4):
                        for k in range(KD):
                            ins = pe.matmul(bank[:, 2 * j:2 * j + 2], w[:, k, j * P:j * P + P], sT[:, self.blk, k, :],
                                            start=(k == 0), stop=(k == KD - 1))
                    ins.then_inc(full_sem, 1)
                    W.used(B.base + c + 1)

            def dve(self, dve, B, ch):
                m = self.m
                for c in range(12):
                    bank = B.full(dve, c)
                    b0 = col[f"ada_b{self.blk}"] + 48 * self.layer + 4 * c
                    dve.tensor_tensor(m[:, 4 * c:4 * c + 4, :], bank[:, 0:8].rearrange("p (a b) -> p a b", b=2),
                                      bc(VT[:, b0:b0 + 4], 2), ALU.add).then_inc(*B.free(c))
                dve_link(ch, dve.drain())
                for q in (1, 4):
                    dve_link(ch, dve.tensor_scalar(m[:, 8 * q:8 * q + 8, :], m[:, 8 * q:8 * q + 8, :], 1.0, None, ALU.add))
                    if self.blk:
                        g0 = col["norm1" if q == 1 else "norm2"] + 8 * self.layer
                        dve_link(ch, dve.tensor_tensor(m[:, 8 * q:8 * q + 8, :], m[:, 8 * q:8 * q + 8, :],
                                                       bc(VT[:, g0:g0 + 8], 2), ALU.mult))
                if not self.blk:
                    for q in (2, 5):
                        dve_link(ch, dve.tensor_scalar(m[:, 8 * q:8 * q + 8, :], m[:, 8 * q:8 * q + 8, :], 1.0 / ALPHA,
                                                       None, ALU.mult))

        def snaked(ap, rev):
            g = ap.rearrange("p (r two c) -> p r two c", two=2, c=GRID)
            return g[:, :, 0, :], (g[:, :, 1, ::-1] if rev else g[:, :, 1, :])

        class Modulate(Stage):
            def __init__(self, m, q, has_ctx, snake):
                self.m, self.q, self.has_ctx, self.snake = m, q, has_ctx, snake

            def act(self, act, B, ch):
                m, q = self.m, self.q
                for k in range(KD):
                    kw = dict(scale=m[:, 8 * (q + 1) + k, 0:1], bias=m[:, 8 * q + k, 0:1])
                    if self.snake:
                        for o, i in zip(snaked(uT[:, k, 0:LAT], False), snaked(hT[:, k, 0:LAT], True)):
                            act.activation(o, i, ACT.Identity, **kw)
                    else:
                        act.activation(uT[:, k, 0:LAT], hT[:, k, 0:LAT], ACT.Identity, **kw)

            def dve(self, dve, B, ch):
                m, q = self.m, self.q
                for k in range(KD if self.has_ctx else 0):
                    dve.tensor_scalar(uT[:, k, LAT:TOK], hT[:, k, LAT:TOK], m[:, 8 * (q + 1) + k, 1:2],
                                      m[:, 8 * q + k, 1:2], ALU.mult, ALU.add)

        def rstd_dve(dve, B, ch, i, T, dim, eps, free=True):
            bank = B.full(dve, i)
            dve.tensor_scalar(rstd[:, 0:T], bank[:, 0:T], 1.0 / dim, eps, ALU.mult, ALU.add).then_inc(*S("var").given())
            dve.wait_ge(*S("root").taken("dve"))
            dve_link(ch, dve.reciprocal(rstd[:, 0:T], rstd[:, 0:T]))

        def rstd_act(act, T):
            act.wait_ge(*S("var").taken("act"))
            act.activation(rstd[:, 0:T], rstd[:, 0:T], ACT.Sqrt).then_inc(*S("root").given())

        class LayerNorm(Stage):
            products = 2

            def __init__(self, i, j, T):
                self.g, self.T = 16 * i + 8 * j, T
                self.sq = arena_at(0, KD, TOK)

            def pe(self, pe, B):
                T = self.T
                bank = B.empty(pe, 0)
                for k in range(KD):
                    ins = pe.matmul(bank[:, 0:T], one, hT[:, k, 0:T], start=(k == 0), stop=(k == KD - 1))
                ins.then_inc(full_sem, 1)
                bank = B.empty(pe, 1)
                for k in range(KD):
                    pe.wait_ge(*S("squares").taken("pe"))
                    ins = pe.matmul(bank[:, 0:T], one, self.sq[:, k, 0:T], start=(k == 0), stop=(k == KD - 1))
                ins.then_inc(full_sem, 1)

            def dve(self, dve, B, ch):
                T = self.T
                bank = B.full(dve, 0)
                for k in range(KD):
                    dve.scalar_tensor_tensor(out=hT[:, k, 0:T], in0=bank[:, 0:T], scalar=-1.0 / D, in1=hT[:, k, 0:T],
                                             op0=ALU.mult, op1=ALU.add).then_inc(*S("centred").given())
                dve_link(ch, dve.drain())
                B.release(dve, 0)
                rstd_dve(dve, B, ch, 1, T, D, LN_EPS / ALPHA ** 2)
                B.release(dve, 1)
                for k in range(KD):
                    dve.tensor_tensor(hT[:, k, 0:T], hT[:, k, 0:T], rstd[:, 0:T], ALU.mult).then_inc(*S("normed").given())

            def act(self, act, B, ch):
                T = self.T
                for k in range(KD):
                    act.wait_ge(*S("centred").taken("act"))
                    act.activation(self.sq[:, k, 0:T], hT[:, k, 0:T], ACT.Square).then_inc(*S("squares").given())
                rstd_act(act, T)
                for k in range(KD):
                    act.wait_ge(*S("normed").taken("act"))
                    act.activation(hT[:, k, 0:T], hT[:, k, 0:T], ACT.Identity, scale=vc("ln_g", self.g + k),
                                   bias=vc("ln_b", self.g + k))

        class RmsNorm(Stage):
            products = 1

            def __init__(self, m, q, T):
                self.m, self.q, self.T = m, q, T
                self.sq = arena_at(0, KD, TOK)

            def pe(self, pe, B):
                T = self.T
                bank = B.empty(pe, 0)
                for k in range(KD):
                    pe.wait_ge(*S("squares").taken("pe"))
                    ins = pe.matmul(bank[:, 0:T], one, self.sq[:, k, 0:T], start=(k == 0), stop=(k == KD - 1))
                ins.then_inc(full_sem, 1)

            def dve(self, dve, B, ch):
                T = self.T
                rstd_dve(dve, B, ch, 0, T, D, RMS_EPS)
                B.release(dve, 0)
                for k in range(KD):
                    dve.tensor_tensor(uT[:, k, 0:T], hT[:, k, 0:T], rstd[:, 0:T], ALU.mult).then_inc(*S("normed").given())

            def act(self, act, B, ch):
                T, m, q = self.T, self.m, self.q
                for k in range(KD):
                    act.activation(self.sq[:, k, 0:T], hT[:, k, 0:T], ACT.Square).then_inc(*S("squares").given())
                rstd_act(act, T)
                for k in range(KD):
                    act.wait_ge(*S("normed").taken("act"))
                    for s in range(T // LAT):
                        v = uT[:, k, s * LAT:s * LAT + LAT]
                        act.activation(v, v, ACT.Identity, scale=m[:, 8 * (q + 1) + k, s:s + 1],
                                       bias=m[:, 8 * q + k, s:s + 1])

        def feature_major(pe, B, i, w, c0, x, kt, t0, t1, m=P):
            bank = B.empty(pe, i)
            for k in range(kt):
                ins = pe.matmul(bank[0:m, 0:t1 - t0], w[:, k, c0:c0 + m], x[:, k, t0:t1], start=(k == 0),
                                stop=(k == kt - 1))
            ins.then_inc(full_sem, 1)

        def token_major(pe, B, i, w, c0, c1, x, kt, t):
            bank = B.empty(pe, i)
            for k in range(kt):
                ins = pe.matmul(bank[:, 0:c1 - c0], x[:, k, t * P:t * P + P], w[:, k, c0:c1], start=(k == 0),
                                stop=(k == kt - 1))
            ins.then_inc(full_sem, 1)

        class Residual(Stage):
            products = KD

            def __init__(self, w, x, kt, m, q, T, snake):
                self.x, self.kt, self.m, self.q, self.T, self.snake = x, kt, m, q, T, snake
                self.per = min(4, SLOT // (kt * P))
                for c in range(0, KD, self.per):
                    W.add([w[:, c * P:(c + self.per) * P]], kt, self.per * P)

            def pe(self, pe, B):
                for c in range(0, KD, self.per):
                    w = W.block(pe)
                    for j in range(self.per):
                        feature_major(pe, B, c + j, w, j * P, self.x, self.kt, 0, self.T)
                    W.used(B.base + c + self.per)

            def dve(self, dve, B, ch):
                for k in range(KD):
                    bank = B.full(dve, k)

                    def add(h, y, s):
                        return dve.scalar_tensor_tensor(out=h, in0=y, scalar=self.m[:, 8 * self.q + k, s:s + 1], in1=h,
                                                        op0=ALU.mult, op1=ALU.add)
                    if self.snake:
                        for y, h in zip(snaked(bank[:, 0:LAT], True), snaked(hT[:, k, 0:LAT], False)):
                            ins = add(h, y, 0)
                    else:
                        ins = add(hT[:, k, 0:LAT], bank[:, 0:LAT], 0)
                    if self.T == TOK:
                        ins = add(hT[:, k, LAT:TOK], bank[:, LAT:TOK], 1)
                    ins.then_inc(*B.free(k))

        class HiddenRelu2(Stage):

            def __init__(self, w1, T):
                self.T, self.hid = T, arena_at(0, 32, T)
                self.products = 32
                for c in range(8):
                    W.add([w1[:, c * 512:c * 512 + 512]], KD, 512)

            def pe(self, pe, B):
                for c in range(8):
                    w = W.block(pe)
                    for j in range(4):
                        feature_major(pe, B, 4 * c + j, w, j * P, uT, KD, 0, self.T)
                    W.used(B.base + 4 * c + 4)

            def act(self, act, B, ch):
                for i in range(32):
                    bank = B.full(act, i)
                    if i >= 2:
                        act.wait_ge(*S("free_a").taken("act"))
                    act.activation(rl[i % 2][:, 0:self.T], bank[:, 0:self.T], ACT.Relu).then_inc(*B.free(i))
                for i in range(2):
                    act.wait_ge(*S("free_a").taken("act"))

            def dve(self, dve, B, ch):
                for i in range(32):
                    B.freed(dve, i)
                    r = rl[i % 2][:, 0:self.T]
                    dve.tensor_tensor(self.hid[:, i, :], r, r, ALU.mult).then_inc(*S("free_a").given())


        HQ = 4
        g_q = arena_at(0, 4, TOK)
        g_k = arena_at(2048, 4, TOK)
        g_v = arena_at(4096, 4, D)
        g_g = arena_at(8192, KD, TOK)
        g_o = arena_at(12288, KD, TOK)
        g_lg = arena_at(16384, 4, 2 * 512)
        g_a = arena_at(20480, 2, TOK)
        ab = arena_at(21504, TOK)
        aexp = arena_at(22016, TOK)

        class GlaProject(Stage):
            products = 4 + 4 + 8 + 8 + 2 + 8

            def __init__(self):
                w = I["gla_w_in"][0]
                for c in range(6):
                    W.add([w[:, c * 512:c * 512 + 512]], KD, 512)
                W.add([w[:, 3072:3104]], KD, 32)

            def pe(self, pe, B):
                i = 0
                for c in range(6):
                    w = W.block(pe)
                    for j in range(4):
                        if c in (2, 3):
                            token_major(pe, B, i, w, 0, 512, uT, KD, j)
                        else:
                            feature_major(pe, B, i, w, j * P, uT, KD, 0, TOK)
                        i += 1
                    W.used(B.base + i)
                w = W.block(pe)
                for z in range(2):
                    feature_major(pe, B, i, w, 16 * z, uT, KD, 0, TOK, m=16)
                    i += 1
                W.used(B.base + i)
                pe.wait_ge(*S("a_rows").taken("pe"))
                for t in range(4):
                    for z in range(2):
                        bank = B.empty(pe, i)
                        pe.matmul(bank[:, :], g_a[0:17, z, t * P:t * P + P], wa2[0:17, z, :], start=True,
                                  stop=True).then_inc(full_sem, 1)
                        i += 1

            def act(self, act, B, ch):
                for i in range(4):
                    bank = B.full(act, i)
                    act.activation(g_q[:, i, :], bank[:, :], ACT.Copy, scale=float(P) ** -0.5).then_inc(*B.free(i))
                for i in range(16, 24):
                    bank = B.full(act, i)
                    act.activation(g_g[:, i - 16, :], bank[:, :], ACT.Silu).then_inc(*B.free(i))
                for i in range(26, 34):
                    bank = B.full(act, i)
                    if i > 26:
                        act.wait_ge(*S("free_a").taken("act"))
                    ch.wait(ch(act.activation(ab, bank[:, :], ACT.Abs)))
                    ch.wait(ch(act.activation(ab, ab, ACT.Exp, scale=-1.0)))
                    act.activation(aexp, ab, ACT.Ln, bias=1.0).then_inc(*S("sg_exp").given())
                act.wait_ge(*S("free_a").taken("act"))

            def dve(self, dve, B, ch):
                dve_link(ch, dve.memset(g_a[0:32, :, :], 1.0))
                for i in range(4, 16):
                    bank = B.full(dve, i)
                    dst = g_k[:, i - 4, :] if i < 8 else g_v[:, (i - 8) % 4, 512 * ((i - 8) // 4):512 * ((i - 8) // 4) + 512]
                    dve.tensor_copy(dst, bank[:, :]).then_inc(*B.free(i))
                for z in range(2):
                    bank = B.full(dve, 24 + z)
                    dve.tensor_copy(g_a[0:16, z, :], bank[0:16, :]).then_inc(*B.free(24 + z))
                S("a_rows").given()
                dve.drain().then_inc(S("a_rows").sem, 1)
                for i in range(26, 34):
                    t, z = (i - 26) // 2, (i - 26) % 2
                    dve.wait_ge(*S("sg_exp").taken("dve"))
                    dve.scalar_tensor_tensor(out=g_lg[:, t, z * 512:z * 512 + 512], in0=B[i][:, :], scalar=0.0, in1=aexp,
                                             op0=ALU.min, op1=ALU.subtract).then_inc(*S("free_a").given())
                    dve.drain().then_inc(*B.free(i))

        uf = uT[:, :, :].rearrange("p k t -> p (k t)")

        def heads(off, n=P):
            return uf[:, off:off + HQ * n].rearrange("p (h t) -> p h t", h=HQ)

        d_s, q_s, k_s, e1_s, sm_s, kt_s = (heads(512 * i) for i in range(6))
        sf_s = uf[:, 3072:4096].rearrange("p (h v) -> p h v", h=HQ)
        st_s = arena_at(22016 + 512, 4, 256)
        r_s, last_s, er_s, el_s, elr_s, lr_s = (small[:, 4 * i:4 * i + 4] for i in range(6))

        class GlaScan(Stage):
            steps = [(z, t, n) for z in range(2) for n, t in enumerate([(2, 3, 0, 1), (3, 2, 1, 0)][z])]
            products = sum(7 if n < 3 else 5 for _, _, n in steps)

            def pe(self, pe, B):
                i = 0
                for z, t, n in self.steps:
                    bank = B.empty(pe, i)
                    for h in range(HQ):
                        ins = pe.matmul(bank[:, h * P:h * P + P], g_lg[:, t, z * 512 + h * P:z * 512 + h * P + P],
                                        tri[z], start=True, stop=True)
                    ins.then_inc(full_sem, 1)
                    pe.wait_ge(*S("gla_q").taken("pe"))
                    bank = B.empty(pe, i + 1)
                    for h in range(HQ):
                        ins = pe.matmul(bank[:, h * P:h * P + P], k_s[:, h, :], q_s[:, h, :], start=True, stop=True)
                    ins.then_inc(full_sem, 1)
                    bank = B.empty(pe, i + 2)
                    for h in range(HQ):
                        ins = pe.transpose(bank[:, h * P:h * P + P], k_s[:, h, :], ident)
                    ins.then_inc(full_sem, 1)
                    pe.wait_ge(*S("gla_sm").taken("pe"))
                    if n:
                        pe.wait_ge(*S("gla_sp").taken("pe"))
                    for b in range(2):
                        bank = B.empty(pe, i + 3 + b)
                        for j in range(4):
                            h, v = 2 * b + j // 2, j % 2
                            ins = pe.matmul(bank[:, j * P:j * P + P], g_v[:, t, h * 256 + v * P:h * 256 + v * P + P],
                                            sm_s[:, h, :], start=True, stop=(n == 0))
                            if n:
                                ins = pe.matmul(bank[:, j * P:j * P + P], sf_s[:, h, v * P:v * P + P], q_s[:, h, :],
                                                start=False, stop=True)
                        ins.then_inc(full_sem, 1)
                    if n < 3:
                        B.freed(pe, i + 2)
                        for b in range(2):
                            bank = B.empty(pe, i + 5 + b)
                            for j in range(2):
                                h = 2 * b + j
                                ins = pe.matmul(bank[:, j * 256:j * 256 + 256], kt_s[:, h, :],
                                                g_v[:, t, h * 256:h * 256 + 256], start=True, stop=True)
                            ins.then_inc(full_sem, 1)
                    i += 7 if n < 3 else 5

            def act(self, act, B, ch):
                i = 0
                for z, t, n in self.steps:
                    act.wait_ge(*S("gla_d").taken("act"))
                    act.activation(e1_s, d_s, ACT.Exp, scale=1 / 16).then_inc(*S("gla_e").given())
                    ch.wait(ch(act.drain()))
                    act.activation(d_s, d_s, ACT.Exp, scale=-1 / 16).then_inc(*S("gla_e").given())
                    act.activation(er_s, r_s, ACT.Exp, scale=1 / 16)
                    act.activation(el_s, last_s, ACT.Exp, scale=1 / 16)
                    act.activation(elr_s, lr_s, ACT.Exp, scale=1 / 16).then_inc(*S("gla_el").given())
                    bank = B.full(act, i + 2)
                    act.activation(kt_s, bank[:, :].rearrange("p (h t) -> p h t", h=HQ), ACT.Copy).then_inc(*B.free(i + 2))
                    i += 7 if n < 3 else 5

            def dve(self, dve, B, ch):
                i = 0
                for z, t, n in self.steps:
                    mid, last = (63, 127) if z == 0 else (64, 0)
                    bank = B.full(dve, i)
                    cum = bank[:, :].rearrange("p (h t) -> p h t", h=HQ)
                    dve.tensor_copy(r_s, cum[:, :, mid])
                    dve_link(ch, dve.tensor_copy(last_s, cum[:, :, last]))
                    dve_link(ch, dve.tensor_tensor(lr_s, last_s, r_s, ALU.subtract))
                    dve_link(ch, dve.tensor_tensor(d_s, cum, bc(r_s, P), ALU.subtract))
                    S("gla_d").given()
                    dve.drain().then_inc(S("gla_d").sem, 1)
                    B.release(dve, i)
                    dve.wait_ge(*S("gla_e").taken("dve"))
                    dve.tensor_tensor(q_s, e1_s, g_q[:, :, t * P:t * P + P], ALU.mult)
                    dve.wait_ge(*S("gla_e").taken("dve"))
                    dve.tensor_tensor(k_s, d_s, g_k[:, :, t * P:t * P + P], ALU.mult).then_inc(*S("gla_q").given())
                    dve.wait_ge(*S("gla_el").taken("dve"))
                    if n:
                        dve.tensor_tensor(sf_s, st_s, bc(er_s, 256), ALU.mult).then_inc(*S("gla_sp").given())
                    bank = B.full(dve, i + 1)
                    dve.tensor_tensor(sm_s, bank[:, :].rearrange("p (h t) -> p h t", h=HQ), bcm(tri[z], HQ),
                                      ALU.mult).then_inc(*S("gla_sm").given())
                    B.release(dve, i + 1)
                    for b in range(2):
                        bank = B.full(dve, i + 3 + b)
                        src = bank[:, :].rearrange("p (h t) -> p h t", h=4)
                        dst = g_o[:, 4 * b:4 * b + 4, t * P:t * P + P]
                        if z == 0:
                            dve.tensor_copy(dst, src).then_inc(*B.free(i + 3 + b))
                        else:
                            dve.tensor_tensor(dst, src, dst, ALU.add).then_inc(*B.free(i + 3 + b))
                    if n < 3:
                        if n:
                            dve_link(ch, dve.tensor_tensor(st_s, st_s, bc(el_s, 256), ALU.mult))
                        for b in range(2):
                            bank = B.full(dve, i + 5 + b)
                            for j in range(2):
                                h = 2 * b + j
                                if n:
                                    ins = dve.scalar_tensor_tensor(out=st_s[:, h, :], in0=bank[:, j * 256:j * 256 + 256],
                                                                   scalar=elr_s[:, h:h + 1], in1=st_s[:, h, :],
                                                                   op0=ALU.mult, op1=ALU.add)
                                else:
                                    ins = dve.tensor_scalar(st_s[:, h, :], bank[:, j * 256:j * 256 + 256],
                                                            elr_s[:, h:h + 1], None, ALU.mult)
                            ins.then_inc(*B.free(i + 5 + b))
                        dve_link(ch, dve.drain())
                    i += 7 if n < 3 else 5

        class GlaGate(Stage):
            products = HQ

            def pe(self, pe, B):
                for h in range(HQ):
                    bank = B.empty(pe, h)
                    for v in range(2):
                        pe.wait_ge(*S("squares").taken("pe"))
                        ins = pe.matmul(bank[:, :], one, uT[:, 2 * h + v, :], start=(v == 0), stop=(v == 1))
                    ins.then_inc(full_sem, 1)

            def act(self, act, B, ch):
                for k in range(KD):
                    act.activation(uT[:, k, :], g_o[:, k, :], ACT.Square).then_inc(*S("squares").given())
                for h in range(HQ):
                    rstd_act(act, TOK)

            def dve(self, dve, B, ch):
                for h in range(HQ):
                    rstd_dve(dve, B, ch, h, TOK, 256, RMS_EPS)
                    B.release(dve, h)
                    for v in range(2):
                        k = 2 * h + v
                        dve_link(ch, dve.scalar_tensor_tensor(out=g_o[:, k, :], in0=g_o[:, k, :], scalar=vc("gla_norm", v),
                                                              in1=rstd[:, :], op0=ALU.mult, op1=ALU.mult))
                        dve_link(ch, dve.tensor_tensor(g_o[:, k, :], g_o[:, k, :], g_g[:, k, :], ALU.mult))

        NG = 8
        s_z = arena_at(0, 16, LAT)
        s_y = arena_at(4096, 16, LAT)
        s_dt = arena_at(8192, 4, 64)
        s_da = arena_at(8448, 4, 64)
        s_cj = arena_at(8704, 4, 64)
        s_t1 = arena_at(8960, 64)
        s_t2 = arena_at(9024, 64)
        PADW = LAT + 4
        s_raw = arena[:, 9088:9088 + 4 * 2 * PADW].rearrange("p (f s t) -> p f s t", f=4, s=2)
        s_acc = arena_at(11168, 4, TOK)
        s_f = arena_at(13216, 4, TOK)
        s_xb = arena_at(15264, 4, 384)
        s_cb = arena_at(16800, 4, P)
        s_dab = arena_at(17312, 4, P)
        s_seg = arena_at(17824, 4, P)
        s_e = arena_at(18336, 4, P)
        s_m = arena_at(18848, 4, P)
        s_ec = arena_at(19360, 4, P)
        s_cx = arena_at(19872, 4, P)
        s_xdt = arena_at(20384, 4, 64)
        s_xw = arena_at(20640, 4, 64)
        s_st = arena_at(20896, 2, 256)
        s_lw, s_el = small[:, 32:36], small[:, 36:40]

        class SsdGates(Stage):
            products = 16 + 4 + 1

            def __init__(self):
                w = I["ssd_w_in"][0]
                for c in range(4):
                    W.add([w[:, c * 512:c * 512 + 512]], KD, 512)
                W.add([w[:, 6144:6208]], KD, 64)

            def pe(self, pe, B):
                for c in range(4):
                    w = W.block(pe)
                    for j in range(4):
                        feature_major(pe, B, 4 * c + j, w, j * P, uT, KD, 0, LAT)
                    W.used(B.base + 4 * c + 4)
                w = W.block(pe)
                for t in range(4):
                    token_major(pe, B, 16 + t, w, 0, 64, uT, KD, t)
                W.used(B.base + 20)
                pe.wait_ge(*S("da_done").taken("pe"))
                bank = B.empty(pe, 20)
                for t in range(4):
                    for z in range(2):
                        c = 64 * t + 32 * z
                        ins = pe.matmul(bank[:, c:c + 32], tri[z], s_da[:, t, 32 * z:32 * z + 32], start=True, stop=True)
                ins.then_inc(full_sem, 1)

            def act(self, act, B, ch):
                for i in range(16):
                    bank = B.full(act, i)
                    act.activation(s_z[:, i, :], bank[:, 0:LAT], ACT.Silu).then_inc(*B.free(i))
                ch.wait(ch(act.activation(alog[:, :], alog[:, :], ACT.Exp)))
                for t in range(4):
                    act.wait_ge(*S("dti").taken("act"))
                    ch.wait(ch(act.activation(s_t1, s_dt[:, t, :], ACT.Abs)))
                    ch.wait(ch(act.activation(s_t1, s_t1, ACT.Exp, scale=-1.0)))
                    act.activation(s_t2, s_t1, ACT.Ln, bias=1.0).then_inc(*S("dtx").given())

            def dve(self, dve, B, ch):
                dve_link(ch, dve.memset(arena[:, 9088:9088 + 4 * 2 * PADW], 0.0))
                for t in range(4):
                    bank = B.full(dve, 16 + t)
                    dve.tensor_tensor(s_dt[:, t, :], bank[:, 0:64], dtb[:, :], ALU.add).then_inc(*S("dti").given())
                    B.release(dve, 16 + t)
                    dve.wait_ge(*S("dtx").taken("dve"))
                    dve_link(ch, dve.scalar_tensor_tensor(out=s_dt[:, t, :], in0=s_dt[:, t, :], scalar=0.0, in1=s_t2,
                                                          op0=ALU.max, op1=ALU.add))
                    ins = dve.scalar_tensor_tensor(out=s_da[:, t, :], in0=s_dt[:, t, :], scalar=-1.0, in1=alog[:, :],
                                                   op0=ALU.mult, op1=ALU.mult)
                    dve_link(ch, ins)
                S("da_done").given()
                dve.drain().then_inc(S("da_done").sem, 1)
                bank = B.full(dve, 20)
                dve.tensor_copy(s_cj, bank[:, 0:256].rearrange("p (t h) -> p t h", t=4)).then_inc(*B.free(20))

        class SsdGroup(Stage):
            steps = [(0, 2), (1, 3), (0, 3), (1, 2), (0, 0), (1, 1), (0, 1), (1, 0)]

            def __init__(self, g):
                self.g = g
                w = I["ssd_w_in"][0]
                W.add([w[:, 2048 + g * 256:2048 + g * 256 + 256], w[:, 4096 + g * P:4096 + g * P + P],
                       w[:, 5120 + g * P:5120 + g * P + P]], KD, 512)
                self.products = 4 + 4 + 1 + sum(1 + (t < 2) + (n < 6) for n, (z, t) in enumerate(self.steps))

            def pe(self, pe, B):
                w = W.block(pe)
                for j in range(4):
                    feature_major(pe, B, j, w, j * P, uT, KD, 0, LAT if j == 3 else TOK)
                W.used(B.base + 4)
                for _ in range(3):
                    pe.wait_ge(*S("feat").taken("pe"))
                for t in range(4):
                    bank = B.empty(pe, 4 + t)
                    for j in range(3):
                        ins = pe.transpose(bank[:, j * P:j * P + P], s_f[:, j, t * P:t * P + P], ident)
                    ins.then_inc(full_sem, 1)
                pe.wait_ge(*S("feat").taken("pe"))
                bank = B.empty(pe, 8)
                for t in range(2):
                    ins = pe.matmul(bank[:, t * P:t * P + P], s_f[:, 2, t * P:t * P + P], s_f[:, 3, t * P:t * P + P],
                                    start=True, stop=True)
                ins.then_inc(full_sem, 1)
                for t in range(4):
                    B.freed(pe, 4 + t)
                i = 9
                for n, (z, t) in enumerate(self.steps):
                    pe.wait_ge(*S("dab").taken("pe"))
                    bank = B.empty(pe, i)
                    for h in range(4):
                        ins = pe.matmul(bank[:, h * P:h * P + P], s_dab[:, h, :], tri[z], start=True, stop=True)
                    ins.then_inc(full_sem, 1)
                    i += 1
                    pe.wait_ge(*S("xw").taken("pe"))
                    if t < 2:
                        bank = B.empty(pe, i)
                        for h in range(4):
                            o = bank[64 * (h % 2):64 * (h % 2) + 64, (h // 2) * P:(h // 2) * P + P]
                            pe.matmul(o, s_xdt[:, h, :], s_m[:, h, :], start=True, stop=False)
                            ins = pe.matmul(o, s_st[:, z, h * 64:h * 64 + 64], s_cx[:, h, :], start=False, stop=True)
                        ins.then_inc(full_sem, 1)
                        i += 1
                    if n < 6:
                        bank = B.empty(pe, i)
                        pe.matmul(bank[:, 0:256], s_xb[:, t, 256:384], s_xw[:, :, :], start=True,
                                  stop=True).then_inc(full_sem, 1)
                        i += 1

            def act(self, act, B, ch):
                g = self.g
                for j in range(4):
                    bank = B.full(act, j)
                    n = 1 if j == 3 else 2
                    act.activation(s_raw[:, j, 0:n, 2:2 + LAT], bank[:, 0:n * LAT].rearrange("p (s t) -> p s t", s=n),
                                   ACT.Copy).then_inc(*B.free(j))
                for j in range(4):
                    T = LAT if j == 3 else TOK
                    f = [2 * g, 2 * g + 1, 16 + g, 24 + g][j]
                    act.wait_ge(*S("conv").taken("act"))
                    act.activation(s_f[:, j, 0:T], s_acc[:, j, 0:T], ACT.Silu, bias=vc("conv_b", f)).then_inc(*S("feat").given())
                for t in range(4):
                    bank = B.full(act, 4 + t)
                    act.activation(s_xb[:, t, :], bank[:, 0:384], ACT.Copy).then_inc(*B.free(4 + t))
                i = 9
                for n, (z, t) in enumerate(self.steps):
                    if n:
                        B.full(act, i - 1)
                    c = 32 * z + 4 * g
                    act.activation(s_dab, bc(s_da[:, t, c:c + 4], P), ACT.Copy).then_inc(*S("dab").given())
                    last = 127 if z == 0 else 0
                    if t < 2:
                        bank = B.full(act, i)
                        cum = bank[:, :].rearrange("p (h t) -> p h t", h=4)
                        act.activation(s_ec, cum, ACT.Exp).then_inc(*S("ecx").given())
                        act.wait_ge(*S("seg").taken("act"))
                        act.activation(s_e, s_seg, ACT.Exp).then_inc(*S("segx").given())
                    act.wait_ge(*S("lw").taken("act"))
                    act.activation(s_el, s_el, ACT.Exp)
                    act.activation(s_lw, s_lw, ACT.Exp).then_inc(*S("lwx").given())
                    i += 1 + (t < 2) + (n < 6)

            def dve(self, dve, B, ch):
                g = self.g
                for j in range(4):
                    f = [2 * g, 2 * g + 1, 16 + g, 24 + g][j]
                    n = 1 if j == 3 else 2
                    B.freed(dve, j)
                    acc = s_acc[:, j, 0:n * LAT].rearrange("p (s t) -> p s t", s=n)
                    dve_link(ch, dve.tensor_scalar(acc, s_raw[:, j, 0:n, 0:LAT], vc("conv_w", f), None, ALU.mult))
                    for tap in range(1, 5):
                        ins = dve.scalar_tensor_tensor(out=acc, in0=s_raw[:, j, 0:n, tap:tap + LAT],
                                                       scalar=vc("conv_w", 32 * tap + f), in1=acc, op0=ALU.mult, op1=ALU.add)
                        if tap < 4:
                            dve_link(ch, ins)
                        else:
                            ins.then_inc(*S("conv").given())
                bank = B.full(dve, 8)
                dve.wait_ge(*S("feat").taken("dve", 4))
                for j in range(2):
                    dve.tensor_scalar(s_y[:, 2 * g + j, :], s_f[:, j, 0:LAT], dcol[:, 2 * g + j:2 * g + j + 1], None, ALU.mult)
                for z in range(2):
                    dve_link(ch, dve.tensor_tensor(s_cb[:, 2 * z:2 * z + 2, :],
                                                   bank[:, 0:256].rearrange("p (t i) -> p t i", t=2), bcm(tri[z], 2), ALU.mult))
                B.release(dve, 8)
                for t in range(4):
                    B.freed(dve, 4 + t)
                i = 9
                for n, (z, t) in enumerate(self.steps):
                    c = 32 * z + 4 * g
                    cj = s_cj[:, t, c:c + 4]
                    last = 127 if z == 0 else 0
                    dve_link(ch, dve.tensor_tensor(s_xdt, s_xb[:, t, 0:256].rearrange("p (h d) -> p h d", h=4),
                                                   bc(s_dt[:, t, c:c + 4], 64), ALU.mult))
                    bank = B.full(dve, i)
                    cum = bank[:, :].rearrange("p (h t) -> p h t", h=4)
                    if t < 2:
                        dve.wait_ge(*S("ecx").taken("dve"))
                        for h in range(4):
                            ins = dve.tensor_scalar(s_seg[:, h, :], cum[:, h, :], cj[:, h:h + 1], 0.0, ALU.subtract, ALU.min)
                        ins.then_inc(*S("seg").given())
                    dve.tensor_copy(s_el, cum[:, :, last])
                    dve.tensor_tensor(s_lw, cum[:, :, last], cj, ALU.subtract).then_inc(*S("lw").given())
                    if t < 2:
                        dve.tensor_tensor(s_cx, s_ec, bcm(s_f[:, 3, t * P:t * P + P], 4), ALU.mult)
                        dve.wait_ge(*S("segx").taken("dve"))
                        dve_link(ch, dve.tensor_tensor(s_m, s_e, bcm(s_cb[:, 2 * z + t, :], 4), ALU.mult))
                    dve.wait_ge(*S("lwx").taken("dve"))
                    B.release(dve, i)
                    i += 1
                    dve.tensor_tensor(s_xw, s_xdt, bc(s_lw, 64), ALU.mult).then_inc(*S("xw").given())
                    if t < 2:
                        bank = B.full(dve, i)
                        y = s_y[:, 2 * g:2 * g + 2, t * P:t * P + P]
                        dve.tensor_tensor(y, bank[:, 0:256].rearrange("p (f i) -> p f i", f=2), y, ALU.add).then_inc(*B.free(i))
                        i += 1
                    if n < 6:
                        st = s_st[:, z, :]
                        if n >= 2:
                            v = st.rearrange("p (h d) -> p h d", h=4)
                            dve_link(ch, dve.tensor_tensor(v, v, bc(s_el, 64), ALU.mult))
                            bank = B.full(dve, i)
                            dve.tensor_tensor(st, bank[:, 0:256], st, ALU.add).then_inc(*B.free(i))
                        else:
                            bank = B.full(dve, i)
                            dve.tensor_copy(st, bank[:, 0:256]).then_inc(*B.free(i))
                        i += 1
                    dve_link(ch, dve.drain())

        s_sq = arena_at(9088, 16, LAT)

        class SsdGate(Stage):
            products = 1

            def pe(self, pe, B):
                bank = B.empty(pe, 0)
                for k in range(16):
                    pe.wait_ge(*S("squares").taken("pe"))
                    ins = pe.matmul(bank[:, 0:LAT], one, s_sq[:, k, :], start=(k == 0), stop=(k == 15))
                ins.then_inc(full_sem, 1)

            def act(self, act, B, ch):
                for k in range(16):
                    act.wait_ge(*S("normed").taken("act"))
                    act.activation(s_sq[:, k, :], s_y[:, k, :], ACT.Square).then_inc(*S("squares").given())
                rstd_act(act, LAT)

            def dve(self, dve, B, ch):
                for k in range(16):
                    dve.tensor_tensor(s_y[:, k, :], s_y[:, k, :], s_z[:, k, :], ALU.mult).then_inc(*S("normed").given())
                dve_link(ch, dve.drain())
                rstd_dve(dve, B, ch, 0, LAT, 2048, RMS_EPS)
                B.release(dve, 0)
                for k in range(16):
                    dve.scalar_tensor_tensor(out=s_y[:, k, :], in0=s_y[:, k, :], scalar=vc("ssd_norm", k), in1=rstd[:, 0:LAT],
                                             op0=ALU.mult, op1=ALU.mult)

        class LoadCtx(Stage):
            products = KD

            def act(self, act, B, ch):
                act.dma_start(xrow[:, 0:2, :], I["ctx_2"].rearrange("o (t p) d -> p (o t) d", p=P))\
                   .then_inc(S("bias_loads").sem, 16)

            def pe(self, pe, B):
                pe.wait_ge(S("bias_loads").sem, 16)
                for k in range(KD):
                    bank = B.empty(pe, k)
                    for t in range(2):
                        ins = pe.transpose(bank[:, t * P:t * P + P], xrow[:, t, k * P:k * P + P], ident)
                    ins.then_inc(full_sem, 1)

            def dve(self, dve, B, ch):
                for k in range(KD):
                    bank = B.full(dve, k)
                    dve.tensor_copy(hT[:, k, LAT:TOK], bank[:, 0:CTX]).then_inc(*B.free(k))

        m_y = arena_at(0, KD, TOK)
        m_q = arena_at(4096, 8, TOK)
        m_k = arena_at(8192, 6, TOK)
        m_v = arena_at(11264, 4, 640)
        m_g = arena_at(13824, 4, TOK)
        m_bias = arena_at(13824, 8, 6, GRID)
        m_pad = arena_at(15872, 4, 2 * (LAT + 2))
        m_gc = arena_at(6144, 4, TOK)
        m_s = [[uT[:, 2 * i + j, :] for j in range(2)] for i in range(2)]
        m_pt = [uT[:, 4 + i, :] for i in range(2)]
        sinks = sb("sinks", [P, 8])

        class EvenProject(Stage):
            products = 24

            def __init__(self):
                w = I["ev_w_in_2"][0]
                for c in range(6):
                    W.add([w[:, c * 512:c * 512 + 512]], KD, 512)

            def pe(self, pe, B):
                for c in range(6):
                    w = W.block(pe)
                    for j in range(4):
                        if c == 5:
                            token_major(pe, B, 4 * c + j, w, 0, 512, uT, KD, j)
                        else:
                            feature_major(pe, B, 4 * c + j, w, j * P, uT, KD, 0, TOK)
                    W.used(B.base + 4 * c + 4)

            def act(self, act, B, ch):
                for i in range(8):
                    bank = B.full(act, i)
                    act.activation((m_g if i < 4 else m_gc)[:, i % 4, :], bank[:, :], ACT.Copy).then_inc(*B.free(i))
                for i in range(12, 24, 2):
                    bank = B.full(act, i)
                    act.activation(self.dst(i), bank[:, :], ACT.Copy).then_inc(*B.free(i))

            def dst(self, i):
                return [m_q, m_k, m_v][(i - 12) // 4][:, i % 4, 0:512]

            def dve(self, dve, B, ch):
                dve_link(ch, dve.memset(arena[:, 15872:15872 + 8 * (LAT + 2)], 0.0))
                for j in range(4):
                    pad = m_pad[:, j, :].rearrange("p (s t) -> p s t", s=2)
                    acc = m_y[:, j, :].rearrange("p (s t) -> p s t", s=2)
                    bank = B.full(dve, 8 + j)
                    B.freed(dve, 4 + j)
                    dve.tensor_tensor(pad[:, :, 1:1 + LAT], bank[:, :].rearrange("p (s t) -> p s t", s=2),
                                      m_gc[:, j, :].rearrange("p (s t) -> p s t", s=2), ALU.mult).then_inc(*B.free(8 + j))
                    B.freed(dve, 8 + j)
                    dve_link(ch, dve.tensor_scalar(acc, pad[:, :, 0:LAT], vc("ev_conv", j), None, ALU.mult))
                    for tap in (1, 2):
                        dve_link(ch, dve.scalar_tensor_tensor(out=acc, in0=pad[:, :, tap:tap + LAT],
                                                              scalar=vc("ev_conv", 4 * tap + j), in1=acc,
                                                              op0=ALU.mult, op1=ALU.add))
                    dve_link(ch, dve.tensor_tensor(m_y[:, j, :], m_y[:, j, :], m_g[:, j, :], ALU.mult))
                for i in range(13, 24, 2):
                    bank = B.full(dve, i)
                    dve.tensor_copy(self.dst(i), bank[:, :]).then_inc(*B.free(i))

        m_braw = arena_at(16896, 8, 6, GRID)

        class BiasLoad(Stage):
            products = 6

            def act(self, act, B, ch):
                t = I["ev_rpb_2"]
                for b in range(2):
                    for h in range(8):
                        src = bass.AP(tensor=t.tensor, offset=h * 15 * 31 + (5 - b) * 31 + 15 - 63,
                                      ap=[[1, GRID], [31, 6], [1, GRID]])
                        act.dma_start(m_braw[64 * b:64 * b + 64, h, :, :], src).then_inc(S("moe_loads").sem, 16)

            def pe(self, pe, B):
                pe.wait_ge(S("moe_loads").sem, 16 * 16)
                raw = m_braw.rearrange("p h m c -> p (h m c)")
                for i in range(6):
                    bank = B.empty(pe, i)
                    pe.matmul(bank[:, :], const[:, C_FLIP:C_FLIP + P], raw[:, i * 512:i * 512 + 512], start=True,
                              stop=True).then_inc(full_sem, 1)

            def dve(self, dve, B, ch):
                v = m_bias.rearrange("p h m c -> p (h m) c")
                for i in range(6):
                    bank = B.full(dve, i)
                    dve.tensor_tensor(v[:, 8 * i:8 * i + 8, :], bank[:, :].rearrange("p (a c) -> p a c", a=8),
                                      bcm(const[:, C_COL:C_COL + GRID], 8), ALU.add).then_inc(*B.free(i))

        class HeadNorm(Stage):

            def __init__(self, tiles, rope):
                self.tiles, self.rope = tiles, rope
                self.products = len(tiles) * (2 if rope else 1)
                self.sq = [rl[0], rl[1]]

            def pe(self, pe, B):
                n = len(self.tiles)
                for i, (x, gain, T) in enumerate(self.tiles):
                    pe.wait_ge(*S("squares").taken("pe"))
                    bank = B.empty(pe, i)
                    pe.matmul(bank[:, 0:T], half, self.sq[i % 2][:, 0:T], start=True, stop=True).then_inc(full_sem, 1)
                if self.rope:
                    for i, (x, gain, T) in enumerate(self.tiles):
                        pe.wait_ge(*S("rope_in").taken("pe"))
                        bank = B.empty(pe, n + i)
                        pe.matmul(bank[:, 0:LAT], rot, x[:, 0:LAT], start=True, stop=True).then_inc(full_sem, 1)

            def act(self, act, B, ch):
                for i, (x, gain, T) in enumerate(self.tiles):
                    if i >= 2:
                        B.full(act, i - 2)
                    act.activation(self.sq[i % 2][:, 0:T], x, ACT.Square).then_inc(*S("squares").given())
                    if i >= 1:
                        rstd_act(act, self.tiles[i - 1][2])
                rstd_act(act, self.tiles[-1][2])

            def dve(self, dve, B, ch):
                n = len(self.tiles)
                for i, (x, gain, T) in enumerate(self.tiles):
                    rstd_dve(dve, B, ch, i, T, 64, RMS_EPS)
                    B.release(dve, i)
                    ins = dve.scalar_tensor_tensor(out=x, in0=x, scalar=vc(gain), in1=rstd[:, 0:T], op0=ALU.mult, op1=ALU.mult)
                    if self.rope:
                        ins.then_inc(*S("rope_in").given())
                        dve.wait_ge(S("rope_in").sem, S("rope_in").made)
                    else:
                        dve_link(ch, ins)
                if self.rope:
                    cos, sin = const[:, C_COS:C_COS + LAT], const[:, C_SIN:C_SIN + LAT]
                    for i, (x, gain, T) in enumerate(self.tiles):
                        bank = B.full(dve, n + i)
                        dve_link(ch, dve.tensor_tensor(rl[0][:, 0:LAT], bank[:, 0:LAT], sin, ALU.mult))
                        dve_link(ch, dve.tensor_tensor(x[:, 0:LAT], x[:, 0:LAT], cos, ALU.mult))
                        dve_link(ch, dve.tensor_tensor(x[:, 0:LAT], x[:, 0:LAT], rl[0][:, 0:LAT], ALU.add))
                        B.release(dve, n + i)

        class Attention(Stage):

            def __init__(self, items, lam=None):
                self.items, self.lam = items, lam
                self.ns = len(items[0]["q"])
                order = []
                for n in range(-1, len(items)):
                    if n + 1 < len(items):
                        order += [("s", n + 1, j) for j in range(self.ns)]
                    if n >= 0:
                        order += [("t", n, 0), ("o", n, 0)]
                self.order = {key: i for i, key in enumerate(order)}
                self.products = len(order)

            def pe(self, pe, B):
                for (kind, n, j), i in self.order.items():
                    it = self.items[n]
                    nk = it["nk"]
                    if kind == "s":
                        bank = B.empty(pe, i)
                        pe.matmul(bank[:, 0:nk], it["q"][j], it["k"][j], start=True, stop=True).then_inc(full_sem, 1)
                    elif kind == "t":
                        pe.wait_ge(*S("pn").taken("pe"))
                        bank = B.empty(pe, i)
                        for t in range(nk // P):
                            ins = pe.transpose(bank[:, t * P:t * P + P], m_s[n % 2][0][:, t * P:t * P + P], ident)
                        ins.then_inc(full_sem, 1)
                    else:
                        B.freed(pe, i - 1)
                        bank = B.empty(pe, i)
                        r0, m = it["rows"]
                        for t, v in enumerate(it["v"]):
                            ins = pe.matmul(bank[r0:r0 + m, 0:P], v, m_pt[n % 2][:, t * P:t * P + P], start=(t == 0),
                                            stop=(t == len(it["v"]) - 1))
                        ins.then_inc(full_sem, 1)

            def stats(self, n, j):
                o = 24 * (n % 2) + 12 * j
                return [small[:, o + x:o + x + 1] for x in range(5)]

            def act(self, act, B, ch):
                def exps(n):
                    it = self.items[n]
                    for j in range(self.ns):
                        mx, nm, den, es, rc = self.stats(n, j)
                        act.wait_ge(*S("nm").taken("act"))
                        s = m_s[n % 2][j][:, 0:it["nk"]]
                        if it["sink"] is not None:
                            act.activation(es, it["sink"], ACT.Exp, bias=nm)
                        act.activation(s, s, ACT.Exp, bias=nm, accum_out=den)
                        act.drain().then_inc(*S("pr").given())
                for n in range(-1, len(self.items)):
                    if n + 1 < len(self.items):
                        exps(n + 1)
                    if n >= 0:
                        i, nk = self.order["t", n, 0], self.items[n]["nk"]
                        if n >= 2:
                            B.full(act, self.order["o", n - 2, 0])
                        bank = B.full(act, i)
                        act.activation(m_pt[n % 2][:, 0:nk], bank[:, 0:nk], ACT.Copy).then_inc(*B.free(i))

            def dve(self, dve, B, ch):
                def scores(n):
                    it = self.items[n]
                    nk = it["nk"]
                    for j in range(self.ns):
                        mx, nm, den, es, rc = self.stats(n, j)
                        i = self.order["s", n, j]
                        bank = B.full(dve, i)
                        if n >= 2 and j == 0:
                            B.full(dve, self.order["t", n - 2, 0])
                        s = m_s[n % 2][j]
                        b = 0
                        if it["bias"] is not None:
                            b = LAT
                            dve.scalar_tensor_tensor(out=s[:, 0:b], in0=bank[:, 0:b], scalar=0.125, in1=it["bias"],
                                                     op0=ALU.mult, op1=ALU.add)
                        dve_link(ch, dve.tensor_scalar(s[:, b:nk], bank[:, b:nk], 0.125, None, ALU.mult))
                        B.release(dve, i)
                        dve_link(ch, dve.tensor_reduce(mx, s[:, 0:nk], AX.X, ALU.max))
                        if it["sink"] is not None:
                            dve_link(ch, dve.tensor_tensor(mx, mx, it["sink"], ALU.max))
                        dve.tensor_scalar(nm, mx, -1.0, None, ALU.mult).then_inc(*S("nm").given())

                def normalise(n):
                    it = self.items[n]
                    for j in range(self.ns):
                        mx, nm, den, es, rc = self.stats(n, j)
                        dve.wait_ge(*S("pr").taken("dve"))
                        if it["sink"] is not None:
                            dve_link(ch, dve.tensor_tensor(den, den, es, ALU.add))
                        dve_link(ch, dve.reciprocal(rc, den))
                    s0 = m_s[n % 2][0][:, 0:it["nk"]]
                    r0 = self.stats(n, 0)[4]
                    if self.ns == 1:
                        dve.tensor_scalar(s0, s0, r0, None, ALU.mult).then_inc(*S("pn").given())
                    else:
                        s1, r1 = m_s[n % 2][1][:, 0:it["nk"]], self.stats(n, 1)[4]
                        dve_link(ch, dve.tensor_scalar(s1, s1, r1, self.lam, ALU.mult, ALU.mult))
                        dve.scalar_tensor_tensor(out=s0, in0=s0, scalar=r0, in1=s1, op0=ALU.mult,
                                                 op1=ALU.add).then_inc(*S("pn").given())
                for n in range(-1, len(self.items)):
                    if n + 1 < len(self.items):
                        scores(n + 1)
                    if n >= 0:
                        normalise(n)
                        i = self.order["o", n, 0]
                        bank = B.full(dve, i)
                        r0, m = self.items[n]["rows"]
                        dve.tensor_copy(self.items[n]["o"], bank[r0:r0 + m, 0:P]).then_inc(*B.free(i))

        def even_items():
            items = []
            for h in range(8):
                r, f = 64 * (h % 2), h // 2
                for t in range(4):
                    lat = t < 2
                    ks = 0 if lat else LAT
                    items.append(dict(
                        q=[m_q[r:r + 64, f, t * P:t * P + P]], k=[m_k[r:r + 64, f, ks:TOK]], nk=TOK - ks,
                        bias=m_bias[:, h, 2 - 2 * t:6 - 2 * t, :].rearrange("p m c -> p (m c)") if lat else None, sink=None,
                        v=[m_v[:, j, h * 64:h * 64 + 64] for j in range(ks // P, 4)], rows=(r, 64),
                        o=m_y[r:r + 64, 4 + f, t * P:t * P + P]))
            return items

        def window_items():
            items = []
            for h in range(8):
                r, f = 64 * (h % 2), h // 2
                for t in range(2):
                    items.append(dict(
                        q=[m_q[r:r + 64, f, t * P:t * P + P]], k=[m_k[r:r + 64, h // 4, :]], nk=TOK,
                        bias=const[:, C_SWA + t * LAT:C_SWA + t * LAT + LAT], sink=sinks[:, h:h + 1],
                        v=[m_v[:, j, 64 * (h // 4):64 * (h // 4) + 64] for j in range(4)], rows=(r, 64),
                        o=m_y[r:r + 64, f, t * P:t * P + P]))
            return items

        def diff_items():
            return [dict(q=[m_q[64 * i:64 * i + 64, 4 + h, t * P:t * P + P] for i in range(2)],
                         k=[m_k[64 * i:64 * i + 64, 2 + h, :] for i in range(2)], nk=TOK, bias=None, sink=None,
                         v=[m_v[:, j, P + h * P:P + h * P + P] for j in range(4)], rows=(0, P),
                         o=m_y[:, 4 + h, t * P:t * P + P])
                    for h in range(4) for t in range(2)]

        class HiddenSwiglu(Stage):

            def __init__(self, w1, w3, T, gate=None):
                self.nf, self.T, self.gate = w1.shape[1] // P, T, gate
                self.hid = arena_at(2048 if gate is not None else 0, self.nf, T)
                self.products = 2 * self.nf
                for c in range(0, self.nf, 4):
                    n = min(4, self.nf - c)
                    for w in (w1, w3):
                        W.add([w[:, c * P:(c + n) * P]], KD, n * P)

            def pe(self, pe, B):
                for c in range(0, self.nf, 4):
                    n = min(4, self.nf - c)
                    a, b = W.block(pe), W.block(pe)
                    for j in range(n):
                        feature_major(pe, B, 2 * (c + j), a, j * P, uT, KD, 0, self.T)
                        feature_major(pe, B, 2 * (c + j) + 1, b, j * P, uT, KD, 0, self.T)
                    W.used(B.base + 2 * (c + n))
                    W.used(B.base + 2 * (c + n))

            def act(self, act, B, ch):
                for f in range(self.nf):
                    bank = B.full(act, 2 * f)
                    if f >= 2:
                        act.wait_ge(*S("free_a").taken("act"))
                    act.activation(rl[f % 2][:, 0:self.T], bank[:, 0:self.T], ACT.Silu).then_inc(*B.free(2 * f))
                for f in range(2):
                    act.wait_ge(*S("free_a").taken("act"))

            def dve(self, dve, B, ch):
                for f in range(self.nf):
                    B.freed(dve, 2 * f)
                    bank = B.full(dve, 2 * f + 1)
                    h = self.hid[:, f, :]
                    dve.tensor_tensor(h, bank[:, 0:self.T], rl[f % 2][:, 0:self.T], ALU.mult).then_inc(*S("free_a").given())
                    B.release(dve, 2 * f + 1)
                    if self.gate is not None:
                        dve_link(ch, dve.drain())
                        dve.tensor_tensor(h, h, self.gate, ALU.mult)

        class OddProject(Stage):
            products = 4 + 4 + 1 + 4 + 4 + 4

            def __init__(self):
                w = I["od_w_in_2"][0]
                for c0, n in ((0, 512), (512, 512), (1024, 256), (1280, 512), (1792, 512)):
                    W.add([w[:, c0:c0 + n]], KD, n)

            def pe(self, pe, B):
                i = 0
                for c in range(5):
                    w = W.block(pe)
                    if c == 2:
                        feature_major(pe, B, i, w, 0, uT, KD, 0, TOK)
                        i += 1
                    for j in range(4):
                        if c == 2:
                            token_major(pe, B, i, w, P, 2 * P, uT, KD, j)
                        elif c == 4:
                            token_major(pe, B, i, w, 0, 512, uT, KD, j)
                        else:
                            feature_major(pe, B, i, w, j * P, uT, KD, 0, LAT if c < 2 else TOK)
                        i += 1
                    W.used(B.base + i)

            def dst(self, i):
                if i < 8:
                    return m_q[:, i, 0:LAT]
                if i == 8:
                    return m_k[:, 0, :]
                if i < 13:
                    return m_v[:, i - 9, 0:P]
                if i < 17:
                    return m_k[:, 2 + i - 13, :]
                return m_v[:, i - 17, P:P + 512]

            def act(self, act, B, ch):
                for i in range(0, 21, 2):
                    bank, d = B.full(act, i), self.dst(i)
                    act.activation(d, bank[:, 0:d.shape[1]], ACT.Copy).then_inc(*B.free(i))

            def dve(self, dve, B, ch):
                for i in range(1, 21, 2):
                    bank, d = B.full(dve, i), self.dst(i)
                    dve.tensor_copy(d, bank[:, 0:d.shape[1]]).then_inc(*B.free(i))

        LAM_INIT = 0.8 - 0.6 * math.exp(-0.3)
        lam_t = small[:, 60:61]

        class KeysAndLambda(Stage):
            products = 3

            def pe(self, pe, B):
                for g in range(2):
                    bank = B.empty(pe, g)
                    pe.matmul(bank[:, :], const[:, C_DUP + g * P:C_DUP + g * P + P], m_k[:, 0, :], start=True,
                              stop=True).then_inc(full_sem, 1)
                pe.wait_ge(*S("lam").taken("pe"))
                bank = B.empty(pe, 2)
                pe.matmul(bank[:, 0:2], one[0:64, :], small[0:64, 56:58], start=True, stop=True).then_inc(full_sem, 1)

            def act(self, act, B, ch):
                act.dma_start(sinks[:, :], flat(I["od_sink_2"]).partition_broadcast(P)).then_inc(S("bias_loads").sem, 16)
                act.wait_ge(S("bias_loads").sem, 32)
                bank = B.full(act, 2)
                act.activation(small[:, 58:60], bank[:, 0:2], ACT.Exp).then_inc(*B.free(2))

            def dve(self, dve, B, ch):
                dve.tensor_tensor(small[0:64, 56:57], lamv[0:64, 0:1], lamv[0:64, 1:2], ALU.mult)
                dve.tensor_tensor(small[0:64, 57:58], lamv[0:64, 2:3], lamv[0:64, 3:4], ALU.mult).then_inc(*S("lam").given())
                for g in range(2):
                    B.full(dve, 1)
                    bank = B.full(dve, g)
                    dve.tensor_copy(m_k[:, g, :], bank[:, :]).then_inc(*B.free(g))
                B.freed(dve, 2)
                dve_link(ch, dve.tensor_tensor(lam_t, small[:, 59:60], small[:, 58:59], ALU.subtract))
                dve_link(ch, dve.tensor_scalar(lam_t, lam_t, -LAM_INIT, None, ALU.add))

        class SubNorm(Stage):
            products = 4

            def pe(self, pe, B):
                for h in range(4):
                    pe.wait_ge(*S("squares").taken("pe"))
                    bank = B.empty(pe, h)
                    pe.matmul(bank[:, 0:LAT], one, uT[:, h, 0:LAT], start=True, stop=True).then_inc(full_sem, 1)

            def act(self, act, B, ch):
                for h in range(4):
                    act.activation(uT[:, h, 0:LAT], m_y[:, 4 + h, 0:LAT], ACT.Square).then_inc(*S("squares").given())
                for h in range(4):
                    rstd_act(act, LAT)

            def dve(self, dve, B, ch):
                dve_link(ch, dve.tensor_scalar(small[:, 61:62], vc("subln"), 1.0 - LAM_INIT, None, ALU.mult))
                for h in range(4):
                    rstd_dve(dve, B, ch, h, LAT, P, RMS_EPS)
                    B.release(dve, h)
                    y = m_y[:, 4 + h, 0:LAT]
                    dve_link(ch, dve.scalar_tensor_tensor(out=y, in0=y, scalar=small[:, 61:62], in1=rstd[:, 0:LAT],
                                                          op0=ALU.mult, op1=ALU.mult))

        NE = 8
        gate_rows = arena_at(0, NE, LAT)
        lg = arena[:, 6144:6240].rearrange("p (t i e) -> p t i e", t=2, i=6)
        gb = arena_at(4096, 2 * NE, P)

        class Router(Stage):
            products = 2 + 4

            def __init__(self):
                W.add([I["moe_router_2"][0]], KD, NE)

            def pe(self, pe, B):
                w = W.block(pe)
                for t in range(2):
                    token_major(pe, B, t, w, 0, NE, uT, KD, t)
                W.used(B.base + 2)
                pe.wait_ge(*S("gates").taken("pe"))
                for b in range(4):
                    bank = B.empty(pe, 2 + b)
                    for j in range(2):
                        for t in range(2):
                            ins = pe.matmul(bank[:, j * LAT + t * P:j * LAT + t * P + P], gb[:, t * NE + 2 * b + j, :], ident,
                                            start=True, stop=True)
                    ins.then_inc(full_sem, 1)

            def act(self, act, B, ch):
                for t in range(2):
                    act.wait_ge(*S("dti").taken("act"))
                    act.activation(lg[:, t, 2, :], lg[:, t, 0, :], ACT.Exp, bias=small[:, 62:63]).then_inc(*S("dtx").given())

            def dve(self, dve, B, ch):
                for t in range(2):
                    l, mx, e, gt, eq, run_ = (lg[:, t, i, :] for i in range(6))
                    bank = B.full(dve, t)
                    dve_link(ch, dve.tensor_copy(l, bank[:, 0:NE]))
                    B.release(dve, t)
                    dve_link(ch, dve.max(mx, l))
                    dve.tensor_scalar(small[:, 62:63], mx[:, 0:1], -1.0, None, ALU.mult).then_inc(*S("dti").given())
                    dve.tensor_scalar(gt, l, mx[:, 1:2], None, ALU.is_gt)
                    dve_link(ch, dve.tensor_scalar(eq, l, mx[:, 1:2], None, ALU.is_equal))
                    dve.tensor_tensor_scan(run_, one[:, 0:NE], eq, 0.0, ALU.mult, ALU.add)
                    dve_link(ch, dve.tensor_reduce(small[:, 63:64], gt, AX.X, ALU.add))
                    dve_link(ch, dve.tensor_scalar(run_, run_, small[:, 63:64], None, ALU.add))
                    dve_link(ch, dve.scalar_tensor_tensor(out=eq, in0=run_, scalar=2.0, in1=eq, op0=ALU.is_le, op1=ALU.mult))
                    dve.wait_ge(*S("dtx").taken("dve"))
                    dve_link(ch, dve.tensor_tensor(l, gt, eq, ALU.add))
                    dve_link(ch, dve.tensor_tensor(l, l, e, ALU.mult))
                    dve_link(ch, dve.tensor_reduce(small[:, 63:64], l, AX.X, ALU.add))
                    dve_link(ch, dve.reciprocal(small[:, 63:64], small[:, 63:64]))
                    dve_link(ch, dve.tensor_scalar(l, l, small[:, 63:64], None, ALU.mult))
                    dve_link(ch, dve.tensor_copy(gb[:, t * NE:t * NE + NE, :], bc(l, P)))
                S("gates").given()
                dve.drain().then_inc(S("gates").sem, 1)
                for b in range(4):
                    bank = B.full(dve, 2 + b)
                    dve.tensor_copy(gate_rows[:, 2 * b:2 * b + 2, :], bank[:, :].rearrange("p (e t) -> p e t", e=2))\
                       .then_inc(*B.free(2 + b))

        class Store(Stage):
            products = 4
            orow = arena_at(0, 2, D)

            def pe(self, pe, B):
                for i in range(4):
                    t, c = i // 2, i % 2
                    bank = B.empty(pe, i)
                    for j in range(4):
                        ins = pe.transpose(bank[:, j * P:j * P + P], hT[:, 4 * c + j, t * P:t * P + P], ident)
                    ins.then_inc(full_sem, 1)

            def dve(self, dve, B, ch):
                for i in range(4):
                    bank = B.full(dve, i)
                    dve.tensor_copy(self.orow[:, i // 2, 512 * (i % 2):512 * (i % 2) + 512], bank[:, :]).then_inc(*B.free(i))

            def act(self, act, B, ch):
                for t in range(2):
                    for c in range(2):
                        B.freed(act, 2 * t + c)
                    act.dma_start(out[0, t * P:t * P + P, :], self.orow[:, t, :]).then_inc(S("stored").sem, 16)
                act.wait_ge(S("stored").sem, 32)

        M = mods
        y8 = g_o
        stages = [Setup()] + [Ada(b, l) for b in range(2) for l in range(2)]
        stages += [Modulate(M[0], 0, True, True), GlaProject(), GlaScan(), GlaGate(),
                   Residual(I["gla_w_out"][0], y8, KD, M[0], 2, TOK, True), LayerNorm(0, 0, TOK),
                   Modulate(M[0], 3, True, False)]
        hid = HiddenRelu2(I["ffn_w1"][0], TOK)
        stages += [hid, Residual(I["ffn_w2"][0], hid.hid, 32, M[0], 5, TOK, False), LayerNorm(0, 1, TOK)]
        mark = {"b1l0": len(stages)}
        stages += [Modulate(M[1], 0, True, True), SsdGates()] + [SsdGroup(g) for g in range(NG)]
        stages += [SsdGate(), Residual(I["ssd_w_out"][0], s_y, 16, M[1], 2, LAT, True), LayerNorm(1, 0, LAT)]
        mark["b1l1m"] = len(stages)
        stages += [Modulate(M[1], 3, False, False)]
        hid = HiddenRelu2(I["ffn_w1"][1], LAT)
        stages += [hid, Residual(I["ffn_w2"][1], hid.hid, 32, M[1], 5, LAT, False), LayerNorm(1, 1, LAT)]
        mark["b1"] = len(stages)
        stages += [LoadCtx(), RmsNorm(M[2], 0, TOK), EvenProject(), BiasLoad(),
                   HeadNorm([(m_q[:, i, :], "ev_q_g_2", TOK) for i in range(4)]
                            + [(m_k[:, i, :], "ev_k_g_2", TOK) for i in range(4)], False),
                   Attention(even_items()), Residual(I["ev_w_out_2"][0], m_y, KD, M[2], 2, TOK, False)]
        mark["b2l0m"] = len(stages)
        stages += [RmsNorm(M[2], 3, TOK)]
        hid = HiddenSwiglu(I["ffn_w1_2"][0], I["ffn_w3_2"][0], TOK)
        stages += [hid, Residual(I["ffn_w2_2"][0], hid.hid, 22, M[2], 5, TOK, False)]
        mark["b2l0"] = len(stages)
        stages += [RmsNorm(M[3], 0, TOK), OddProject(),
                   HeadNorm([(m_q[:, i, 0:LAT], "od_cq_g_2" if i < 4 else "od_dq_g_2", LAT) for i in range(8)]
                            + [(m_k[:, 0, :], "od_ck_g_2", TOK)]
                            + [(m_k[:, 2 + i, :], "od_dk_g_2", TOK) for i in range(4)], True),
                   KeysAndLambda(), Attention(window_items()), Attention(diff_items(), lam_t), SubNorm(),
                   Residual(I["od_w_out_2"][0], m_y, KD, M[3], 2, LAT, False)]
        mark["b2l1m"] = len(stages)
        stages += [RmsNorm(M[3], 3, LAT), Router()]
        for e in range(NE):
            hid = HiddenSwiglu(I["moe_w1_2"][0, e], I["moe_w3_2"][0, e], LAT, gate_rows[:, e, :])
            stages += [hid, Residual(I["moe_w2_2"][0, e], hid.hid, 11, M[3], 5, LAT, False)]
        if stop is not None:
            keep = mark[stop]
            cut = stages[keep:]
            ncut = 0
            stages = stages[:keep]
            W.limit = True
        stages.append(Store())

        block = ctx.enter_context(nc.Block())

        def run(name, eng, ch):
            B = Banks(banks_t, full_sem, free_sem)
            for n, st in enumerate(stages):
                if n:
                    for other in ENG:
                        if other != name:
                            eng.wait_ge(stage_done[other], n)
                getattr_part = {"pe": lambda: st.pe(eng, B), "act": lambda: st.act(eng, B, ch),
                                "dve": lambda: st.dve(eng, B, ch)}[name]
                getattr_part()
                eng.drain().then_inc(stage_done[name], 1)
                B.base += st.products

        @block.tensor
        def _(pe):
            run("pe", pe, None)

        @block.scalar
        def _(act):
            run("act", act, Chain(act, chain_sem["act"]))

        @block.vector
        def _(dve):
            run("dve", dve, Chain(dve, chain_sem["dve"]))

        @block.sync
        def _(sync):
            for n, (pieces, kt, cols) in enumerate(W.plan[:len(W.done)]):
                if n >= SLOTS:
                    sync.wait_ge(full_sem, W.done[n - SLOTS])
                v = W.view(n)
                at = 0
                for piece in pieces:
                    c = piece.shape[1]
                    sync.dma_start(v[:, :, at:at + c], piece.rearrange("(k p) c -> p k c", p=P))\
                        .then_inc(W.landed[n % SLOTS], 16)
                    at += c


_OUTS = [((1, 256, 1024), "float32")]
_STOP = None


def kernel(**inputs):
    import concourse.bacc as _bacc
    from concourse.bass_utils import run_bass_kernel_spmd as _run

    nc = _bacc.Bacc("TRN2", target_bir_lowering=False, num_devices=1)
    arrays, aps = {}, {}
    for name, a in list(inputs.items()) + [("const", constants())]:
        a = np.ascontiguousarray(a)
        if a.size == 0 or name.startswith("hy_"):
            continue
        arrays[f"in_{name}"] = a
        aps[name] = nc.dram_tensor(f"in_{name}", a.shape, mybir.dt.from_np(a.dtype), kind="ExternalInput").ap()
    o = nc.dram_tensor("out_0", _OUTS[0][0], F32, kind="ExternalOutput").ap()
    build(nc, aps, o, _STOP)
    r = _run(nc, [arrays], core_ids=[0])
    return r.results[0]["out_0"]
```

```python
from contextlib import ExitStack
import math

import numpy as np

import concourse.bass as bass
from concourse import mybir

F32 = mybir.dt.float32
ALU = mybir.AluOpType
ACT = mybir.ActivationFunctionType
AX = mybir.AxisListType

P = 128
D = 1024
KD = D // P
LAT = 256
CTX = 256
TOK = LAT + CTX
ROWS, GRID = 4, 64
ALPHA = 4 ** 0.25
LN_EPS, RMS_EPS = 1e-5, 1e-6
NBANK = 6
SLOTS = 4
SLOT = 4096
NEG = -1e30
ARENA = 22528

C_ID, C_TRIF, C_TRIB, C_ONE, C_HALF, C_ROT, C_DUP = 0, 128, 256, 384, 512, 640, 768
C_COL, C_SWA, C_COS, C_SIN, C_FLIP, C_IOTA, C_END = 1024, 1088, 1600, 1856, 2112, 2240, 2368


def constants():
    c = np.zeros((P, C_END), np.float32)
    i = np.arange(P)
    c[:, C_ID:C_ID + P] = np.eye(P)
    c[:, C_TRIF:C_TRIF + P] = i[:, None] <= i[None, :]
    c[:, C_TRIB:C_TRIB + P] = i[:, None] >= i[None, :]
    c[:, C_ONE:C_ONE + P] = 1.0
    c[:, C_HALF:C_HALF + P] = (i[:, None] // 64) == (i[None, :] // 64)
    for f in range(P):
        if (f % 32) < 16:
            c[f + 16, C_ROT + f] = -1.0
        else:
            c[f - 16, C_ROT + f] = 1.0
    for g in range(2):
        for f in range(P):
            c[64 * g + f % 64, C_DUP + 128 * g + f] = 1.0
    c[i, C_FLIP + 64 * (i // 64) + 63 - i % 64] = 1.0
    c[:, C_IOTA:C_IOTA + P] = i[None, :]
    col = np.arange(GRID)
    c0 = np.clip(col - 8, 0, GRID - 16)
    ok = (col[None, :] >= c0[:, None]) & (col[None, :] < c0[:, None] + 16)
    c[:, C_COL:C_COL + GRID] = np.where(np.tile(ok, (2, 1)), 0.0, NEG)
    k = np.arange(LAT)
    for t in range(2):
        q = t * P + i
        c[:, C_SWA + t * LAT:C_SWA + (t + 1) * LAT] = np.where(np.abs(k[None, :] - q[:, None]) <= 128, 0.0, NEG)
    inv = np.float32(10000.0) ** (-np.arange(16, dtype=np.float32) / np.float32(16))
    pos = np.stack([k // GRID, k % GRID]).astype(np.float32)
    f = i % 64
    ang = pos[f // 32] * inv[f % 16][:, None].astype(np.float32)
    c[:, C_COS:C_COS + LAT] = np.cos(ang)
    c[:, C_SIN:C_SIN + LAT] = np.sin(ang)
    return c


STAGE_NAMES = []


class Signal:

    def __init__(self, sem):
        self.sem, self.made, self.seen = sem, 0, {}

    def given(self):
        self.made += 1
        return self.sem, 1

    def taken(self, who, n=1):
        self.seen[who] = self.seen.get(who, 0) + n
        return self.sem, self.seen[who]


class Chain:

    def __init__(self, eng, sem):
        self.eng, self.sem, self.n = eng, sem, 0

    def __call__(self, ins):
        ins.then_inc(self.sem, 1)
        self.n += 1
        return self.n

    def wait(self, n=None):
        self.eng.wait_ge(self.sem, self.n if n is None else n)


class Banks:

    def __init__(self, banks, full, free):
        self.banks, self.full_sem, self.free_sem, self.base = banks, full, free, 0

    def __getitem__(self, i):
        return self.banks[(self.base + i) % NBANK]

    def empty(self, pe, i):
        g = self.base + i
        if g >= NBANK:
            pe.wait_ge(self.free_sem[g % NBANK], g // NBANK)
        return self.banks[g % NBANK]

    def full(self, eng, i):
        eng.wait_ge(self.full_sem, self.base + i + 1)
        return self.banks[(self.base + i) % NBANK]

    def freed(self, eng, i):
        g = self.base + i
        eng.wait_ge(self.free_sem[g % NBANK], g // NBANK + 1)

    def release(self, eng, i):
        eng.drain().then_inc(*self.free(i))

    def free(self, i):
        return self.free_sem[(self.base + i) % NBANK], 1


class Weights:

    def __init__(self, slots, landed):
        self.slots, self.landed, self.plan, self.done = slots, landed, [], []
        self.dmas = [0] * SLOTS
        self.second_pass = None

    def block(self, pe, pieces, kt):
        n = len(self.plan)
        self.plan.append((pieces, kt))
        self.dmas[n % SLOTS] += len(pieces)
        pe.wait_ge(self.landed[n % SLOTS], 16 * self.dmas[n % SLOTS])
        return self.view(n)

    def view(self, n):
        pieces, kt = self.plan[n]
        cols = sum(p.shape[1] for p in pieces)
        return self.slots[n % SLOTS][:, 0:kt * cols].rearrange("p (k c) -> p k c", k=kt)

    def used(self, sem, count):
        self.done.append((sem, count))


def build(nc, I, out, stop=None):
    ctx = ExitStack()
    with ctx:
        def sb(name, shape):
            return ctx.enter_context(nc.sbuf_tensor(name, shape, F32))

        def sem(name):
            return ctx.enter_context(nc.semaphore(name))

        const = sb("const", [P, C_END])
        hT = sb("hT", [P, KD, TOK])
        uT = sb("uT", [P, KD, TOK])
        slots = [sb(f"slot{i}", [P, SLOT]) for i in range(SLOTS)]
        arena = sb("arena", [P, ARENA])
        mods = [sb(f"mod{i}", [P, 48, 2]) for i in range(4)]
        sT = sb("sT", [P, 2, KD, 2])
        rstd = sb("rstd", [P, TOK])
        small = sb("small", [P, 64])
        banks_t = [ctx.enter_context(nc.psum_tensor(f"bank{i}", [P, 512], F32)) for i in range(8)]

        ident = const[:, C_ID:C_ID + P]
        tri = [const[:, C_TRIF:C_TRIF + P], const[:, C_TRIB:C_TRIB + P]]
        one = const[:, C_ONE:C_ONE + P]
        half = const[:, C_HALF:C_HALF + P]
        rot = const[:, C_ROT:C_ROT + P]

        full_sem = sem("products")
        free_sem = [sem(f"bank_free{i}") for i in range(NBANK)]
        W = Weights(slots, [sem(f"weights_landed{i}") for i in range(SLOTS)])
        signals = {}

        def S(name):
            if name not in signals:
                signals[name] = Signal(sem(name))
            return signals[name]

        ENG = ("pe", "act", "dve")
        stage_done = {e: sem(f"stage_done_{e}") for e in ENG}
        for n in ("loads", "setup_rows", "sil", "mod_lat", "mod_ready", "centred", "squares", "var", "root", "normed",
                  "evac_act", "evac_dve", "a_rows", "sg_exp", "lg", "gla_d", "gla_e", "gla_q", "gla_sm", "gla_kt",
                  "gla_s", "gla_sp", "gla_el", "res_done",
                  "raw", "conv", "feat", "xb", "dab", "seg", "segx", "mm", "cx", "xdt", "xw", "st", "lw", "lwx", "ecx", "cbm",
                  "s2", "nm", "pr", "pn", "pt", "gates", "hid", "tmp", "ot", "outrow", "stored", "dti", "dtx",
                  "free_a", "free_b", "free_c", "free_d", "bias_loads", "rope_in", "convd", "ada_rows", "ada_cols", "ada_copied", "ada_free", "moe_loads", "da_done", "ready", "lam", "picked", "placed", "gate_cols", "overflow_known", "moe_rl"):
            S(n)
        chain_sem = {e: sem(f"steps_{e}") for e in ENG}

        rows, col = [], {}

        def rowvec(name, ap, n):
            col[name] = sum(r[1] for r in rows)
            rows.append((ap, n))

        def flat(ap):
            k = len(ap.shape)
            names = " ".join(f"a{i}" for i in range(k))
            return ap.rearrange(f"{names} -> ({names})") if k > 1 else ap

        def r128(ap):
            return flat(ap).rearrange("(r p) -> r p", p=P)
        for b, s in enumerate(("", "_2")):
            rowvec(f"c{b}", r128(I["c" + s]), KD)
            rowvec(f"cc{b}", r128(I["c_ctx" + s]), KD)
            rowvec(f"ada_b{b}", r128(I["ada_b" + s]), 96)
        rowvec("ln_g", r128(I["ln_g"]), 32)
        rowvec("ln_b", r128(I["ln_b"]), 32)
        rowvec("gla_norm", r128(I["gla_norm"]), 2)
        rowvec("conv_w", r128(I["ssd_conv_w"]), 160)
        rowvec("conv_b", r128(I["ssd_conv_b"]), 32)
        rowvec("ssd_norm", r128(I["ssd_norm"]), 16)
        rowvec("norm1", r128(I["norm1_g_2"]), 16)
        rowvec("norm2", r128(I["norm2_g_2"]), 16)
        rowvec("ev_conv", r128(I["ev_conv_w_2"]), 12)
        rowvec("subln", r128(I["od_subln_g_2"]), 1)
        for nm in ("ev_q_g_2", "ev_k_g_2", "od_cq_g_2", "od_ck_g_2", "od_dq_g_2", "od_dk_g_2"):
            rowvec(nm, ("twice", I[nm]), 1)
        NR = sum(r[1] for r in rows)
        NT = -(-NR // P)
        VT = sb("vectors", [P, NR])

        def vc(name, i=0):
            return VT[:, col[name] + i:col[name] + i + 1]

        def arena_at(off, *dims):
            n = int(np.prod(dims))
            assert off + n <= ARENA, (off, dims)
            v = arena[:, off:off + n]
            if len(dims) == 2:
                v = v.rearrange("p (a b) -> p a b", a=dims[0])
            if len(dims) == 3:
                v = v.rearrange("p (a b c) -> p a b c", a=dims[0], b=dims[1])
            return v

        def bc(ap, n):
            return ap.unsqueeze(2).broadcast_to([ap.shape[0], ap.shape[1], n])

        def bcm(ap, n):
            return ap.unsqueeze(1).broadcast_to([ap.shape[0], n, ap.shape[1]])

        SEQ = {"lat": (0, LAT), "ctx": (LAT, TOK)}

        class Stage:
            products = 0

            def pe(self, pe, B):
                pass

            def act(self, act, B, ch):
                pass

            def dve(self, dve, B, ch):
                pass

        def dve_link(ch, ins):
            n = ch(ins)
            ch.wait(n)

        raw_rows = arena_at(0, NT, P)
        xrow = arena_at(NT * P, 4, D)
        dvec = sb("ssd_d_rows", [P, 32])
        dcol = sb("ssd_d", [P, 16])
        dtb = sb("dt_bias", [P, 64])
        alog = sb("a_log", [P, 64])
        halves = sb("halves", [P, 2, TOK])
        wa2 = halves
        rl = [halves[:, 0, :], halves[:, 1, :]]
        lamv = sb("lam_v", [P, 4])

        class Setup(Stage):
            products = NT + KD

            def act(self, act, B, ch):
                loads = S("loads")
                n = [0]

                def load(dst, src):
                    act.dma_start(dst, src).then_inc(loads.sem, 16)
                    n[0] += 16
                load(const[:, :], I["const"])
                at = 0
                for ap, k in rows:
                    if isinstance(ap, tuple):
                        for h in range(2):
                            load(raw_rows[at % P:at % P + 1, at // P, 64 * h:64 * h + 64],
                                 ap[1])
                        at += 1
                        continue
                    done = 0
                    while done < k:
                        m = min(k - done, P - at % P)
                        load(raw_rows[at % P:at % P + m, at // P, :], ap[done:done + m, :])
                        at += m
                        done += m
                for i, nm in enumerate(("x", "ctx")):
                    load(xrow[:, 2 * i:2 * i + 2, :], I[nm].rearrange("o (t p) d -> p (o t) d", p=P))
                load(dvec[:, :], flat(I["ssd_d"]).partition_broadcast(P))
                load(dtb[:, :], flat(I["ssd_dt_bias"]).partition_broadcast(P))
                load(alog[:, :], flat(I["ssd_a_log"]).partition_broadcast(P))
                for z in range(2):
                    load(wa2[0:16, z, :], I["gla_w_a2"][0, z])
                    load(wa2[16:17, z, :], I["gla_b_a2"][0:1, z])
                for j, nm in enumerate(("od_lam_q1_2", "od_lam_k1_2", "od_lam_q2_2", "od_lam_k2_2")):
                    load(lamv[0:64, j:j + 1], I[nm].rearrange("o p -> p o"))
                self.total = n[0]
                act.wait_ge(loads.sem, self.total)
                S("ready").given()
                act.drain().then_inc(S("ready").sem, 1)
                act.wait_ge(*S("setup_rows").taken("act"))
                for b in range(2):
                    for s, nm in enumerate(("c", "cc")):
                        c0 = col[f"{nm}{b}"]
                        ins = act.activation(sT[:, b, :, s], VT[:, c0:c0 + KD], ACT.Silu)
                ch(ins)

            def pe(self, pe, B):
                pe.wait_ge(*S("ready").taken("pe"))
                for t in range(NT):
                    r = min(P, NR - t * P)
                    bank = B.empty(pe, t)
                    pe.transpose(bank[:, 0:r], raw_rows[0:r, t, :], ident[0:r, 0:r]).then_inc(full_sem, 1)
                for k in range(KD):
                    bank = B.empty(pe, NT + k)
                    for t in range(4):
                        ins = pe.transpose(bank[:, t * P:t * P + P], xrow[:, t, k * P:k * P + P], ident)
                    ins.then_inc(full_sem, 1)

            def dve(self, dve, B, ch):
                for t in range(NT):
                    r = min(P, NR - t * P)
                    bank = B.full(dve, t)
                    dve.tensor_copy(VT[:, t * P:t * P + r], bank[:, 0:r]).then_inc(*B.free(t))
                dve.wait_ge(*S("ready").taken("dve"))
                S("setup_rows").given()
                dve.drain().then_inc(S("setup_rows").sem, 1)
                for k in range(KD):
                    bank = B.full(dve, NT + k)
                    dve.tensor_copy(hT[:, k, :], bank[:, :]).then_inc(*B.free(NT + k))
                d2 = dvec[:, :].rearrange("p (t a) -> p t a", a=2)
                dve.tensor_copy(dcol[0:64, :], d2[0:64, :, 0])
                dve_link(ch, dve.tensor_copy(dcol[64:P, :], d2[64:P, :, 1]))

        ada_rows_bank, ada_cols_bank = banks_t[NBANK], banks_t[NBANK + 1]
        ada_row = sb("ada_row", [2, 512])

        class Ada(Stage):

            def __init__(self, blk, layer):
                self.blk, self.layer = blk, layer
                self.w = I["ada_w" + ("_2" if blk else "")][layer]
                self.m = mods[2 * blk + layer]

            def pe(self, pe, B):
                rows, cols = S("ada_rows"), S("ada_cols")
                if cols.made:
                    pe.wait_ge(*S("ada_free").taken("pe"))
                for c in range(13):
                    if c < 12:
                        w = W.block(pe, [self.w[:, c * 512:c * 512 + 512]], KD)
                        if c:
                            pe.wait_ge(*S("ada_copied").taken("pe"))
                        for k in range(KD):
                            ins = pe.matmul(ada_rows_bank[0:2, :], sT[:, self.blk, k, :], w[:, k, :], start=(k == 0),
                                            stop=(k == KD - 1))
                        ins.then_inc(*rows.given())
                        W.used(rows.sem, rows.made)
                    if c == 12:
                        pe.wait_ge(*S("ada_copied").taken("pe", 1))
                    if c:
                        for j in range(4):
                            o = 8 * (c - 1) + 2 * j
                            ins = pe.transpose(ada_cols_bank[:, o:o + 2], ada_row[0:2, j * P:j * P + P], ident[0:2, 0:2])
                        ins.then_inc(*cols.given())

            def act(self, act, B, ch):
                for c in range(12):
                    act.wait_ge(*S("ada_rows").taken("act"))
                    if c:
                        act.wait_ge(*S("ada_cols").taken("act"))
                    act.activation(ada_row[0:2, :], ada_rows_bank[0:2, :], ACT.Copy).then_inc(*S("ada_copied").given())
                act.wait_ge(*S("ada_cols").taken("act"))

            def dve(self, dve, B, ch):
                m = self.m
                dve.wait_ge(*S("ada_cols").taken("dve", 12))
                b0 = col[f"ada_b{self.blk}"] + 48 * self.layer
                dve.tensor_tensor(m[:, :, :], ada_cols_bank[:, 0:96].rearrange("p (a b) -> p a b", b=2),
                                  bc(VT[:, b0:b0 + 48], 2), ALU.add).then_inc(*S("ada_free").given())
                dve.wait_ge(S("ada_free").sem, S("ada_free").made)
                for q in (1, 4):
                    dve_link(ch, dve.tensor_scalar(m[:, 8 * q:8 * q + 8, :], m[:, 8 * q:8 * q + 8, :], 1.0, None, ALU.add))
                    if self.blk:
                        g0 = col["norm1" if q == 1 else "norm2"] + 8 * self.layer
                        dve_link(ch, dve.tensor_tensor(m[:, 8 * q:8 * q + 8, :], m[:, 8 * q:8 * q + 8, :],
                                                       bc(VT[:, g0:g0 + 8], 2), ALU.mult))
                if not self.blk:
                    for q in (2, 5):
                        dve_link(ch, dve.tensor_scalar(m[:, 8 * q:8 * q + 8, :], m[:, 8 * q:8 * q + 8, :], 1.0 / ALPHA,
                                                       None, ALU.mult))

        def snaked(ap, rev):
            g = ap.rearrange("p (r two c) -> p r two c", two=2, c=GRID)
            return g[:, :, 0, :], (g[:, :, 1, ::-1] if rev else g[:, :, 1, :])

        class Modulate(Stage):
            def __init__(self, m, q, has_ctx, snake):
                self.m, self.q, self.has_ctx, self.snake = m, q, has_ctx, snake

            def act(self, act, B, ch):
                m, q = self.m, self.q
                for k in range(KD):
                    kw = dict(scale=m[:, 8 * (q + 1) + k, 0:1], bias=m[:, 8 * q + k, 0:1])
                    if self.snake:
                        for o, i in zip(snaked(uT[:, k, 0:LAT], False), snaked(hT[:, k, 0:LAT], True)):
                            act.activation(o, i, ACT.Identity, **kw)
                    else:
                        act.activation(uT[:, k, 0:LAT], hT[:, k, 0:LAT], ACT.Identity, **kw)

            def dve(self, dve, B, ch):
                m, q = self.m, self.q
                for k in range(KD if self.has_ctx else 0):
                    dve.tensor_scalar(uT[:, k, LAT:TOK], hT[:, k, LAT:TOK], m[:, 8 * (q + 1) + k, 1:2],
                                      m[:, 8 * q + k, 1:2], ALU.mult, ALU.add)

        def rstd_dve(dve, B, ch, i, T, dim, eps, free=True):
            bank = B.full(dve, i)
            dve.tensor_scalar(rstd[:, 0:T], bank[:, 0:T], 1.0 / dim, eps, ALU.mult, ALU.add).then_inc(*S("var").given())
            dve.wait_ge(*S("root").taken("dve"))
            dve_link(ch, dve.reciprocal(rstd[:, 0:T], rstd[:, 0:T]))

        def rstd_act(act, T):
            act.wait_ge(*S("var").taken("act"))
            act.activation(rstd[:, 0:T], rstd[:, 0:T], ACT.Sqrt).then_inc(*S("root").given())

        class LayerNorm(Stage):
            products = 2

            def __init__(self, i, j, T):
                self.g, self.T = 16 * i + 8 * j, T
                self.sq = arena_at(0, KD, TOK)

            def pe(self, pe, B):
                T = self.T
                bank = B.empty(pe, 0)
                for k in range(KD):
                    ins = pe.matmul(bank[:, 0:T], one, hT[:, k, 0:T], start=(k == 0), stop=(k == KD - 1))
                ins.then_inc(full_sem, 1)
                bank = B.empty(pe, 1)
                for k in range(KD):
                    pe.wait_ge(*S("squares").taken("pe"))
                    ins = pe.matmul(bank[:, 0:T], one, self.sq[:, k, 0:T], start=(k == 0), stop=(k == KD - 1))
                ins.then_inc(full_sem, 1)

            def dve(self, dve, B, ch):
                T = self.T
                bank = B.full(dve, 0)
                for k in range(KD):
                    dve.scalar_tensor_tensor(out=hT[:, k, 0:T], in0=bank[:, 0:T], scalar=-1.0 / D, in1=hT[:, k, 0:T],
                                             op0=ALU.mult, op1=ALU.add).then_inc(*S("centred").given())
                dve_link(ch, dve.drain())
                B.release(dve, 0)
                rstd_dve(dve, B, ch, 1, T, D, LN_EPS / ALPHA ** 2)
                B.release(dve, 1)
                for k in range(KD):
                    dve.tensor_tensor(hT[:, k, 0:T], hT[:, k, 0:T], rstd[:, 0:T], ALU.mult).then_inc(*S("normed").given())

            def act(self, act, B, ch):
                T = self.T
                for k in range(KD):
                    act.wait_ge(*S("centred").taken("act"))
                    act.activation(self.sq[:, k, 0:T], hT[:, k, 0:T], ACT.Square).then_inc(*S("squares").given())
                rstd_act(act, T)
                for k in range(KD):
                    act.wait_ge(*S("normed").taken("act"))
                    act.activation(hT[:, k, 0:T], hT[:, k, 0:T], ACT.Identity, scale=vc("ln_g", self.g + k),
                                   bias=vc("ln_b", self.g + k))

        class RmsNorm(Stage):
            products = 1

            def __init__(self, m, q, T):
                self.m, self.q, self.T = m, q, T
                self.sq = arena_at(0, KD, TOK)

            def pe(self, pe, B):
                T = self.T
                bank = B.empty(pe, 0)
                for k in range(KD):
                    pe.wait_ge(*S("squares").taken("pe"))
                    ins = pe.matmul(bank[:, 0:T], one, self.sq[:, k, 0:T], start=(k == 0), stop=(k == KD - 1))
                ins.then_inc(full_sem, 1)

            def dve(self, dve, B, ch):
                T = self.T
                rstd_dve(dve, B, ch, 0, T, D, RMS_EPS)
                B.release(dve, 0)
                for k in range(KD):
                    dve.tensor_tensor(uT[:, k, 0:T], hT[:, k, 0:T], rstd[:, 0:T], ALU.mult).then_inc(*S("normed").given())

            def act(self, act, B, ch):
                T, m, q = self.T, self.m, self.q
                for k in range(KD):
                    act.activation(self.sq[:, k, 0:T], hT[:, k, 0:T], ACT.Square).then_inc(*S("squares").given())
                rstd_act(act, T)
                for k in range(KD):
                    act.wait_ge(*S("normed").taken("act"))
                    for s in range(T // LAT):
                        v = uT[:, k, s * LAT:s * LAT + LAT]
                        act.activation(v, v, ACT.Identity, scale=m[:, 8 * (q + 1) + k, s:s + 1],
                                       bias=m[:, 8 * q + k, s:s + 1])

        def feature_major(pe, B, i, w, c0, x, kt, t0, t1, m=P):
            bank = B.empty(pe, i)
            for k in range(kt):
                ins = pe.matmul(bank[0:m, 0:t1 - t0], w[:, k, c0:c0 + m], x[:, k, t0:t1], start=(k == 0),
                                stop=(k == kt - 1))
            ins.then_inc(full_sem, 1)

        def token_major(pe, B, i, w, c0, c1, x, kt, t):
            bank = B.empty(pe, i)
            for k in range(kt):
                ins = pe.matmul(bank[:, 0:c1 - c0], x[:, k, t * P:t * P + P], w[:, k, c0:c1], start=(k == 0),
                                stop=(k == kt - 1))
            ins.then_inc(full_sem, 1)

        class Residual(Stage):
            products = KD

            def __init__(self, w, x, kt, m, q, T, snake):
                self.x, self.kt, self.m, self.q, self.T, self.snake = x, kt, m, q, T, snake
                self.per = min(4, SLOT // (kt * P))
                self.w = w

            def pe(self, pe, B):
                for c in range(0, KD, self.per):
                    w = W.block(pe, [self.w[:, c * P:(c + self.per) * P]], self.kt)
                    for j in range(self.per):
                        feature_major(pe, B, c + j, w, j * P, self.x, self.kt, 0, self.T)
                    W.used(full_sem, B.base + c + self.per)

            def dve(self, dve, B, ch):
                for k in range(KD):
                    bank = B.full(dve, k)

                    def add(h, y, s):
                        return dve.scalar_tensor_tensor(out=h, in0=y, scalar=self.m[:, 8 * self.q + k, s:s + 1], in1=h,
                                                        op0=ALU.mult, op1=ALU.add)
                    if self.snake:
                        for y, h in zip(snaked(bank[:, 0:LAT], True), snaked(hT[:, k, 0:LAT], False)):
                            ins = add(h, y, 0)
                    else:
                        ins = add(hT[:, k, 0:LAT], bank[:, 0:LAT], 0)
                    if self.T == TOK:
                        ins = add(hT[:, k, LAT:TOK], bank[:, LAT:TOK], 1)
                    ins.then_inc(*B.free(k))

        class HiddenRelu2(Stage):

            def __init__(self, w1, T):
                self.T, self.hid = T, arena_at(0, 32, T)
                self.products, self.w1 = 32, w1

            def pe(self, pe, B):
                for c in range(8):
                    w = W.block(pe, [self.w1[:, c * 512:c * 512 + 512]], KD)
                    for j in range(4):
                        feature_major(pe, B, 4 * c + j, w, j * P, uT, KD, 0, self.T)
                    W.used(full_sem, B.base + 4 * c + 4)

            def act(self, act, B, ch):
                for i in range(32):
                    bank = B.full(act, i)
                    if i >= 2:
                        act.wait_ge(*S("free_a").taken("act"))
                    act.activation(rl[i % 2][:, 0:self.T], bank[:, 0:self.T], ACT.Relu).then_inc(*B.free(i))
                for i in range(2):
                    act.wait_ge(*S("free_a").taken("act"))

            def dve(self, dve, B, ch):
                for i in range(32):
                    B.freed(dve, i)
                    r = rl[i % 2][:, 0:self.T]
                    dve.tensor_tensor(self.hid[:, i, :], r, r, ALU.mult).then_inc(*S("free_a").given())


        HQ = 4
        g_q = arena_at(0, 4, TOK)
        g_k = arena_at(2048, 4, TOK)
        g_v = arena_at(4096, 4, D)
        g_g = arena_at(8192, KD, TOK)
        g_o = arena_at(12288, KD, TOK)
        g_lg = arena_at(16384, 4, 2 * 512)
        g_a = arena_at(20480, 2, TOK)
        ab = arena_at(21504, TOK)
        aexp = arena_at(22016, TOK)

        class GlaProject(Stage):
            products = 4 + 4 + 8 + 8 + 2 + 8

            def pe(self, pe, B):
                w_in = I["gla_w_in"][0]
                i = 0
                for c in range(6):
                    w = W.block(pe, [w_in[:, c * 512:c * 512 + 512]], KD)
                    for j in range(4):
                        if c in (2, 3):
                            token_major(pe, B, i, w, 0, 512, uT, KD, j)
                        else:
                            feature_major(pe, B, i, w, j * P, uT, KD, 0, TOK)
                        i += 1
                    W.used(full_sem, B.base + i)
                w = W.block(pe, [w_in[:, 3072:3104]], KD)
                for z in range(2):
                    feature_major(pe, B, i, w, 16 * z, uT, KD, 0, TOK, m=16)
                    i += 1
                W.used(full_sem, B.base + i)
                pe.wait_ge(*S("a_rows").taken("pe"))
                for t in range(4):
                    for z in range(2):
                        bank = B.empty(pe, i)
                        pe.matmul(bank[:, :], g_a[0:17, z, t * P:t * P + P], wa2[0:17, z, :], start=True,
                                  stop=True).then_inc(full_sem, 1)
                        i += 1

            def act(self, act, B, ch):
                for i in range(4):
                    bank = B.full(act, i)
                    act.activation(g_q[:, i, :], bank[:, :], ACT.Copy, scale=float(P) ** -0.5).then_inc(*B.free(i))
                for i in range(16, 24):
                    bank = B.full(act, i)
                    act.activation(g_g[:, i - 16, :], bank[:, :], ACT.Silu).then_inc(*B.free(i))
                for i in range(26, 34):
                    bank = B.full(act, i)
                    if i > 26:
                        act.wait_ge(*S("free_a").taken("act"))
                    ch.wait(ch(act.activation(ab, bank[:, :], ACT.Abs)))
                    ch.wait(ch(act.activation(ab, ab, ACT.Exp, scale=-1.0)))
                    act.activation(aexp, ab, ACT.Ln, bias=1.0).then_inc(*S("sg_exp").given())
                act.wait_ge(*S("free_a").taken("act"))

            def dve(self, dve, B, ch):
                dve_link(ch, dve.memset(g_a[0:32, :, :], 1.0))
                for i in range(4, 16):
                    bank = B.full(dve, i)
                    dst = g_k[:, i - 4, :] if i < 8 else g_v[:, (i - 8) % 4, 512 * ((i - 8) // 4):512 * ((i - 8) // 4) + 512]
                    dve.tensor_copy(dst, bank[:, :]).then_inc(*B.free(i))
                for z in range(2):
                    bank = B.full(dve, 24 + z)
                    dve.tensor_copy(g_a[0:16, z, :], bank[0:16, :]).then_inc(*B.free(24 + z))
                S("a_rows").given()
                dve.drain().then_inc(S("a_rows").sem, 1)
                for i in range(26, 34):
                    t, z = (i - 26) // 2, (i - 26) % 2
                    dve.wait_ge(*S("sg_exp").taken("dve"))
                    dve.scalar_tensor_tensor(out=g_lg[:, t, z * 512:z * 512 + 512], in0=B[i][:, :], scalar=0.0, in1=aexp,
                                             op0=ALU.min, op1=ALU.subtract).then_inc(*S("free_a").given())
                    dve.drain().then_inc(*B.free(i))

        uf = uT[:, :, :].rearrange("p k t -> p (k t)")

        def heads(off, n=P):
            return uf[:, off:off + HQ * n].rearrange("p (h t) -> p h t", h=HQ)

        d_s, q_s, k_s, e1_s, sm_s, kt_s = (heads(512 * i) for i in range(6))
        sf_s = uf[:, 3072:4096].rearrange("p (h v) -> p h v", h=HQ)
        st_s = arena_at(21504, 4, 256)
        r_s, last_s, er_s, el_s, elr_s, lr_s = (small[:, 4 * i:4 * i + 4] for i in range(6))

        class GlaScan(Stage):
            steps = [(z, t, n) for z in range(2) for n, t in enumerate([(2, 3, 0, 1), (3, 2, 1, 0)][z])]
            products = sum(7 if n < 3 else 5 for _, _, n in steps)

            def pe(self, pe, B):
                i = 0
                for z, t, n in self.steps:
                    bank = B.empty(pe, i)
                    for h in range(HQ):
                        ins = pe.matmul(bank[:, h * P:h * P + P], g_lg[:, t, z * 512 + h * P:z * 512 + h * P + P],
                                        tri[z], start=True, stop=True)
                    ins.then_inc(full_sem, 1)
                    pe.wait_ge(*S("gla_q").taken("pe"))
                    bank = B.empty(pe, i + 1)
                    for h in range(HQ):
                        ins = pe.matmul(bank[:, h * P:h * P + P], k_s[:, h, :], q_s[:, h, :], start=True, stop=True)
                    ins.then_inc(full_sem, 1)
                    bank = B.empty(pe, i + 2)
                    for h in range(HQ):
                        ins = pe.transpose(bank[:, h * P:h * P + P], k_s[:, h, :], ident)
                    ins.then_inc(full_sem, 1)
                    pe.wait_ge(*S("gla_sm").taken("pe"))
                    if n:
                        pe.wait_ge(*S("gla_sp").taken("pe"))
                    for b in range(2):
                        bank = B.empty(pe, i + 3 + b)
                        for j in range(4):
                            h, v = 2 * b + j // 2, j % 2
                            ins = pe.matmul(bank[:, j * P:j * P + P], g_v[:, t, h * 256 + v * P:h * 256 + v * P + P],
                                            sm_s[:, h, :], start=True, stop=(n == 0))
                            if n:
                                ins = pe.matmul(bank[:, j * P:j * P + P], sf_s[:, h, v * P:v * P + P], q_s[:, h, :],
                                                start=False, stop=True)
                        ins.then_inc(full_sem, 1)
                    if n < 3:
                        B.freed(pe, i + 2)
                        for b in range(2):
                            bank = B.empty(pe, i + 5 + b)
                            for j in range(2):
                                h = 2 * b + j
                                ins = pe.matmul(bank[:, j * 256:j * 256 + 256], kt_s[:, h, :],
                                                g_v[:, t, h * 256:h * 256 + 256], start=True, stop=True)
                            ins.then_inc(full_sem, 1)
                    i += 7 if n < 3 else 5

            def act(self, act, B, ch):
                i = 0
                for z, t, n in self.steps:
                    act.wait_ge(*S("gla_d").taken("act"))
                    act.activation(e1_s, d_s, ACT.Exp, scale=1 / 16).then_inc(*S("gla_e").given())
                    ch.wait(ch(act.drain()))
                    act.activation(d_s, d_s, ACT.Exp, scale=-1 / 16).then_inc(*S("gla_e").given())
                    act.activation(er_s, r_s, ACT.Exp, scale=1 / 16)
                    act.activation(el_s, last_s, ACT.Exp, scale=1 / 16)
                    act.activation(elr_s, lr_s, ACT.Exp, scale=1 / 16).then_inc(*S("gla_el").given())
                    bank = B.full(act, i + 2)
                    act.activation(kt_s, bank[:, :].rearrange("p (h t) -> p h t", h=HQ), ACT.Copy).then_inc(*B.free(i + 2))
                    i += 7 if n < 3 else 5

            def dve(self, dve, B, ch):
                i = 0
                for z, t, n in self.steps:
                    mid, last = (63, 127) if z == 0 else (64, 0)
                    bank = B.full(dve, i)
                    cum = bank[:, :].rearrange("p (h t) -> p h t", h=HQ)
                    dve.tensor_copy(r_s, cum[:, :, mid])
                    dve_link(ch, dve.tensor_copy(last_s, cum[:, :, last]))
                    dve_link(ch, dve.tensor_tensor(lr_s, last_s, r_s, ALU.subtract))
                    dve_link(ch, dve.tensor_tensor(d_s, cum, bc(r_s, P), ALU.subtract))
                    S("gla_d").given()
                    dve.drain().then_inc(S("gla_d").sem, 1)
                    B.release(dve, i)
                    dve.wait_ge(*S("gla_e").taken("dve"))
                    dve.tensor_tensor(q_s, e1_s, g_q[:, :, t * P:t * P + P], ALU.mult)
                    dve.wait_ge(*S("gla_e").taken("dve"))
                    dve.tensor_tensor(k_s, d_s, g_k[:, :, t * P:t * P + P], ALU.mult).then_inc(*S("gla_q").given())
                    dve.wait_ge(*S("gla_el").taken("dve"))
                    if n:
                        dve.tensor_tensor(sf_s, st_s, bc(er_s, 256), ALU.mult).then_inc(*S("gla_sp").given())
                    bank = B.full(dve, i + 1)
                    dve.tensor_tensor(sm_s, bank[:, :].rearrange("p (h t) -> p h t", h=HQ), bcm(tri[z], HQ),
                                      ALU.mult).then_inc(*S("gla_sm").given())
                    B.release(dve, i + 1)
                    for b in range(2):
                        bank = B.full(dve, i + 3 + b)
                        src = bank[:, :].rearrange("p (h t) -> p h t", h=4)
                        dst = g_o[:, 4 * b:4 * b + 4, t * P:t * P + P]
                        if z == 0:
                            dve.tensor_copy(dst, src).then_inc(*B.free(i + 3 + b))
                        else:
                            dve.tensor_tensor(dst, src, dst, ALU.add).then_inc(*B.free(i + 3 + b))
                    if n < 3:
                        if n:
                            dve_link(ch, dve.tensor_tensor(st_s, st_s, bc(el_s, 256), ALU.mult))
                        for b in range(2):
                            bank = B.full(dve, i + 5 + b)
                            for j in range(2):
                                h = 2 * b + j
                                if n:
                                    ins = dve.scalar_tensor_tensor(out=st_s[:, h, :], in0=bank[:, j * 256:j * 256 + 256],
                                                                   scalar=elr_s[:, h:h + 1], in1=st_s[:, h, :],
                                                                   op0=ALU.mult, op1=ALU.add)
                                else:
                                    ins = dve.tensor_scalar(st_s[:, h, :], bank[:, j * 256:j * 256 + 256],
                                                            elr_s[:, h:h + 1], None, ALU.mult)
                            ins.then_inc(*B.free(i + 5 + b))
                        dve_link(ch, dve.drain())
                    i += 7 if n < 3 else 5

        class GlaGate(Stage):
            products = HQ

            def pe(self, pe, B):
                for h in range(HQ):
                    bank = B.empty(pe, h)
                    for v in range(2):
                        pe.wait_ge(*S("squares").taken("pe"))
                        ins = pe.matmul(bank[:, :], one, uT[:, 2 * h + v, :], start=(v == 0), stop=(v == 1))
                    ins.then_inc(full_sem, 1)

            def act(self, act, B, ch):
                for k in range(KD):
                    act.activation(uT[:, k, :], g_o[:, k, :], ACT.Square).then_inc(*S("squares").given())
                for h in range(HQ):
                    rstd_act(act, TOK)

            def dve(self, dve, B, ch):
                for h in range(HQ):
                    rstd_dve(dve, B, ch, h, TOK, 256, RMS_EPS)
                    B.release(dve, h)
                    for v in range(2):
                        k = 2 * h + v
                        dve_link(ch, dve.scalar_tensor_tensor(out=g_o[:, k, :], in0=g_o[:, k, :], scalar=vc("gla_norm", v),
                                                              in1=rstd[:, :], op0=ALU.mult, op1=ALU.mult))
                        dve_link(ch, dve.tensor_tensor(g_o[:, k, :], g_o[:, k, :], g_g[:, k, :], ALU.mult))

        NG = 8
        s_z = arena_at(0, 16, LAT)
        s_y = arena_at(4096, 16, LAT)
        s_dt = arena_at(8192, 4, 64)
        s_da = arena_at(8448, 4, 64)
        s_cj = arena_at(8704, 4, 64)
        s_t1 = arena_at(8960, 64)
        s_t2 = arena_at(9024, 64)
        PADW = LAT + 4
        s_raw = arena[:, 9088:9088 + 4 * 2 * PADW].rearrange("p (f s t) -> p f s t", f=4, s=2)
        s_acc = arena_at(11168, 2, TOK)
        s_f = arena_at(12192, 3, TOK)
        s_c = arena_at(13728, 2, LAT)
        s_xb = arena_at(14240, 2, 4 * 384)
        s_cb = arena_at(17312, 4, P)
        s_dab = [arena_at(17824 + 2048 * i, 4, P) for i in range(2)]
        s_m = [arena_at(18336 + 2048 * i, 4, P) for i in range(2)]
        s_cx = [arena_at(18848 + 2048 * i, 4, P) for i in range(2)]
        s_xdt = [arena_at(19360 + 2048 * i, 4, 64) for i in range(2)]
        s_xw = [arena_at(19616 + 2048 * i, 4, 64) for i in range(2)]
        s_st = arena_at(21920, 2, 256)
        s_lw = [small[:, 32 + 8 * i:36 + 8 * i] for i in range(3)]
        s_el = [small[:, 36 + 8 * i:40 + 8 * i] for i in range(3)]

        class SsdGates(Stage):
            products = 16 + 4 + 1

            def pe(self, pe, B):
                w_in = I["ssd_w_in"][0]
                for c in range(4):
                    w = W.block(pe, [w_in[:, c * 512:c * 512 + 512]], KD)
                    for j in range(4):
                        feature_major(pe, B, 4 * c + j, w, j * P, uT, KD, 0, LAT)
                    W.used(full_sem, B.base + 4 * c + 4)
                w = W.block(pe, [w_in[:, 6144:6208]], KD)
                for t in range(4):
                    token_major(pe, B, 16 + t, w, 0, 64, uT, KD, t)
                W.used(full_sem, B.base + 20)
                pe.wait_ge(*S("da_done").taken("pe"))
                bank = B.empty(pe, 20)
                for t in range(4):
                    for z in range(2):
                        c = 64 * t + 32 * z
                        ins = pe.matmul(bank[:, c:c + 32], tri[z], s_da[:, t, 32 * z:32 * z + 32], start=True, stop=True)
                ins.then_inc(full_sem, 1)

            def act(self, act, B, ch):
                for i in range(16):
                    bank = B.full(act, i)
                    act.activation(s_z[:, i, :], bank[:, 0:LAT], ACT.Silu).then_inc(*B.free(i))
                ch.wait(ch(act.activation(alog[:, :], alog[:, :], ACT.Exp)))
                for t in range(4):
                    act.wait_ge(*S("dti").taken("act"))
                    ch.wait(ch(act.activation(s_t1, s_dt[:, t, :], ACT.Abs)))
                    ch.wait(ch(act.activation(s_t1, s_t1, ACT.Exp, scale=-1.0)))
                    act.activation(s_t2, s_t1, ACT.Ln, bias=1.0).then_inc(*S("dtx").given())

            def dve(self, dve, B, ch):
                dve_link(ch, dve.memset(arena[:, 9088:9088 + 4 * 2 * PADW], 0.0))
                for t in range(4):
                    bank = B.full(dve, 16 + t)
                    dve.tensor_tensor(s_dt[:, t, :], bank[:, 0:64], dtb[:, :], ALU.add).then_inc(*S("dti").given())
                    B.release(dve, 16 + t)
                    dve.wait_ge(*S("dtx").taken("dve"))
                    dve_link(ch, dve.scalar_tensor_tensor(out=s_dt[:, t, :], in0=s_dt[:, t, :], scalar=0.0, in1=s_t2,
                                                          op0=ALU.max, op1=ALU.add))
                    ins = dve.scalar_tensor_tensor(out=s_da[:, t, :], in0=s_dt[:, t, :], scalar=-1.0, in1=alog[:, :],
                                                   op0=ALU.mult, op1=ALU.mult)
                    dve_link(ch, ins)
                S("da_done").given()
                dve.drain().then_inc(S("da_done").sem, 1)
                bank = B.full(dve, 20)
                dve.tensor_copy(s_cj, bank[:, 0:256].rearrange("p (t h) -> p t h", t=4)).then_inc(*B.free(20))

        class SsdGroups(Stage):
            steps = [(0, 2), (1, 3), (0, 3), (1, 2), (0, 0), (1, 1), (0, 1), (1, 0)]

            def __init__(self):
                N, order = 8 * NG, []

                def ahead(g, n):
                    if g >= NG:
                        return []
                    out = [("project", g, n)] if n < 4 else []
                    if 1 <= n < 5:
                        out += [("convolve", g, n - 1)]
                    if n in (5, 6):
                        out += [("turn", g, 2 * (n - 5) + t) for t in range(2)]
                    if n == 6:
                        out += [("overlap", g, 0)]
                    return out
                for n in range(8):
                    order += ahead(0, n)
                order += [("spread", 0, 0), ("spread", 1, 0), ("sums", 0, 0), ("decays", 0, 0)]
                for k in range(N + 1):
                    if k + 1 < N:
                        order += [("sums", k + 1, 0)]
                    if k + 2 < N:
                        order += [("spread", k + 2, 0)]
                    if k < N:
                        order += [("products", k, 0)]
                    if k:
                        order += [("state", k - 1, 0)]
                    if k + 1 < N:
                        order += [("decays", k + 1, 0)]
                    if k < N:
                        order += ahead(k // 8 + 1, k % 8)
                self.order, self.index, i = order, {}, 0
                for ev in order:
                    kind, k, _ = ev
                    count = {"project": 1, "turn": 1, "overlap": 1, "sums": 1}.get(kind, 0)
                    if kind == "products":
                        z, t = self.steps[k % 8]
                        count = (t < 2) + (k % 8 < 6)
                    if count:
                        self.index[ev] = i
                        i += count
                self.products = i

            def tile(self, g, j):
                return [2 * g, 2 * g + 1, 16 + g, 24 + g][j]

            def last(self, k):
                z, t = self.steps[k % 8]
                return self.index["products", k, 0] + (t < 2) + (k % 8 < 6) - 1

            def feat(self, g, j):
                return s_f[:, j, :] if j < 3 else s_c[:, g % 2, :]

            def pe(self, pe, B):
                w_in = I["ssd_w_in"][0]
                w = None
                for ev in self.order:
                    kind, k, j = ev
                    i = self.index.get(ev)
                    if kind == "project":
                        if j == 0:
                            w = W.block(pe, [w_in[:, 2048 + k * 256:2048 + k * 256 + 256],
                                             w_in[:, 4096 + k * P:4096 + k * P + P],
                                             w_in[:, 5120 + k * P:5120 + k * P + P]], KD)
                        feature_major(pe, B, i, w, j * P, uT, KD, 0, LAT if j == 3 else TOK)
                        if j == 3:
                            W.used(full_sem, B.base + i + 1)
                    if kind == "turn":
                        if j == 0:
                            pe.wait_ge(*S("feat").taken("pe", 4))
                        bank = B.empty(pe, i)
                        for f in range(3):
                            ins = pe.transpose(bank[:, f * P:f * P + P], s_f[:, f, j * P:j * P + P], ident)
                        ins.then_inc(full_sem, 1)
                    if kind == "overlap":
                        bank = B.empty(pe, i)
                        for t in range(2):
                            ins = pe.matmul(bank[:, t * P:t * P + P], s_f[:, 2, t * P:t * P + P],
                                            s_c[:, k % 2, t * P:t * P + P], start=True, stop=True)
                        ins.then_inc(full_sem, 1)
                    if kind == "sums":
                        z, t = self.steps[k % 8]
                        pe.wait_ge(*S("dab").taken("pe"))
                        bank = B.empty(pe, i)
                        for h in range(4):
                            ins = pe.matmul(bank[:, h * P:h * P + P], s_dab[k % 2][:, h, :], tri[z], start=True, stop=True)
                        ins.then_inc(full_sem, 1)
                    if kind == "products":
                        (z, t), g, n = self.steps[k % 8], k // 8, k % 8
                        pe.wait_ge(*S("xw").taken("pe"))
                        if n >= 2:
                            pe.wait_ge(*S("st").taken("pe"))
                        if t < 2:
                            bank = B.empty(pe, i)
                            for h in range(4):
                                o = bank[64 * (h % 2):64 * (h % 2) + 64, (h // 2) * P:(h // 2) * P + P]
                                pe.matmul(o, s_xdt[k % 2][:, h, :], s_m[k % 2][:, h, :], start=True, stop=False)
                                ins = pe.matmul(o, s_st[:, z, h * 64:h * 64 + 64], s_cx[k % 2][:, h, :], start=False, stop=True)
                            ins.then_inc(full_sem, 1)
                            i += 1
                        if n < 6:
                            bank = B.empty(pe, i)
                            pe.matmul(bank[:, 0:256], s_xb[:, g % 2, t * 384 + 256:t * 384 + 384], s_xw[k % 2][:, :, :],
                                      start=True, stop=True).then_inc(full_sem, 1)

            def act(self, act, B, ch):
                for ev in self.order:
                    kind, k, j = ev
                    i = self.index.get(ev)
                    if kind == "project":
                        bank = B.full(act, i)
                        if k:
                            act.wait_ge(*S("conv").taken("act"))
                        n = 1 if j == 3 else 2
                        act.activation(s_raw[:, j, 0:n, 2:2 + LAT], bank[:, 0:n * LAT].rearrange("p (s t) -> p s t", s=n),
                                       ACT.Copy).then_inc(*B.free(i))
                    if kind == "convolve":
                        T = LAT if j == 3 else TOK
                        act.wait_ge(*S("convd").taken("act"))
                        act.activation(self.feat(k, j)[:, 0:T], s_acc[:, j % 2, 0:T], ACT.Silu,
                                       bias=vc("conv_b", self.tile(k, j))).then_inc(*S("feat").given())
                    if kind == "turn":
                        bank = B.full(act, i)
                        act.activation(s_xb[:, k % 2, j * 384:j * 384 + 384], bank[:, 0:384], ACT.Copy).then_inc(*B.free(i))
                    if kind == "spread":
                        (z, t), g = self.steps[k % 8], k // 8
                        c = 32 * z + 4 * g
                        if k >= 2:
                            B.full(act, self.index["sums", k - 2, 0])
                        act.activation(s_dab[k % 2], bc(s_da[:, t, c:c + 4], P), ACT.Copy).then_inc(*S("dab").given())
                    if kind == "sums" and self.steps[k % 8][1] < 2:
                        bank = B.full(act, i)
                        if k >= 2:
                            B.full(act, self.last(k - 2))
                        act.activation(s_cx[k % 2], bank[:, :].rearrange("p (h t) -> p h t", h=4),
                                       ACT.Exp).then_inc(*S("ecx").given())
                    if kind == "decays":
                        if self.steps[k % 8][1] < 2:
                            act.wait_ge(*S("seg").taken("act"))
                            act.activation(s_m[k % 2], s_m[k % 2], ACT.Exp).then_inc(*S("segx").given())
                        act.wait_ge(*S("lw").taken("act"))
                        lo = 32 + 8 * (k % 3)
                        act.activation(small[:, lo:lo + 8], small[:, lo:lo + 8], ACT.Exp).then_inc(*S("lwx").given())

            def dve(self, dve, B, ch):
                for ev in self.order:
                    kind, k, j = ev
                    i = self.index.get(ev)
                    if kind == "convolve":
                        f = self.tile(k, j)
                        n = 1 if j == 3 else 2
                        B.freed(dve, self.index["project", k, j])
                        if j >= 2:
                            dve.wait_ge(*S("feat").taken("dve"))
                        acc = s_acc[:, j % 2, 0:n * LAT].rearrange("p (s t) -> p s t", s=n)
                        dve_link(ch, dve.tensor_scalar(acc, s_raw[:, j, 0:n, 0:LAT], vc("conv_w", f), None, ALU.mult))
                        for tap in range(1, 5):
                            ins = dve.scalar_tensor_tensor(out=acc, in0=s_raw[:, j, 0:n, tap:tap + LAT],
                                                           scalar=vc("conv_w", 32 * tap + f), in1=acc,
                                                           op0=ALU.mult, op1=ALU.add)
                            if tap < 4:
                                dve_link(ch, ins)
                            else:
                                ins.then_inc(*S("convd").given())
                        if k < NG - 1:
                            dve.drain().then_inc(*S("conv").given())
                    if kind == "overlap":
                        dve.wait_ge(*S("feat").taken("dve", 2))
                        bank = B.full(dve, i)
                        for f in range(2):
                            c = 2 * k + f
                            dve.tensor_scalar(s_y[:, c, :], s_f[:, f, 0:LAT], dcol[:, c:c + 1], None, ALU.mult)
                        for z in range(2):
                            dve_link(ch, dve.tensor_tensor(s_cb[:, 2 * z:2 * z + 2, :],
                                                           bank[:, 0:256].rearrange("p (t i) -> p t i", t=2),
                                                           bcm(tri[z], 2), ALU.mult))
                        B.release(dve, i)
                        for t in range(4):
                            B.freed(dve, self.index["turn", k, t])
                    if kind == "sums":
                        (z, t), g = self.steps[k % 8], k // 8
                        c = 32 * z + 4 * g
                        last = 127 if z == 0 else 0
                        cj = s_cj[:, t, c:c + 4]
                        bank = B.full(dve, i)
                        cum = bank[:, :].rearrange("p (h t) -> p h t", h=4)
                        if t < 2:
                            dve.wait_ge(*S("ecx").taken("dve"))
                            if k >= 2:
                                B.full(dve, self.last(k - 2))
                            for h in range(4):
                                ins = dve.tensor_scalar(s_m[k % 2][:, h, :], cum[:, h, :], cj[:, h:h + 1], 0.0,
                                                        ALU.subtract, ALU.min)
                            ins.then_inc(*S("seg").given())
                        dve.tensor_copy(s_el[k % 3], cum[:, :, last])
                        dve.tensor_tensor(s_lw[k % 3], cum[:, :, last], cj, ALU.subtract).then_inc(*S("lw").given())
                        B.release(dve, i)
                    if kind == "decays":
                        (z, t), g = self.steps[k % 8], k // 8
                        c = 32 * z + 4 * g
                        xdt, xw = s_xdt[k % 2], s_xw[k % 2]
                        dve_link(ch, dve.tensor_tensor(xdt, s_xb[:, g % 2, t * 384:t * 384 + 256].rearrange(
                            "p (h d) -> p h d", h=4), bc(s_dt[:, t, c:c + 4], 64), ALU.mult))
                        if t < 2:
                            dve.tensor_tensor(s_cx[k % 2], s_cx[k % 2], bcm(s_c[:, g % 2, t * P:t * P + P], 4), ALU.mult)
                            dve.wait_ge(*S("segx").taken("dve"))
                            dve_link(ch, dve.tensor_tensor(s_m[k % 2], s_m[k % 2], bcm(s_cb[:, 2 * z + t, :], 4), ALU.mult))
                        dve.wait_ge(*S("lwx").taken("dve"))
                        dve.tensor_tensor(xw, xdt, bc(s_lw[k % 3], 64), ALU.mult).then_inc(*S("xw").given())
                    if kind == "state":
                        (z, t), g, n = self.steps[k % 8], k // 8, k % 8
                        i = self.index["products", k, 0]
                        if t < 2:
                            bank = B.full(dve, i)
                            y = s_y[:, 2 * g:2 * g + 2, t * P:t * P + P]
                            dve.tensor_tensor(y, bank[:, 0:256].rearrange("p (f i) -> p f i", f=2), y,
                                              ALU.add).then_inc(*B.free(i))
                            i += 1
                        if n < 6:
                            st = s_st[:, z, :]
                            if n >= 2:
                                v = st.rearrange("p (h d) -> p h d", h=4)
                                dve_link(ch, dve.tensor_tensor(v, v, bc(s_el[k % 3], 64), ALU.mult))
                            bank = B.full(dve, i)
                            if n >= 2:
                                ins = dve.tensor_tensor(st, bank[:, 0:256], st, ALU.add)
                            else:
                                ins = dve.tensor_copy(st, bank[:, 0:256])
                            ins.then_inc(*S("st").given())
                            B.release(dve, i)

        s_sq = arena_at(9088, 16, LAT)

        class SsdGate(Stage):
            products = 1

            def pe(self, pe, B):
                bank = B.empty(pe, 0)
                for k in range(16):
                    pe.wait_ge(*S("squares").taken("pe"))
                    ins = pe.matmul(bank[:, 0:LAT], one, s_sq[:, k, :], start=(k == 0), stop=(k == 15))
                ins.then_inc(full_sem, 1)

            def act(self, act, B, ch):
                for k in range(16):
                    act.wait_ge(*S("normed").taken("act"))
                    act.activation(s_sq[:, k, :], s_y[:, k, :], ACT.Square).then_inc(*S("squares").given())
                rstd_act(act, LAT)

            def dve(self, dve, B, ch):
                for k in range(16):
                    dve.tensor_tensor(s_y[:, k, :], s_y[:, k, :], s_z[:, k, :], ALU.mult).then_inc(*S("normed").given())
                dve_link(ch, dve.drain())
                rstd_dve(dve, B, ch, 0, LAT, 2048, RMS_EPS)
                B.release(dve, 0)
                for k in range(16):
                    dve.scalar_tensor_tensor(out=s_y[:, k, :], in0=s_y[:, k, :], scalar=vc("ssd_norm", k), in1=rstd[:, 0:LAT],
                                             op0=ALU.mult, op1=ALU.mult)

        class LoadCtx(Stage):
            products = KD

            def act(self, act, B, ch):
                act.dma_start(xrow[:, 0:2, :], I["ctx_2"].rearrange("o (t p) d -> p (o t) d", p=P))\
                   .then_inc(S("bias_loads").sem, 16)

            def pe(self, pe, B):
                pe.wait_ge(S("bias_loads").sem, 16)
                for k in range(KD):
                    bank = B.empty(pe, k)
                    for t in range(2):
                        ins = pe.transpose(bank[:, t * P:t * P + P], xrow[:, t, k * P:k * P + P], ident)
                    ins.then_inc(full_sem, 1)

            def dve(self, dve, B, ch):
                for k in range(KD):
                    bank = B.full(dve, k)
                    dve.tensor_copy(hT[:, k, LAT:TOK], bank[:, 0:CTX]).then_inc(*B.free(k))

        m_y = arena_at(0, KD, TOK)
        m_q = arena_at(4096, 8, TOK)
        m_k = arena_at(8192, 6, TOK)
        m_v = arena_at(11264, 4, 640)
        m_g = arena_at(13824, 4, TOK)
        m_bias = arena_at(13824, 8, 6, GRID)
        m_pad = arena_at(15872, 4, 2 * (LAT + 2))
        m_gc = arena_at(6144, 4, TOK)
        m_s = [[uT[:, 2 * i + j, :] for j in range(2)] for i in range(2)]
        m_pt = [uT[:, 4 + i, :] for i in range(2)]
        sinks = sb("sinks", [P, 8])

        class EvenProject(Stage):
            products = 24

            def pe(self, pe, B):
                w_in = I["ev_w_in_2"][0]
                for c in range(6):
                    w = W.block(pe, [w_in[:, c * 512:c * 512 + 512]], KD)
                    for j in range(4):
                        if c == 5:
                            token_major(pe, B, 4 * c + j, w, 0, 512, uT, KD, j)
                        else:
                            feature_major(pe, B, 4 * c + j, w, j * P, uT, KD, 0, TOK)
                    W.used(full_sem, B.base + 4 * c + 4)

            def act(self, act, B, ch):
                for i in range(8):
                    bank = B.full(act, i)
                    act.activation((m_g if i < 4 else m_gc)[:, i % 4, :], bank[:, :], ACT.Copy).then_inc(*B.free(i))
                for i in range(12, 24, 2):
                    bank = B.full(act, i)
                    act.activation(self.dst(i), bank[:, :], ACT.Copy).then_inc(*B.free(i))

            def dst(self, i):
                return [m_q, m_k, m_v][(i - 12) // 4][:, i % 4, 0:512]

            def dve(self, dve, B, ch):
                dve_link(ch, dve.memset(arena[:, 15872:15872 + 8 * (LAT + 2)], 0.0))
                for j in range(4):
                    pad = m_pad[:, j, :].rearrange("p (s t) -> p s t", s=2)
                    acc = m_y[:, j, :].rearrange("p (s t) -> p s t", s=2)
                    bank = B.full(dve, 8 + j)
                    B.freed(dve, 4 + j)
                    dve.tensor_tensor(pad[:, :, 1:1 + LAT], bank[:, :].rearrange("p (s t) -> p s t", s=2),
                                      m_gc[:, j, :].rearrange("p (s t) -> p s t", s=2), ALU.mult).then_inc(*B.free(8 + j))
                    B.freed(dve, 8 + j)
                    dve_link(ch, dve.tensor_scalar(acc, pad[:, :, 0:LAT], vc("ev_conv", j), None, ALU.mult))
                    for tap in (1, 2):
                        dve_link(ch, dve.scalar_tensor_tensor(out=acc, in0=pad[:, :, tap:tap + LAT],
                                                              scalar=vc("ev_conv", 4 * tap + j), in1=acc,
                                                              op0=ALU.mult, op1=ALU.add))
                    dve_link(ch, dve.tensor_tensor(m_y[:, j, :], m_y[:, j, :], m_g[:, j, :], ALU.mult))
                for i in range(13, 24, 2):
                    bank = B.full(dve, i)
                    dve.tensor_copy(self.dst(i), bank[:, :]).then_inc(*B.free(i))

        m_braw = arena_at(16896, 8, 6, GRID)

        class BiasLoad(Stage):
            products = 6

            def act(self, act, B, ch):
                t = I["ev_rpb_2"]
                for b in range(2):
                    for h in range(8):
                        src = bass.AP(tensor=t.tensor, offset=h * 15 * 31 + (5 - b) * 31 + 15 - 63,
                                      ap=[[1, GRID], [31, 6], [1, GRID]])
                        act.dma_start(m_braw[64 * b:64 * b + 64, h, :, :], src).then_inc(S("moe_loads").sem, 16)

            def pe(self, pe, B):
                pe.wait_ge(S("moe_loads").sem, 16 * 16)
                raw = m_braw.rearrange("p h m c -> p (h m c)")
                for i in range(6):
                    bank = B.empty(pe, i)
                    pe.matmul(bank[:, :], const[:, C_FLIP:C_FLIP + P], raw[:, i * 512:i * 512 + 512], start=True,
                              stop=True).then_inc(full_sem, 1)

            def dve(self, dve, B, ch):
                v = m_bias.rearrange("p h m c -> p (h m) c")
                for i in range(6):
                    bank = B.full(dve, i)
                    dve.tensor_tensor(v[:, 8 * i:8 * i + 8, :], bank[:, :].rearrange("p (a c) -> p a c", a=8),
                                      bcm(const[:, C_COL:C_COL + GRID], 8), ALU.add).then_inc(*B.free(i))

        class HeadNorm(Stage):

            def __init__(self, tiles, rope):
                self.tiles, self.rope = tiles, rope
                self.products = len(tiles) * (2 if rope else 1)
                self.sq = [rl[0], rl[1]]

            def pe(self, pe, B):
                n = len(self.tiles)
                for i, (x, gain, T) in enumerate(self.tiles):
                    pe.wait_ge(*S("squares").taken("pe"))
                    bank = B.empty(pe, i)
                    pe.matmul(bank[:, 0:T], half, self.sq[i % 2][:, 0:T], start=True, stop=True).then_inc(full_sem, 1)
                if self.rope:
                    for i, (x, gain, T) in enumerate(self.tiles):
                        pe.wait_ge(*S("rope_in").taken("pe"))
                        bank = B.empty(pe, n + i)
                        pe.matmul(bank[:, 0:LAT], rot, x[:, 0:LAT], start=True, stop=True).then_inc(full_sem, 1)

            def act(self, act, B, ch):
                for i, (x, gain, T) in enumerate(self.tiles):
                    if i >= 2:
                        B.full(act, i - 2)
                    act.activation(self.sq[i % 2][:, 0:T], x, ACT.Square).then_inc(*S("squares").given())
                    if i >= 1:
                        rstd_act(act, self.tiles[i - 1][2])
                rstd_act(act, self.tiles[-1][2])

            def dve(self, dve, B, ch):
                n = len(self.tiles)
                for i, (x, gain, T) in enumerate(self.tiles):
                    rstd_dve(dve, B, ch, i, T, 64, RMS_EPS)
                    B.release(dve, i)
                    ins = dve.scalar_tensor_tensor(out=x, in0=x, scalar=vc(gain), in1=rstd[:, 0:T], op0=ALU.mult, op1=ALU.mult)
                    if self.rope:
                        ins.then_inc(*S("rope_in").given())
                        dve.wait_ge(S("rope_in").sem, S("rope_in").made)
                    else:
                        dve_link(ch, ins)
                if self.rope:
                    cos, sin = const[:, C_COS:C_COS + LAT], const[:, C_SIN:C_SIN + LAT]
                    for i, (x, gain, T) in enumerate(self.tiles):
                        bank = B.full(dve, n + i)
                        dve_link(ch, dve.tensor_tensor(rl[0][:, 0:LAT], bank[:, 0:LAT], sin, ALU.mult))
                        dve_link(ch, dve.tensor_tensor(x[:, 0:LAT], x[:, 0:LAT], cos, ALU.mult))
                        dve_link(ch, dve.tensor_tensor(x[:, 0:LAT], x[:, 0:LAT], rl[0][:, 0:LAT], ALU.add))
                        B.release(dve, n + i)

        class Attention(Stage):

            def __init__(self, items, lam=None):
                self.items, self.lam = items, lam
                self.ns = len(items[0]["q"])
                order = []
                for n in range(-1, len(items)):
                    if n + 1 < len(items):
                        order += [("s", n + 1, j) for j in range(self.ns)]
                    if n >= 0:
                        order += [("t", n, 0), ("o", n, 0)]
                self.order = {key: i for i, key in enumerate(order)}
                self.products = len(order)

            def pe(self, pe, B):
                for (kind, n, j), i in self.order.items():
                    it = self.items[n]
                    nk = it["nk"]
                    if kind == "s":
                        bank = B.empty(pe, i)
                        pe.matmul(bank[:, 0:nk], it["q"][j], it["k"][j], start=True, stop=True).then_inc(full_sem, 1)
                    elif kind == "t":
                        pe.wait_ge(*S("pn").taken("pe"))
                        bank = B.empty(pe, i)
                        for t in range(nk // P):
                            ins = pe.transpose(bank[:, t * P:t * P + P], m_s[n % 2][0][:, t * P:t * P + P], ident)
                        ins.then_inc(full_sem, 1)
                    else:
                        B.freed(pe, i - 1)
                        bank = B.empty(pe, i)
                        r0, m = it["rows"]
                        for t, v in enumerate(it["v"]):
                            ins = pe.matmul(bank[r0:r0 + m, 0:P], v, m_pt[n % 2][:, t * P:t * P + P], start=(t == 0),
                                            stop=(t == len(it["v"]) - 1))
                        ins.then_inc(full_sem, 1)

            def stats(self, n, j):
                o = 24 * (n % 2) + 12 * j
                return [small[:, o + x:o + x + 1] for x in range(5)]

            def act(self, act, B, ch):
                def exps(n):
                    it = self.items[n]
                    for j in range(self.ns):
                        mx, nm, den, es, rc = self.stats(n, j)
                        act.wait_ge(*S("nm").taken("act"))
                        s = m_s[n % 2][j][:, 0:it["nk"]]
                        if it["sink"] is not None:
                            act.activation(es, it["sink"], ACT.Exp, bias=nm)
                        act.activation(s, s, ACT.Exp, bias=nm, accum_out=den)
                        act.drain().then_inc(*S("pr").given())
                for n in range(-1, len(self.items)):
                    if n + 1 < len(self.items):
                        exps(n + 1)
                    if n >= 0:
                        i, nk = self.order["t", n, 0], self.items[n]["nk"]
                        if n >= 2:
                            B.full(act, self.order["o", n - 2, 0])
                        bank = B.full(act, i)
                        act.activation(m_pt[n % 2][:, 0:nk], bank[:, 0:nk], ACT.Copy).then_inc(*B.free(i))

            def dve(self, dve, B, ch):
                def scores(n):
                    it = self.items[n]
                    nk = it["nk"]
                    for j in range(self.ns):
                        mx, nm, den, es, rc = self.stats(n, j)
                        i = self.order["s", n, j]
                        bank = B.full(dve, i)
                        if n >= 2 and j == 0:
                            B.full(dve, self.order["t", n - 2, 0])
                        s = m_s[n % 2][j]
                        b = 0
                        if it["bias"] is not None:
                            b = LAT
                            dve.scalar_tensor_tensor(out=s[:, 0:b], in0=bank[:, 0:b], scalar=0.125, in1=it["bias"],
                                                     op0=ALU.mult, op1=ALU.add)
                        dve_link(ch, dve.tensor_scalar(s[:, b:nk], bank[:, b:nk], 0.125, None, ALU.mult))
                        B.release(dve, i)
                        dve_link(ch, dve.tensor_reduce(mx, s[:, 0:nk], AX.X, ALU.max))
                        if it["sink"] is not None:
                            dve_link(ch, dve.tensor_tensor(mx, mx, it["sink"], ALU.max))
                        dve.tensor_scalar(nm, mx, -1.0, None, ALU.mult).then_inc(*S("nm").given())

                def normalise(n):
                    it = self.items[n]
                    for j in range(self.ns):
                        mx, nm, den, es, rc = self.stats(n, j)
                        dve.wait_ge(*S("pr").taken("dve"))
                        if it["sink"] is not None:
                            dve_link(ch, dve.tensor_tensor(den, den, es, ALU.add))
                        dve_link(ch, dve.reciprocal(rc, den))
                    s0 = m_s[n % 2][0][:, 0:it["nk"]]
                    r0 = self.stats(n, 0)[4]
                    if self.ns == 1:
                        dve.tensor_scalar(s0, s0, r0, None, ALU.mult).then_inc(*S("pn").given())
                    else:
                        s1, r1 = m_s[n % 2][1][:, 0:it["nk"]], self.stats(n, 1)[4]
                        dve_link(ch, dve.tensor_scalar(s1, s1, r1, self.lam, ALU.mult, ALU.mult))
                        dve.scalar_tensor_tensor(out=s0, in0=s0, scalar=r0, in1=s1, op0=ALU.mult,
                                                 op1=ALU.add).then_inc(*S("pn").given())
                for n in range(-1, len(self.items)):
                    if n + 1 < len(self.items):
                        scores(n + 1)
                    if n >= 0:
                        normalise(n)
                        i = self.order["o", n, 0]
                        bank = B.full(dve, i)
                        r0, m = self.items[n]["rows"]
                        dve.tensor_copy(self.items[n]["o"], bank[r0:r0 + m, 0:P]).then_inc(*B.free(i))

        def even_items():
            items = []
            for h in range(8):
                r, f = 64 * (h % 2), h // 2
                for t in range(4):
                    lat = t < 2
                    ks = 0 if lat else LAT
                    items.append(dict(
                        q=[m_q[r:r + 64, f, t * P:t * P + P]], k=[m_k[r:r + 64, f, ks:TOK]], nk=TOK - ks,
                        bias=m_bias[:, h, 2 - 2 * t:6 - 2 * t, :].rearrange("p m c -> p (m c)") if lat else None, sink=None,
                        v=[m_v[:, j, h * 64:h * 64 + 64] for j in range(ks // P, 4)], rows=(r, 64),
                        o=m_y[r:r + 64, 4 + f, t * P:t * P + P]))
            return items

        def window_items():
            items = []
            for h in range(8):
                r, f = 64 * (h % 2), h // 2
                for t in range(2):
                    items.append(dict(
                        q=[m_q[r:r + 64, f, t * P:t * P + P]], k=[m_k[r:r + 64, h // 4, :]], nk=TOK,
                        bias=const[:, C_SWA + t * LAT:C_SWA + t * LAT + LAT], sink=sinks[:, h:h + 1],
                        v=[m_v[:, j, 64 * (h // 4):64 * (h // 4) + 64] for j in range(4)], rows=(r, 64),
                        o=m_y[r:r + 64, f, t * P:t * P + P]))
            return items

        def diff_items():
            return [dict(q=[m_q[64 * i:64 * i + 64, 4 + h, t * P:t * P + P] for i in range(2)],
                         k=[m_k[64 * i:64 * i + 64, 2 + h, :] for i in range(2)], nk=TOK, bias=None, sink=None,
                         v=[m_v[:, j, P + h * P:P + h * P + P] for j in range(4)], rows=(0, P),
                         o=m_y[:, 4 + h, t * P:t * P + P])
                    for h in range(4) for t in range(2)]

        class HiddenSwiglu(Stage):

            def __init__(self, w1, w3, T):
                self.nf, self.T = w1.shape[1] // P, T
                self.hid = arena_at(0, self.nf, T)
                self.products = 2 * self.nf
                self.w = (w1, w3)

            def pe(self, pe, B):
                for c in range(0, self.nf, 4):
                    n = min(4, self.nf - c)
                    a, b = (W.block(pe, [w[:, c * P:(c + n) * P]], KD) for w in self.w)
                    for j in range(n):
                        feature_major(pe, B, 2 * (c + j), a, j * P, uT, KD, 0, self.T)
                        feature_major(pe, B, 2 * (c + j) + 1, b, j * P, uT, KD, 0, self.T)
                    W.used(full_sem, B.base + 2 * (c + n))
                    W.used(full_sem, B.base + 2 * (c + n))

            def act(self, act, B, ch):
                for f in range(self.nf):
                    bank = B.full(act, 2 * f)
                    if f >= 2:
                        act.wait_ge(*S("free_a").taken("act"))
                    act.activation(rl[f % 2][:, 0:self.T], bank[:, 0:self.T], ACT.Silu).then_inc(*B.free(2 * f))
                for f in range(2):
                    act.wait_ge(*S("free_a").taken("act"))

            def dve(self, dve, B, ch):
                for f in range(self.nf):
                    B.freed(dve, 2 * f)
                    bank = B.full(dve, 2 * f + 1)
                    h = self.hid[:, f, :]
                    dve.tensor_tensor(h, bank[:, 0:self.T], rl[f % 2][:, 0:self.T], ALU.mult).then_inc(*S("free_a").given())
                    B.release(dve, 2 * f + 1)

        class OddProject(Stage):
            products = 4 + 4 + 1 + 4 + 4 + 4

            cuts = ((0, 512), (512, 1024), (1024, 1280), (1280, 1792), (1792, 2304))

            def pe(self, pe, B):
                i = 0
                for c, (c0, c1) in enumerate(self.cuts):
                    w = W.block(pe, [I["od_w_in_2"][0][:, c0:c1]], KD)
                    if c == 2:
                        feature_major(pe, B, i, w, 0, uT, KD, 0, TOK)
                        i += 1
                    for j in range(4):
                        if c == 2:
                            token_major(pe, B, i, w, P, 2 * P, uT, KD, j)
                        elif c == 4:
                            token_major(pe, B, i, w, 0, 512, uT, KD, j)
                        else:
                            feature_major(pe, B, i, w, j * P, uT, KD, 0, LAT if c < 2 else TOK)
                        i += 1
                    W.used(full_sem, B.base + i)

            def dst(self, i):
                if i < 8:
                    return m_q[:, i, 0:LAT]
                if i == 8:
                    return m_k[:, 0, :]
                if i < 13:
                    return m_v[:, i - 9, 0:P]
                if i < 17:
                    return m_k[:, 2 + i - 13, :]
                return m_v[:, i - 17, P:P + 512]

            def act(self, act, B, ch):
                for i in range(0, 21, 2):
                    bank, d = B.full(act, i), self.dst(i)
                    act.activation(d, bank[:, 0:d.shape[1]], ACT.Copy).then_inc(*B.free(i))

            def dve(self, dve, B, ch):
                for i in range(1, 21, 2):
                    bank, d = B.full(dve, i), self.dst(i)
                    dve.tensor_copy(d, bank[:, 0:d.shape[1]]).then_inc(*B.free(i))

        LAM_INIT = 0.8 - 0.6 * math.exp(-0.3)
        lam_t = small[:, 60:61]

        class KeysAndLambda(Stage):
            products = 3

            def pe(self, pe, B):
                for g in range(2):
                    bank = B.empty(pe, g)
                    pe.matmul(bank[:, :], const[:, C_DUP + g * P:C_DUP + g * P + P], m_k[:, 0, :], start=True,
                              stop=True).then_inc(full_sem, 1)
                pe.wait_ge(*S("lam").taken("pe"))
                bank = B.empty(pe, 2)
                pe.matmul(bank[:, 0:2], one[0:64, :], small[0:64, 56:58], start=True, stop=True).then_inc(full_sem, 1)

            def act(self, act, B, ch):
                act.dma_start(sinks[:, :], flat(I["od_sink_2"]).partition_broadcast(P)).then_inc(S("bias_loads").sem, 16)
                act.wait_ge(S("bias_loads").sem, 32)
                bank = B.full(act, 2)
                act.activation(small[:, 58:60], bank[:, 0:2], ACT.Exp).then_inc(*B.free(2))

            def dve(self, dve, B, ch):
                dve.tensor_tensor(small[0:64, 56:57], lamv[0:64, 0:1], lamv[0:64, 1:2], ALU.mult)
                dve.tensor_tensor(small[0:64, 57:58], lamv[0:64, 2:3], lamv[0:64, 3:4], ALU.mult).then_inc(*S("lam").given())
                for g in range(2):
                    B.full(dve, 1)
                    bank = B.full(dve, g)
                    dve.tensor_copy(m_k[:, g, :], bank[:, :]).then_inc(*B.free(g))
                B.freed(dve, 2)
                dve_link(ch, dve.tensor_tensor(lam_t, small[:, 59:60], small[:, 58:59], ALU.subtract))
                dve_link(ch, dve.tensor_scalar(lam_t, lam_t, -LAM_INIT, None, ALU.add))

        class SubNorm(Stage):
            products = 4

            def pe(self, pe, B):
                for h in range(4):
                    pe.wait_ge(*S("squares").taken("pe"))
                    bank = B.empty(pe, h)
                    pe.matmul(bank[:, 0:LAT], one, uT[:, h, 0:LAT], start=True, stop=True).then_inc(full_sem, 1)

            def act(self, act, B, ch):
                for h in range(4):
                    act.activation(uT[:, h, 0:LAT], m_y[:, 4 + h, 0:LAT], ACT.Square).then_inc(*S("squares").given())
                for h in range(4):
                    rstd_act(act, LAT)

            def dve(self, dve, B, ch):
                dve_link(ch, dve.tensor_scalar(small[:, 61:62], vc("subln"), 1.0 - LAM_INIT, None, ALU.mult))
                for h in range(4):
                    rstd_dve(dve, B, ch, h, LAT, P, RMS_EPS)
                    B.release(dve, h)
                    y = m_y[:, 4 + h, 0:LAT]
                    dve_link(ch, dve.scalar_tensor_tensor(out=y, in0=y, scalar=small[:, 61:62], in1=rstd[:, 0:LAT],
                                                          op0=ALU.mult, op1=ALU.mult))

        NE = 8
        lg = arena[:, 6144:6240].rearrange("p (t i e) -> p t i e", t=2, i=6)
        routing = sb("routing", [P, 7, NE])
        overflow = ctx.enter_context(nc.sbuf_tensor("overflow", [1, 1], mybir.dt.int32))

        class Router(Stage):
            products = 2 + 1

            def pe(self, pe, B):
                w = W.block(pe, [I["moe_router_2"][0]], KD)
                for t in range(2):
                    token_major(pe, B, t, w, 0, NE, uT, KD, t)
                W.used(full_sem, B.base + 2)
                pe.wait_ge(*S("picked").taken("pe"))
                bank = B.empty(pe, 2)
                pe.matmul(bank[:, 0:NE], tri[0], routing[:, 0, :], start=True, stop=True)
                for c, m in ((1, tri[0]), (2, one)):
                    pe.matmul(bank[:, c * NE:c * NE + NE], one, routing[:, 0, :], start=True, stop=False)
                    ins = pe.matmul(bank[:, c * NE:c * NE + NE], m, routing[:, 1, :], start=False, stop=True)
                ins.then_inc(full_sem, 1)

            def act(self, act, B, ch):
                for t in range(2):
                    act.wait_ge(*S("dti").taken("act"))
                    act.activation(lg[:, t, 2, :], lg[:, t, 0, :], ACT.Exp, bias=small[:, 62:63]).then_inc(*S("dtx").given())

            def dve(self, dve, B, ch):
                for t in range(2):
                    l, mx, e, gt, eq, run_ = (lg[:, t, i, :] for i in range(6))
                    bank = B.full(dve, t)
                    dve_link(ch, dve.tensor_copy(l, bank[:, 0:NE]))
                    B.release(dve, t)
                    dve_link(ch, dve.max(mx, l))
                    dve.tensor_scalar(small[:, 62:63], mx[:, 0:1], -1.0, None, ALU.mult).then_inc(*S("dti").given())
                    dve.tensor_scalar(gt, l, mx[:, 1:2], None, ALU.is_gt)
                    dve_link(ch, dve.tensor_scalar(eq, l, mx[:, 1:2], None, ALU.is_equal))
                    dve.tensor_tensor_scan(run_, one[:, 0:NE], eq, 0.0, ALU.mult, ALU.add)
                    dve_link(ch, dve.tensor_reduce(small[:, 63:64], gt, AX.X, ALU.add))
                    dve_link(ch, dve.tensor_scalar(run_, run_, small[:, 63:64], None, ALU.add))
                    dve_link(ch, dve.scalar_tensor_tensor(out=eq, in0=run_, scalar=2.0, in1=eq, op0=ALU.is_le, op1=ALU.mult))
                    dve.wait_ge(*S("dtx").taken("dve"))
                    dve_link(ch, dve.tensor_tensor(routing[:, t, :], gt, eq, ALU.add))
                    dve_link(ch, dve.tensor_tensor(l, routing[:, t, :], e, ALU.mult))
                    dve_link(ch, dve.tensor_reduce(small[:, 63:64], l, AX.X, ALU.add))
                    dve_link(ch, dve.reciprocal(small[:, 63:64], small[:, 63:64]))
                    dve_link(ch, dve.tensor_scalar(routing[:, 4 + t, :], l, small[:, 63:64], None, ALU.mult))
                S("picked").given()
                dve.drain().then_inc(S("picked").sem, 1)
                bank = B.full(dve, 2)
                place = routing[:, 2:4, :].rearrange("p t e -> p (t e)")
                dve_link(ch, dve.tensor_tensor(place, bank[:, 0:2 * NE], routing[:, 0:2, :].rearrange("p t e -> p (t e)"),
                                               ALU.mult))
                dve_link(ch, dve.tensor_scalar(place, place, -1.0, None, ALU.add))
                dve_link(ch, dve.tensor_reduce(small[0:1, 63:64], bank[0:1, 2 * NE:3 * NE], AX.X, ALU.max))
                B.release(dve, 2)
                dve_link(ch, dve.tensor_scalar(small[0:1, 62:63], small[0:1, 63:64], float(P), None, ALU.is_gt))
                dve.tensor_copy(overflow[:, :], small[0:1, 62:63]).then_inc(*S("overflow_known").given())

        NFE = I["moe_w1_2"].shape[3] // P
        m_xt = arena_at(0, 2, D)
        m_sel = arena_at(2048, 2, NE * P)
        m_selg = arena_at(4096, 2, NE * P)
        m_slot = arena_at(6144, NE, LAT)
        m_x = arena_at(8192, KD, NE * P)
        m_hid = [arena_at(16384 + i * NFE * P, NFE, P) for i in range(2)]
        m_yt = [arena_at(16384 + 2 * NFE * P + i * D, D) for i in range(2)]
        place = routing[:, 2:4, :]

        class Experts(Stage):
            XT, ST, GA = 0, 4, 8
            NH = (NFE + 1) // 2
            FIRST = 24
            products = 24 + NE * (NH + 4 + 4)

            def __init__(self, n):
                self.n = n

            def hidden(self, e):
                return self.FIRST + e * (self.NH + 8) - (4 if e else 0)

            def scatter(self, e):
                return self.hidden(e + 1) + self.NH if e < NE - 1 else self.products - 4

            def output(self, e):
                return self.hidden(e) + self.NH + (4 if e else 0)

            def tiles(self, i):
                return range(2 * i, min(2 * i + 2, NFE))

            def pe(self, pe, B):
                if self.n == 1:
                    W.second_pass = len(W.plan)
                for i in range(4):
                    t, c = i // 2, i % 2
                    bank = B.empty(pe, self.XT + i)
                    for j in range(4):
                        ins = pe.transpose(bank[:, j * P:j * P + P], uT[:, 4 * c + j, t * P:t * P + P], ident)
                    ins.then_inc(full_sem, 1)
                pe.wait_ge(*S("gate_cols").taken("pe"))
                for i in range(4):
                    bank = B.empty(pe, self.ST + i)
                    for j in range(2):
                        for t in range(2):
                            c = (2 * i + j) * P
                            ins = pe.transpose(bank[:, j * LAT + t * P:j * LAT + t * P + P], m_selg[:, t, c:c + P], ident)
                    ins.then_inc(full_sem, 1)
                for i in range(4):
                    B.freed(pe, self.XT + i)
                for i in range(16):
                    c, k = i // KD, i % KD
                    bank = B.empty(pe, self.GA + i)
                    for t in range(2):
                        ins = pe.matmul(bank[:, :], m_xt[:, t, k * P:k * P + P], m_sel[:, t, c * 512:c * 512 + 512],
                                        start=(t == 0), stop=(t == 1))
                    ins.then_inc(full_sem, 1)
                for e in range(NE):
                    if e in (0, 4):
                        for k in range(2, KD):
                            B.freed(pe, self.GA + 2 * e + k)
                    h0 = self.hidden(e)
                    for c in range(0, NFE, 4):
                        n = min(4, NFE - c)
                        w1, w3 = (W.block(pe, [I[nm][0, e][:, c * P:(c + n) * P]], KD) for nm in ("moe_w1_2", "moe_w3_2"))
                        for i in range(c // 2, (c + n + 1) // 2):
                            bank = B.empty(pe, h0 + i)
                            for f in self.tiles(i):
                                for half_, w in enumerate((w1, w3)):
                                    o = half_ * 256 + (f % 2) * P
                                    for k in range(KD):
                                        ins = pe.matmul(bank[:, o:o + P], w[:, k, (f - c) * P:(f - c) * P + P],
                                                        m_x[:, k, e * P:e * P + P], start=(k == 0), stop=(k == KD - 1))
                            ins.then_inc(full_sem, 1)
                        for _ in range(2):
                            W.used(full_sem, B.base + h0 + (c + n + 1) // 2)
                    if e:
                        self.scatter_pe(pe, B, e - 1)
                    for i in range(self.NH):
                        B.freed(pe, h0 + i)
                    hid = m_hid[e % 2]
                    for i in range(4):
                        w = W.block(pe, [I["moe_w2_2"][0, e][:, i * 256:i * 256 + 256]], NFE)
                        bank = B.empty(pe, self.output(e) + i)
                        for k in range(NFE):
                            ins = pe.matmul(bank[:, 0:256], hid[:, k, :], w[:, k, :], start=(k == 0), stop=(k == NFE - 1))
                        ins.then_inc(full_sem, 1)
                        W.used(full_sem, B.base + self.output(e) + i + 1)
                self.scatter_pe(pe, B, NE - 1)

            def scatter_pe(self, pe, B, e):
                for i in range(4):
                    B.freed(pe, self.output(e) + i)
                for i in range(4):
                    bank = B.empty(pe, self.scatter(e) + i)
                    for j in range(2):
                        f = 2 * i + j
                        ins = pe.matmul(bank[:, j * LAT:j * LAT + LAT], m_yt[e % 2][:, f * P:f * P + P], m_slot[:, e, :],
                                        start=True, stop=True)
                    ins.then_inc(full_sem, 1)

            def act(self, act, B, ch):
                for i in range(4):
                    t, c = i // 2, i % 2
                    bank = B.full(act, self.XT + i)
                    act.activation(m_xt[:, t, c * 512:c * 512 + 512], bank[:, :], ACT.Copy).then_inc(*B.free(self.XT + i))
                for i in range(0, 16, 2):
                    c, k = i // KD, i % KD
                    bank = B.full(act, self.GA + i)
                    act.activation(m_x[:, k, c * 512:c * 512 + 512], bank[:, :], ACT.Copy).then_inc(*B.free(self.GA + i))
                n = 0
                for e in range(NE):
                    for i in range(self.NH):
                        bank = B.full(act, self.hidden(e) + i)
                        w = P * len(self.tiles(i))
                        if n >= 2:
                            act.wait_ge(*S("moe_rl").taken("act"))
                        act.activation(rl[n % 2][:, 0:w], bank[:, 0:w], ACT.Silu).then_inc(*S("hid").given())
                        n += 1
                    if e >= 2:
                        B.full(act, self.scatter(e - 2) + 3)
                    for i in range(4):
                        bank = B.full(act, self.output(e) + i)
                        act.activation(m_yt[e % 2][:, i * 256:i * 256 + 256], bank[:, 0:256], ACT.Copy)\
                           .then_inc(*B.free(self.output(e) + i))
                act.wait_ge(*S("moe_rl").taken("act", 2))

            def dve(self, dve, B, ch):
                if self.n == 1:
                    dve_link(ch, dve.tensor_scalar(place, place, -float(P), None, ALU.add))
                iota = const[:, C_IOTA:C_IOTA + P]
                for t in range(2):
                    for e in range(NE):
                        v, g = place[:, t, e:e + 1], routing[:, 4 + t, e:e + 1]
                        dve.tensor_scalar(m_sel[:, t, e * P:e * P + P], iota, v, None, ALU.is_equal)
                        dve.tensor_scalar(m_selg[:, t, e * P:e * P + P], iota, v, g, ALU.is_equal, ALU.mult)
                S("gate_cols").given()
                dve.drain().then_inc(S("gate_cols").sem, 1)
                for i in range(4):
                    bank = B.full(dve, self.ST + i)
                    dve.tensor_copy(m_slot[:, 2 * i:2 * i + 2, :], bank[:, :].rearrange("p (e t) -> p e t", e=2))\
                       .then_inc(*B.free(self.ST + i))
                for i in range(1, 16, 2):
                    c, k = i // KD, i % KD
                    bank = B.full(dve, self.GA + i)
                    dve.tensor_copy(m_x[:, k, c * 512:c * 512 + 512], bank[:, :]).then_inc(*B.free(self.GA + i))
                n = 0
                for e in range(NE + 1):
                    for i in range(self.NH if e < NE else 0):
                        w = P * len(self.tiles(i))
                        f = 2 * i
                        if i == 0 and e >= 2:
                            B.full(dve, self.output(e - 2) + 3)
                        dve.wait_ge(*S("hid").taken("dve"))
                        bank = B[self.hidden(e) + i]
                        dst = m_hid[e % 2][:, f:f + w // P, :].rearrange("p f t -> p (f t)")
                        dve.tensor_tensor(dst, bank[:, 256:256 + w], rl[n % 2][:, 0:w], ALU.mult)\
                           .then_inc(*S("moe_rl").given())
                        B.release(dve, self.hidden(e) + i)
                        n += 1
                    if e:
                        dve_link(ch, dve.drain())
                        for i in range(4):
                            bank = B.full(dve, self.scatter(e - 1) + i)
                            for j in range(2):
                                f = 2 * i + j
                                ins = dve.scalar_tensor_tensor(out=hT[:, f, 0:LAT], in0=bank[:, j * LAT:j * LAT + LAT],
                                                               scalar=mods[3][:, 40 + f, 0:1], in1=hT[:, f, 0:LAT],
                                                               op0=ALU.mult, op1=ALU.add)
                            ins.then_inc(*B.free(self.scatter(e - 1) + i))

        class Store(Stage):
            products = 4
            orow = arena_at(0, 2, D)

            def pe(self, pe, B):
                for i in range(4):
                    t, c = i // 2, i % 2
                    bank = B.empty(pe, i)
                    for j in range(4):
                        ins = pe.transpose(bank[:, j * P:j * P + P], hT[:, 4 * c + j, t * P:t * P + P], ident)
                    ins.then_inc(B.full_sem, 1)

            def dve(self, dve, B, ch):
                for i in range(4):
                    bank = B.full(dve, i)
                    dve.tensor_copy(self.orow[:, i // 2, 512 * (i % 2):512 * (i % 2) + 512], bank[:, :]).then_inc(*B.free(i))

            def act(self, act, B, ch):
                for t in range(2):
                    for c in range(2):
                        B.freed(act, 2 * t + c)
                    act.dma_start(out[0, t * P:t * P + P, :], self.orow[:, t, :]).then_inc(S("stored").sem, 16)
                act.wait_ge(S("stored").sem, 32)

        M = mods
        y8 = g_o
        stages = [Setup()] + [Ada(b, l) for b in range(2) for l in range(2)]
        stages += [Modulate(M[0], 0, True, True), GlaProject(), GlaScan(), GlaGate(),
                   Residual(I["gla_w_out"][0], y8, KD, M[0], 2, TOK, True), LayerNorm(0, 0, TOK),
                   Modulate(M[0], 3, True, False)]
        hid = HiddenRelu2(I["ffn_w1"][0], TOK)
        stages += [hid, Residual(I["ffn_w2"][0], hid.hid, 32, M[0], 5, TOK, False), LayerNorm(0, 1, TOK)]
        mark = {"b1l0": len(stages)}
        stages += [Modulate(M[1], 0, True, True), SsdGates()] + [SsdGroups()]
        stages += [SsdGate(), Residual(I["ssd_w_out"][0], s_y, 16, M[1], 2, LAT, True), LayerNorm(1, 0, LAT)]
        mark["b1l1m"] = len(stages)
        stages += [Modulate(M[1], 3, False, False)]
        hid = HiddenRelu2(I["ffn_w1"][1], LAT)
        stages += [hid, Residual(I["ffn_w2"][1], hid.hid, 32, M[1], 5, LAT, False), LayerNorm(1, 1, LAT)]
        mark["b1"] = len(stages)
        stages += [LoadCtx(), RmsNorm(M[2], 0, TOK), EvenProject(), BiasLoad(),
                   HeadNorm([(m_q[:, i, :], "ev_q_g_2", TOK) for i in range(4)]
                            + [(m_k[:, i, :], "ev_k_g_2", TOK) for i in range(4)], False),
                   Attention(even_items()), Residual(I["ev_w_out_2"][0], m_y, KD, M[2], 2, TOK, False)]
        mark["b2l0m"] = len(stages)
        stages += [RmsNorm(M[2], 3, TOK)]
        hid = HiddenSwiglu(I["ffn_w1_2"][0], I["ffn_w3_2"][0], TOK)
        stages += [hid, Residual(I["ffn_w2_2"][0], hid.hid, 22, M[2], 5, TOK, False)]
        mark["b2l0"] = len(stages)
        stages += [RmsNorm(M[3], 0, TOK), OddProject(),
                   HeadNorm([(m_q[:, i, 0:LAT], "od_cq_g_2" if i < 4 else "od_dq_g_2", LAT) for i in range(8)]
                            + [(m_k[:, 0, :], "od_ck_g_2", TOK)]
                            + [(m_k[:, 2 + i, :], "od_dk_g_2", TOK) for i in range(4)], True),
                   KeysAndLambda(), Attention(window_items()), Attention(diff_items(), lam_t), SubNorm(),
                   Residual(I["od_w_out_2"][0], m_y, KD, M[3], 2, LAT, False)]
        mark["b2l1m"] = len(stages)
        stages += [RmsNorm(M[3], 3, LAT), Router()]
        loop_at = len(stages) + 1
        stages += [Experts(0), Experts(1)]
        if stop is not None:
            stages, loop_at = stages[:mark[stop]], None
        STAGE_NAMES[:] = [type(s).__name__ for s in stages] + ["Store"]
        stored_full, stored_free = sem("store_products"), [sem(f"store_bank_free{i}") for i in range(NBANK)]
        experts_done = {e: sem(f"experts_done_{e}") for e in ENG}
        block = ctx.enter_context(nc.Block())

        def part(name, st, eng, B, ch):
            if name == "pe":
                st.pe(eng, B)
            elif name == "act":
                st.act(eng, B, ch)
            else:
                st.dve(eng, B, ch)

        def run(name, eng, ch):
            B = Banks(banks_t, full_sem, free_sem)

            def stage(n, st):
                if n:
                    for other in ENG:
                        if other != name:
                            eng.wait_ge(stage_done[other], n)
                part(name, st, eng, B, ch)
                eng.drain().then_inc(stage_done[name], 1)
                B.base += st.products
            for n, st in enumerate(stages):
                if n == loop_at:
                    again = eng.value_load(overflow[0:1, 0:1], min_val=0, max_val=1)
                    with eng.If(again > 0):
                        stage(n, st)
                else:
                    stage(n, st)
            eng.drain().then_inc(experts_done[name], 1)
            for other in ENG:
                if other != name:
                    eng.wait_ge(experts_done[other], 1)
            part(name, Store(), eng, Banks(banks_t, stored_full, stored_free), None)

        @block.tensor
        def _(pe):
            run("pe", pe, None)

        @block.scalar
        def _(act):
            run("act", act, Chain(act, chain_sem["act"]))

        @block.vector
        def _(dve):
            run("dve", dve, Chain(dve, chain_sem["dve"]))

        @block.sync
        def _(sync):
            def stream(blocks):
                for n in blocks:
                    pieces, kt = W.plan[n]
                    if n >= SLOTS:
                        sync.wait_ge(*W.done[n - SLOTS])
                    v = W.view(n)
                    at = 0
                    for piece in pieces:
                        c = piece.shape[1]
                        sync.dma_start(v[:, :, at:at + c], piece.rearrange("(k p) c -> p k c", p=P))\
                            .then_inc(W.landed[n % SLOTS], 16)
                        at += c
            stream(range(W.second_pass or len(W.plan)))
            if loop_at is not None:
                sync.wait_ge(*S("overflow_known").taken("sync"))
                again = sync.value_load(overflow[0:1, 0:1], min_val=0, max_val=1)
                with sync.If(again > 0):
                    stream(range(W.second_pass, len(W.plan)))


_OUTS = [((1, 256, 1024), "float32")]
_STOP = None


def kernel(**inputs):
    import concourse.bacc as _bacc
    from concourse.bass_utils import run_bass_kernel_spmd as _run

    nc = _bacc.Bacc("TRN2", target_bir_lowering=False, num_devices=1)
    arrays, aps = {}, {}
    for name, a in list(inputs.items()) + [("const", constants())]:
        a = np.ascontiguousarray(a)
        if a.size == 0 or name.startswith("hy_"):
            continue
        arrays[f"in_{name}"] = a
        aps[name] = nc.dram_tensor(f"in_{name}", a.shape, mybir.dt.from_np(a.dtype), kind="ExternalInput").ap()
    o = nc.dram_tensor("out_0", _OUTS[0][0], F32, kind="ExternalOutput").ap()
    build(nc, aps, o, _STOP)
    r = _run(nc, [arrays], core_ids=[0])
    return r.results[0]["out_0"]
```

```python
from contextlib import ExitStack
import math

import numpy as np

import concourse.bass as bass
from concourse import mybir

F32 = mybir.dt.float32
ALU = mybir.AluOpType
ACT = mybir.ActivationFunctionType
AX = mybir.AxisListType

P = 128
D = 1024
KD = D // P
LAT = 256
CTX = 256
TOK = LAT + CTX
ROWS, GRID = 4, 64
ALPHA = 4 ** 0.25
LN_EPS, RMS_EPS = 1e-5, 1e-6
NBANK = 6
SLOTS = 4
SLOT = 4096
NEG = -1e30
ARENA = 22528

C_ID, C_TRIF, C_TRIB, C_ONE, C_HALF, C_ROT, C_DUP = 0, 128, 256, 384, 512, 640, 768
C_COL, C_SWA, C_COS, C_SIN, C_FLIP, C_IOTA, C_END = 1024, 1088, 1600, 1856, 2112, 2240, 2368


def constants():
    c = np.zeros((P, C_END), np.float32)
    i = np.arange(P)
    c[:, C_ID:C_ID + P] = np.eye(P)
    c[:, C_TRIF:C_TRIF + P] = i[:, None] <= i[None, :]
    c[:, C_TRIB:C_TRIB + P] = i[:, None] >= i[None, :]
    c[:, C_ONE:C_ONE + P] = 1.0
    c[:, C_HALF:C_HALF + P] = (i[:, None] // 64) == (i[None, :] // 64)
    for f in range(P):
        if (f % 32) < 16:
            c[f + 16, C_ROT + f] = -1.0
        else:
            c[f - 16, C_ROT + f] = 1.0
    for g in range(2):
        for f in range(P):
            c[64 * g + f % 64, C_DUP + 128 * g + f] = 1.0
    c[i, C_FLIP + 64 * (i // 64) + 63 - i % 64] = 1.0
    c[:, C_IOTA:C_IOTA + P] = i[None, :]
    col = np.arange(GRID)
    c0 = np.clip(col - 8, 0, GRID - 16)
    ok = (col[None, :] >= c0[:, None]) & (col[None, :] < c0[:, None] + 16)
    c[:, C_COL:C_COL + GRID] = np.where(np.tile(ok, (2, 1)), 0.0, NEG)
    k = np.arange(LAT)
    for t in range(2):
        q = t * P + i
        c[:, C_SWA + t * LAT:C_SWA + (t + 1) * LAT] = np.where(np.abs(k[None, :] - q[:, None]) <= 128, 0.0, NEG)
    inv = np.float32(10000.0) ** (-np.arange(16, dtype=np.float32) / np.float32(16))
    pos = np.stack([k // GRID, k % GRID]).astype(np.float32)
    f = i % 64
    ang = pos[f // 32] * inv[f % 16][:, None].astype(np.float32)
    c[:, C_COS:C_COS + LAT] = np.cos(ang)
    c[:, C_SIN:C_SIN + LAT] = np.sin(ang)
    return c


class Signal:

    def __init__(self, sem):
        self.sem, self.made, self.seen = sem, 0, {}

    def given(self):
        self.made += 1
        return self.sem, 1

    def taken(self, who, n=1):
        self.seen[who] = self.seen.get(who, 0) + n
        return self.sem, self.seen[who]


class Chain:

    def __init__(self, eng, sem):
        self.eng, self.sem, self.n = eng, sem, 0

    def __call__(self, ins):
        ins.then_inc(self.sem, 1)
        self.n += 1
        return self.n

    def wait(self, n=None):
        self.eng.wait_ge(self.sem, self.n if n is None else n)


class Banks:

    def __init__(self, banks, full, free):
        self.banks, self.full_sem, self.free_sem, self.base = banks, full, free, 0

    def __getitem__(self, i):
        return self.banks[(self.base + i) % NBANK]

    def empty(self, pe, i):
        g = self.base + i
        if g >= NBANK:
            pe.wait_ge(self.free_sem[g % NBANK], g // NBANK)
        return self.banks[g % NBANK]

    def full(self, eng, i):
        eng.wait_ge(self.full_sem, self.base + i + 1)
        return self.banks[(self.base + i) % NBANK]

    def freed(self, eng, i):
        g = self.base + i
        eng.wait_ge(self.free_sem[g % NBANK], g // NBANK + 1)

    def release(self, eng, i):
        eng.drain().then_inc(*self.free(i))

    def free(self, i):
        return self.free_sem[(self.base + i) % NBANK], 1


class Weights:

    def __init__(self, slots, landed):
        self.slots, self.landed, self.plan, self.done = slots, landed, [], []
        self.dmas = [0] * SLOTS
        self.loads = []
        self.second_pass = None

    def block(self, pe, pieces, kt):
        n = len(self.plan)
        self.plan.append((pieces, kt))
        self.dmas[n % SLOTS] += len(pieces)
        pe.wait_ge(self.landed[n % SLOTS], 16 * self.dmas[n % SLOTS])
        return self.view(n)

    def view(self, n):
        pieces, kt = self.plan[n]
        cols = sum(p.shape[1] for p in pieces)
        return self.slots[n % SLOTS][:, 0:kt * cols].rearrange("p (k c) -> p k c", k=kt)

    def used(self, sem, count):
        self.done.append((sem, count))


def build(nc, I, out, stop=None):
    ctx = ExitStack()
    with ctx:
        def sb(name, shape):
            return ctx.enter_context(nc.sbuf_tensor(name, shape, F32))

        def sem(name):
            return ctx.enter_context(nc.semaphore(name))

        const = sb("const", [P, C_END])
        hT = sb("hT", [P, KD, TOK])
        uT = sb("uT", [P, KD, TOK])
        slots = [sb(f"slot{i}", [P, SLOT]) for i in range(SLOTS)]
        arena = sb("arena", [P, ARENA])
        mods = [sb(f"mod{i}", [P, 48, 2]) for i in range(4)]
        sT = sb("sT", [P, 2, KD, 2])
        rstds = [sb(f"rstd{i}", [P, TOK]) for i in range(2)]
        eps_cols = sb("eps", [P, 2])
        eps_col = {LN_EPS / ALPHA ** 2: eps_cols[:, 0:1], RMS_EPS: eps_cols[:, 1:2]}
        small = sb("small", [P, 64])
        banks_t = [ctx.enter_context(nc.psum_tensor(f"bank{i}", [P, 512], F32)) for i in range(8)]

        ident = const[:, C_ID:C_ID + P]
        tri = [const[:, C_TRIF:C_TRIF + P], const[:, C_TRIB:C_TRIB + P]]
        one = const[:, C_ONE:C_ONE + P]
        half = const[:, C_HALF:C_HALF + P]
        rot = const[:, C_ROT:C_ROT + P]

        full_sem = sem("products")
        free_sem = [sem(f"bank_free{i}") for i in range(NBANK)]
        W = Weights(slots, [sem(f"weights_landed{i}") for i in range(SLOTS)])
        signals = {}

        def S(name):
            if name not in signals:
                signals[name] = Signal(sem(name))
            return signals[name]

        ENG = ("pe", "act", "dve")
        stage_done = {e: sem(f"stage_done_{e}") for e in ENG}
        for n in ("loads", "setup_rows", "centred", "squares", "rstd_used", "root", "normed", "a_rows",
                  "sg_exp", "gla_d", "gla_e", "gla_q", "gla_sm", "gla_sp", "gla_el", "conv", "feat", "dab",
                  "seg", "segx", "xw", "st", "lw", "lwx", "ecx", "nm", "pr", "pn", "hid", "stored", "dti",
                  "dtx", "free_a", "bias_loads", "rope_in", "convd", "ada_rows", "ada_cols", "ada_copied",
                  "ada_free", "moe_loads", "da_done", "ready", "lam", "picked", "gate_cols", "overflow_known",
                  "moe_rl", "guest_rows", "guest_copied", "guest_cols", "guest_read"):
            S(n)
        chain_sem = {e: sem(f"steps_{e}") for e in ENG}

        rows, col = [], {}

        def rowvec(name, ap, n):
            col[name] = sum(r[1] for r in rows)
            rows.append((ap, n))

        def flat(ap):
            k = len(ap.shape)
            names = " ".join(f"a{i}" for i in range(k))
            return ap.rearrange(f"{names} -> ({names})") if k > 1 else ap

        def r128(ap):
            return flat(ap).rearrange("(r p) -> r p", p=P)
        for b, s in enumerate(("", "_2")):
            rowvec(f"c{b}", r128(I["c" + s]), KD)
            rowvec(f"cc{b}", r128(I["c_ctx" + s]), KD)
            rowvec(f"ada_b{b}", r128(I["ada_b" + s]), 96)
        rowvec("ln_g", r128(I["ln_g"]), 32)
        rowvec("ln_b", r128(I["ln_b"]), 32)
        rowvec("gla_norm", r128(I["gla_norm"]), 2)
        rowvec("conv_w", r128(I["ssd_conv_w"]), 160)
        rowvec("conv_b", r128(I["ssd_conv_b"]), 32)
        rowvec("ssd_norm", r128(I["ssd_norm"]), 16)
        rowvec("norm1", r128(I["norm1_g_2"]), 16)
        rowvec("norm2", r128(I["norm2_g_2"]), 16)
        rowvec("ev_conv", r128(I["ev_conv_w_2"]), 12)
        rowvec("subln", r128(I["od_subln_g_2"]), 1)
        for nm in ("ev_q_g_2", "ev_k_g_2", "od_cq_g_2", "od_ck_g_2", "od_dq_g_2", "od_dk_g_2"):
            rowvec(nm, ("twice", I[nm]), 1)
        NR = sum(r[1] for r in rows)
        NT = -(-NR // P)
        VT = sb("vectors", [P, NR])

        def vc(name, i=0):
            return VT[:, col[name] + i:col[name] + i + 1]

        def arena_at(off, *dims):
            n = int(np.prod(dims))
            assert off + n <= ARENA, (off, dims)
            v = arena[:, off:off + n]
            if len(dims) == 2:
                v = v.rearrange("p (a b) -> p a b", a=dims[0])
            if len(dims) == 3:
                v = v.rearrange("p (a b c) -> p a b c", a=dims[0], b=dims[1])
            return v

        def bc(ap, n):
            return ap.unsqueeze(2).broadcast_to([ap.shape[0], ap.shape[1], n])

        def bcm(ap, n):
            return ap.unsqueeze(1).broadcast_to([ap.shape[0], n, ap.shape[1]])

        SEQ = {"lat": (0, LAT), "ctx": (LAT, TOK)}

        class Stage:
            products = 0
            guest = None

            def pe(self, pe, B):
                pass

            def act(self, act, B, ch):
                pass

            def dve(self, dve, B, ch):
                pass

        def dve_link(ch, ins):
            n = ch(ins)
            ch.wait(n)

        raw_rows = arena_at(0, NT, P)
        xrow = arena_at(NT * P, 4, D)
        dvec = sb("ssd_d_rows", [P, 32])
        dcol = sb("ssd_d", [P, 16])
        dtb = sb("dt_bias", [P, 64])
        alog = sb("a_log", [P, 64])
        halves = sb("halves", [P, 2, TOK])
        wa2 = halves
        rl = [halves[:, 0, :], halves[:, 1, :]]
        lamv = sb("lam_v", [P, 4])

        class Setup(Stage):
            products = NT + KD

            def act(self, act, B, ch):
                loads = S("loads")
                n = [0]

                def load(dst, src):
                    act.dma_start(dst, src).then_inc(loads.sem, 16)
                    n[0] += 16
                load(const[:, :], I["const"])
                at = 0
                for ap, k in rows:
                    if isinstance(ap, tuple):
                        for h in range(2):
                            load(raw_rows[at % P:at % P + 1, at // P, 64 * h:64 * h + 64],
                                 ap[1])
                        at += 1
                        continue
                    done = 0
                    while done < k:
                        m = min(k - done, P - at % P)
                        load(raw_rows[at % P:at % P + m, at // P, :], ap[done:done + m, :])
                        at += m
                        done += m
                for i, nm in enumerate(("x", "ctx")):
                    load(xrow[:, 2 * i:2 * i + 2, :], I[nm].rearrange("o (t p) d -> p (o t) d", p=P))
                load(dvec[:, :], flat(I["ssd_d"]).partition_broadcast(P))
                load(dtb[:, :], flat(I["ssd_dt_bias"]).partition_broadcast(P))
                load(alog[:, :], flat(I["ssd_a_log"]).partition_broadcast(P))
                for z in range(2):
                    load(wa2[0:16, z, :], I["gla_w_a2"][0, z])
                    load(wa2[16:17, z, :], I["gla_b_a2"][0:1, z])
                for j, nm in enumerate(("od_lam_q1_2", "od_lam_k1_2", "od_lam_q2_2", "od_lam_k2_2")):
                    load(lamv[0:64, j:j + 1], I[nm].rearrange("o p -> p o"))
                self.total = n[0]
                act.wait_ge(loads.sem, self.total)
                S("ready").given()
                act.drain().then_inc(S("ready").sem, 1)
                act.wait_ge(*S("setup_rows").taken("act"))
                for b in range(2):
                    for s, nm in enumerate(("c", "cc")):
                        c0 = col[f"{nm}{b}"]
                        ins = act.activation(sT[:, b, :, s], VT[:, c0:c0 + KD], ACT.Silu)
                ch(ins)

            def pe(self, pe, B):
                pe.wait_ge(*S("ready").taken("pe"))
                for t in range(NT):
                    r = min(P, NR - t * P)
                    bank = B.empty(pe, t)
                    pe.transpose(bank[:, 0:r], raw_rows[0:r, t, :], ident[0:r, 0:r]).then_inc(full_sem, 1)
                for k in range(KD):
                    bank = B.empty(pe, NT + k)
                    for t in range(4):
                        ins = pe.transpose(bank[:, t * P:t * P + P], xrow[:, t, k * P:k * P + P], ident)
                    ins.then_inc(full_sem, 1)

            def dve(self, dve, B, ch):
                for eps, c in eps_col.items():
                    dve.memset(c, eps)
                for t in range(NT):
                    r = min(P, NR - t * P)
                    bank = B.full(dve, t)
                    dve.tensor_copy(VT[:, t * P:t * P + r], bank[:, 0:r]).then_inc(*B.free(t))
                dve.wait_ge(*S("ready").taken("dve"))
                S("setup_rows").given()
                dve.drain().then_inc(S("setup_rows").sem, 1)
                for k in range(KD):
                    bank = B.full(dve, NT + k)
                    dve.tensor_copy(hT[:, k, :], bank[:, :]).then_inc(*B.free(NT + k))
                d2 = dvec[:, :].rearrange("p (t a) -> p t a", a=2)
                dve.tensor_copy(dcol[0:64, :], d2[0:64, :, 0])
                dve_link(ch, dve.tensor_copy(dcol[64:P, :], d2[64:P, :, 1]))

        ada_rows_bank, ada_cols_bank = banks_t[NBANK], banks_t[NBANK + 1]
        ada_row = rstds[1][0:2, :]

        class Ada(Stage):

            def __init__(self, blk, layer):
                self.blk, self.layer = blk, layer
                self.w = I["ada_w" + ("_2" if blk else "")][layer]
                self.m = mods[2 * blk + layer]

            def pe(self, pe, B):
                rows, cols = S("ada_rows"), S("ada_cols")
                if cols.made:
                    pe.wait_ge(*S("ada_free").taken("pe"))
                for c in range(13):
                    if c < 12:
                        w = W.block(pe, [self.w[:, c * 512:c * 512 + 512]], KD)
                        if c:
                            pe.wait_ge(*S("ada_copied").taken("pe"))
                        for k in range(KD):
                            ins = pe.matmul(ada_rows_bank[0:2, :], sT[:, self.blk, k, :], w[:, k, :], start=(k == 0),
                                            stop=(k == KD - 1))
                        ins.then_inc(*rows.given())
                        W.used(rows.sem, rows.made)
                    if c == 12:
                        pe.wait_ge(*S("ada_copied").taken("pe", 1))
                    if c:
                        for j in range(4):
                            o = 8 * (c - 1) + 2 * j
                            ins = pe.transpose(ada_cols_bank[:, o:o + 2], ada_row[0:2, j * P:j * P + P], ident[0:2, 0:2])
                        ins.then_inc(*cols.given())

            def act(self, act, B, ch):
                for c in range(12):
                    act.wait_ge(*S("ada_rows").taken("act"))
                    if c:
                        act.wait_ge(*S("ada_cols").taken("act"))
                    act.activation(ada_row[0:2, :], ada_rows_bank[0:2, :], ACT.Copy).then_inc(*S("ada_copied").given())
                act.wait_ge(*S("ada_cols").taken("act"))

            def dve(self, dve, B, ch):
                dve.wait_ge(*S("ada_cols").taken("dve", 12))
                ada_finish(dve, ch, self.blk, self.layer, S("ada_free"))

        def ada_finish(dve, ch, blk, layer, read):
            m = mods[2 * blk + layer]
            b0 = col[f"ada_b{blk}"] + 48 * layer
            dve.tensor_tensor(m[:, :, :], ada_cols_bank[:, 0:96].rearrange("p (a b) -> p a b", b=2),
                              bc(VT[:, b0:b0 + 48], 2), ALU.add).then_inc(*read.given())
            dve.wait_ge(read.sem, read.made)
            for q in (1, 4):
                dve_link(ch, dve.tensor_scalar(m[:, 8 * q:8 * q + 8, :], m[:, 8 * q:8 * q + 8, :], 1.0, None, ALU.add))
                if blk:
                    g0 = col["norm1" if q == 1 else "norm2"] + 8 * layer
                    dve_link(ch, dve.tensor_tensor(m[:, 8 * q:8 * q + 8, :], m[:, 8 * q:8 * q + 8, :],
                                                   bc(VT[:, g0:g0 + 8], 2), ALU.mult))
            if not blk:
                for q in (2, 5):
                    dve_link(ch, dve.tensor_scalar(m[:, 8 * q:8 * q + 8, :], m[:, 8 * q:8 * q + 8, :], 1.0 / ALPHA,
                                                   None, ALU.mult))

        GUEST = 256
        GUESTS = 6 * D // GUEST
        guests = []
        guest_w = [arena_at(16384 + i * KD * GUEST, KD, GUEST) for i in range(2)]
        guest_acc = [arena_at(16384 + 2 * KD * GUEST + i * 2 * GUEST, 2, GUEST) for i in range(2)]
        guest_landed = [sem(f"guest_landed{i}") for i in range(2)]
        guest_summed = sem("guest_summed")

        class AdaGuest:

            def __init__(self, blk, layer):
                self.blk, self.layer = blk, layer
                self.w = I["ada_w" + ("_2" if blk else "")][layer]
                self.first = len(guests) * GUESTS
                self.stage = None
                self.host_blocks, self.nth = None, 0
                self.at = {2 + (19 * n) // 16: n for n in range(GUESTS)}
                guests.append(self)

            def pe(self, pe, place):
                n = self.at.get(place, GUESTS if place == 31 else None)
                if n is None:
                    return
                cols = S("guest_cols")
                if n:
                    pe.wait_ge(*S("guest_copied").taken("pe"))
                    for j in range(4):
                        o = 2 * (2 * (n - 1) + j % 2) + j // 2
                        ins = pe.transpose(ada_cols_bank[:, o:o + 1], ada_row[0:1, j * P:j * P + P], ident[0:1, 0:1])
                if n == GUESTS:
                    ins.then_inc(*cols.given())
                    return
                if self.host_blocks != len(W.plan):
                    self.host_blocks, self.nth = len(W.plan), 0
                W.loads.append((len(W.plan) + (0 if self.nth < 2 else 1), self, n))
                self.nth += 1
                pe.wait_ge(guest_summed, 2 * (self.first + n + 1))
                pe.matmul(ada_rows_bank[0:1, :], one[:, 0:1], guest_acc[n % 2].rearrange("p s c -> p (s c)"), start=True,
                          stop=True).then_inc(*S("guest_rows").given())

            def act(self, act, place):
                if place in self.at:
                    act.wait_ge(*S("guest_rows").taken("act"))
                    act.activation(ada_row[0:1, :], ada_rows_bank[0:1, :], ACT.Copy).then_inc(*S("guest_copied").given())

            def dve(self, dve, ch):
                dve.wait_ge(*S("guest_cols").taken("dve"))
                ada_finish(dve, ch, self.blk, self.layer, S("guest_read"))

            def load(self, sync, n):
                g = self.first + n
                if n < 2:
                    for e in ENG:
                        sync.wait_ge(stage_done[e], self.stage)
                if g >= 2:
                    sync.wait_ge(guest_summed, 2 * (g - 1))
                sync.dma_start(guest_w[n % 2], self.w[:, n * GUEST:n * GUEST + GUEST].rearrange("(k p) c -> p k c", p=P))\
                    .then_inc(guest_landed[n % 2], 16)

            def sums(self, dve, ch, places):
                for n in (self.at[p + 2] for p in places if p + 2 in self.at):
                    g = self.first + n
                    dve.wait_ge(guest_landed[n % 2], 16 * (g // 2 + 1))
                    if n >= 2:
                        dve.wait_ge(S("guest_rows").sem, g - 1)
                    w, acc, last = guest_w[n % 2], guest_acc[n % 2], [None, None]
                    for k in range(KD):
                        for s in range(2):
                            c = sT[:, self.blk, k, s:s + 1]
                            if k:
                                ch.wait(last[s])
                                ins = dve.scalar_tensor_tensor(out=acc[:, s, :], in0=w[:, k, :], scalar=c, in1=acc[:, s, :],
                                                               op0=ALU.mult, op1=ALU.add)
                            else:
                                ins = dve.tensor_scalar(acc[:, s, :], w[:, 0, :], c, None, ALU.mult)
                            if k == KD - 1:
                                ins.then_inc(guest_summed, 1)
                            else:
                                last[s] = ch(ins)

        def snaked(ap, rev):
            g = ap.rearrange("p (r two c) -> p r two c", two=2, c=GRID)
            return g[:, :, 0, :], (g[:, :, 1, ::-1] if rev else g[:, :, 1, :])

        class Modulate(Stage):
            def __init__(self, m, q, has_ctx, snake):
                self.m, self.q, self.has_ctx, self.snake = m, q, has_ctx, snake

            def act(self, act, B, ch):
                m, q = self.m, self.q
                for k in range(KD):
                    kw = dict(scale=m[:, 8 * (q + 1) + k, 0:1], bias=m[:, 8 * q + k, 0:1])
                    if self.snake:
                        for o, i in zip(snaked(uT[:, k, 0:LAT], False), snaked(hT[:, k, 0:LAT], True)):
                            act.activation(o, i, ACT.Identity, **kw)
                    else:
                        act.activation(uT[:, k, 0:LAT], hT[:, k, 0:LAT], ACT.Identity, **kw)

            def dve(self, dve, B, ch):
                m, q = self.m, self.q
                for k in range(KD if self.has_ctx else 0):
                    dve.tensor_scalar(uT[:, k, LAT:TOK], hT[:, k, LAT:TOK], m[:, 8 * (q + 1) + k, 1:2],
                                      m[:, 8 * q + k, 1:2], ALU.mult, ALU.add)

        def rstd_act(act, B, ch, n, i, T, dim, eps):
            r = rstds[n % 2][:, 0:T]
            bank = B.full(act, i)
            if n >= 2:
                act.wait_ge(*S("rstd_used").taken("act"))
            ch.wait(ch(act.activation(r, bank[:, 0:T], ACT.Ln, scale=1.0 / dim, bias=eps_col[eps])))
            act.activation(r, r, ACT.Exp, scale=-0.5).then_inc(*S("root").given())

        def rstd_wait(dve, n, T):
            dve.wait_ge(*S("root").taken("dve"))
            return rstds[n % 2][:, 0:T]

        def rstd_drop(act, N):
            act.wait_ge(*S("rstd_used").taken("act", min(N, 2)))

        class LayerNorm(Stage):
            products = 2

            def __init__(self, i, j, T):
                self.g, self.T = 16 * i + 8 * j, T
                self.sq = arena_at(0, KD, TOK)

            def pe(self, pe, B):
                T = self.T
                bank = B.empty(pe, 0)
                for k in range(KD):
                    ins = pe.matmul(bank[:, 0:T], one, hT[:, k, 0:T], start=(k == 0), stop=(k == KD - 1))
                ins.then_inc(full_sem, 1)
                bank = B.empty(pe, 1)
                for k in range(KD):
                    pe.wait_ge(*S("squares").taken("pe"))
                    ins = pe.matmul(bank[:, 0:T], one, self.sq[:, k, 0:T], start=(k == 0), stop=(k == KD - 1))
                ins.then_inc(full_sem, 1)

            def dve(self, dve, B, ch):
                T = self.T
                bank = B.full(dve, 0)
                for k in range(KD):
                    dve.scalar_tensor_tensor(out=hT[:, k, 0:T], in0=bank[:, 0:T], scalar=-1.0 / D, in1=hT[:, k, 0:T],
                                             op0=ALU.mult, op1=ALU.add).then_inc(*S("centred").given())
                dve_link(ch, dve.drain())
                B.release(dve, 0)
                r = rstd_wait(dve, 0, T)
                B.release(dve, 1)
                for k in range(KD):
                    dve.tensor_tensor(hT[:, k, 0:T], hT[:, k, 0:T], r, ALU.mult).then_inc(*S("normed").given())

            def act(self, act, B, ch):
                T = self.T
                for k in range(KD):
                    act.wait_ge(*S("centred").taken("act"))
                    act.activation(self.sq[:, k, 0:T], hT[:, k, 0:T], ACT.Square).then_inc(*S("squares").given())
                rstd_act(act, B, ch, 0, 1, T, D, LN_EPS / ALPHA ** 2)
                for k in range(KD):
                    act.wait_ge(*S("normed").taken("act"))
                    act.activation(hT[:, k, 0:T], hT[:, k, 0:T], ACT.Identity, scale=vc("ln_g", self.g + k),
                                   bias=vc("ln_b", self.g + k))

        class RmsNorm(Stage):
            products = 1

            def __init__(self, m, q, T):
                self.m, self.q, self.T = m, q, T
                self.sq = arena_at(0, KD, TOK)

            def pe(self, pe, B):
                T = self.T
                bank = B.empty(pe, 0)
                for k in range(KD):
                    pe.wait_ge(*S("squares").taken("pe"))
                    ins = pe.matmul(bank[:, 0:T], one, self.sq[:, k, 0:T], start=(k == 0), stop=(k == KD - 1))
                ins.then_inc(full_sem, 1)

            def dve(self, dve, B, ch):
                T = self.T
                r = rstd_wait(dve, 0, T)
                B.release(dve, 0)
                for k in range(KD):
                    dve.tensor_tensor(uT[:, k, 0:T], hT[:, k, 0:T], r, ALU.mult).then_inc(*S("normed").given())

            def act(self, act, B, ch):
                T, m, q = self.T, self.m, self.q
                for k in range(KD):
                    act.activation(self.sq[:, k, 0:T], hT[:, k, 0:T], ACT.Square).then_inc(*S("squares").given())
                rstd_act(act, B, ch, 0, 0, T, D, RMS_EPS)
                for k in range(KD):
                    act.wait_ge(*S("normed").taken("act"))
                    for s in range(T // LAT):
                        v = uT[:, k, s * LAT:s * LAT + LAT]
                        act.activation(v, v, ACT.Identity, scale=m[:, 8 * (q + 1) + k, s:s + 1],
                                       bias=m[:, 8 * q + k, s:s + 1])

        def feature_major(pe, B, i, w, c0, x, kt, t0, t1, m=P, after=None):
            bank = B.empty(pe, i)
            for k in range(kt):
                ins = pe.matmul(bank[0:m, 0:t1 - t0], w[:, k, c0:c0 + m], x[:, k, t0:t1], start=(k == 0),
                                stop=(k == kt - 1))
                if k == kt - 1:
                    ins.then_inc(full_sem, 1)
                if after and (k + 1) % (kt // 4) == 0:
                    after[(k + 1) // (kt // 4) - 1]()

        def token_major(pe, B, i, w, c0, c1, x, kt, t):
            bank = B.empty(pe, i)
            for k in range(kt):
                ins = pe.matmul(bank[:, 0:c1 - c0], x[:, k, t * P:t * P + P], w[:, k, c0:c1], start=(k == 0),
                                stop=(k == kt - 1))
            ins.then_inc(full_sem, 1)

        class Residual(Stage):
            products = KD

            def __init__(self, w, x, kt, m, q, T, snake, guest=None):
                self.guest = guest
                self.x, self.kt, self.m, self.q, self.T, self.snake = x, kt, m, q, T, snake
                self.per = min(4, SLOT // (kt * P))
                self.w = w

            def pe(self, pe, B):
                for c in range(0, KD, self.per):
                    w = W.block(pe, [self.w[:, c * P:(c + self.per) * P]], self.kt)
                    for j in range(self.per):
                        places = self.guest and [lambda p=p: self.guest.pe(pe, p) for p in range(4 * (c + j), 4 * (c + j) + 4)]
                        feature_major(pe, B, c + j, w, j * P, self.x, self.kt, 0, self.T, after=places)
                    W.used(full_sem, B.base + c + self.per)

            def act(self, act, B, ch):
                if self.guest:
                    for p in range(32):
                        self.guest.act(act, p)

            def dve(self, dve, B, ch):
                for k in range(KD):
                    if self.guest:
                        self.guest.sums(dve, ch, range(4 * k, 4 * k + 4))
                    bank = B.full(dve, k)

                    def add(h, y, s):
                        return dve.scalar_tensor_tensor(out=h, in0=y, scalar=self.m[:, 8 * self.q + k, s:s + 1], in1=h,
                                                        op0=ALU.mult, op1=ALU.add)
                    if self.snake:
                        for y, h in zip(snaked(bank[:, 0:LAT], True), snaked(hT[:, k, 0:LAT], False)):
                            ins = add(h, y, 0)
                    else:
                        ins = add(hT[:, k, 0:LAT], bank[:, 0:LAT], 0)
                    if self.T == TOK:
                        ins = add(hT[:, k, LAT:TOK], bank[:, LAT:TOK], 1)
                    ins.then_inc(*B.free(k))
                if self.guest:
                    self.guest.dve(dve, ch)

        class HiddenRelu2(Stage):

            def __init__(self, w1, T, guest=None):
                self.guest = guest
                self.T, self.hid = T, arena_at(0, 32, T)
                self.products, self.w1 = 32, w1

            def pe(self, pe, B):
                for c in range(8):
                    w = W.block(pe, [self.w1[:, c * 512:c * 512 + 512]], KD)
                    for j in range(4):
                        feature_major(pe, B, 4 * c + j, w, j * P, uT, KD, 0, self.T)
                        if self.guest:
                            self.guest.pe(pe, 4 * c + j)
                    W.used(full_sem, B.base + 4 * c + 4)

            def act(self, act, B, ch):
                for i in range(32):
                    bank = B.full(act, i)
                    if i >= 2:
                        act.wait_ge(*S("free_a").taken("act"))
                    act.activation(rl[i % 2][:, 0:self.T], bank[:, 0:self.T], ACT.Relu).then_inc(*B.free(i))
                    if self.guest:
                        self.guest.act(act, i)
                for i in range(2):
                    act.wait_ge(*S("free_a").taken("act"))

            def dve(self, dve, B, ch):
                for i in range(32):
                    B.freed(dve, i)
                    r = rl[i % 2][:, 0:self.T]
                    dve.tensor_tensor(self.hid[:, i, :], r, r, ALU.mult).then_inc(*S("free_a").given())
                    if self.guest:
                        self.guest.sums(dve, ch, (i,))
                if self.guest:
                    self.guest.dve(dve, ch)


        HQ = 4
        g_q = arena_at(0, 4, TOK)
        g_k = arena_at(2048, 4, TOK)
        g_v = arena_at(4096, 4, D)
        g_g = arena_at(8192, KD, TOK)
        g_o = arena_at(12288, KD, TOK)
        g_lg = arena_at(16384, 4, 2 * 512)
        g_a = arena_at(20480, 2, TOK)
        ab = arena_at(21504, TOK)
        aexp = arena_at(22016, TOK)

        class GlaProject(Stage):
            projections = [(kind, j) for kind, n in (("a", 2), ("q", 4), ("k", 4), ("v", 8), ("g", 8)) for j in range(n)]
            order = []
            for i_, step_ in enumerate(projections):
                order.append(step_)
                if 6 <= i_ < 14:
                    order.append(("logit", i_ - 6))
            products = len(order)

            def pe(self, pe, B):
                w_in = I["gla_w_in"][0]
                first = dict(a=3072, q=0, k=512, v=1024, g=2048)
                for i, (kind, j) in enumerate(self.order):
                    if kind == "logit":
                        if j == 0:
                            pe.wait_ge(*S("a_rows").taken("pe"))
                        t, z = j // 2, j % 2
                        bank = B.empty(pe, i)
                        pe.matmul(bank[:, :], g_a[0:17, z, t * P:t * P + P], wa2[0:17, z, :], start=True,
                                  stop=True).then_inc(full_sem, 1)
                        continue
                    if j % 4 == 0:
                        c = first[kind] + 128 * j
                        w = W.block(pe, [w_in[:, c:c + (32 if kind == "a" else 512)]], KD)
                    if kind == "a":
                        feature_major(pe, B, i, w, 16 * j, uT, KD, 0, TOK, m=16)
                    elif kind == "v":
                        token_major(pe, B, i, w, 0, 512, uT, KD, j % 4)
                    else:
                        feature_major(pe, B, i, w, (j % 4) * P, uT, KD, 0, TOK)
                    if j % 4 == 3 or (kind, j) == ("a", 1):
                        W.used(full_sem, B.base + i + 1)

            def act(self, act, B, ch):
                for i, (kind, j) in enumerate(self.order):
                    if kind == "q":
                        act.activation(g_q[:, j, :], B.full(act, i)[:, :], ACT.Copy, scale=float(P) ** -0.5).then_inc(*B.free(i))
                    elif kind == "g":
                        act.activation(g_g[:, j, :], B.full(act, i)[:, :], ACT.Silu).then_inc(*B.free(i))
                    elif kind == "logit":
                        bank = B.full(act, i)
                        if j:
                            act.wait_ge(*S("free_a").taken("act"))
                        ch.wait(ch(act.activation(ab, bank[:, :], ACT.Abs)))
                        ch.wait(ch(act.activation(ab, ab, ACT.Exp, scale=-1.0)))
                        act.activation(aexp, ab, ACT.Ln, bias=1.0).then_inc(*S("sg_exp").given())
                act.wait_ge(*S("free_a").taken("act"))

            def dve(self, dve, B, ch):
                dve_link(ch, dve.memset(g_a[0:32, :, :], 1.0))
                for i, (kind, j) in enumerate(self.order):
                    if kind == "a":
                        dve.tensor_copy(g_a[0:16, j, :], B.full(dve, i)[0:16, :]).then_inc(*B.free(i))
                        if j == 1:
                            S("a_rows").given()
                            dve.drain().then_inc(S("a_rows").sem, 1)
                    elif kind == "k":
                        dve.tensor_copy(g_k[:, j, :], B.full(dve, i)[:, :]).then_inc(*B.free(i))
                    elif kind == "v":
                        dst = g_v[:, j % 4, 512 * (j // 4):512 * (j // 4) + 512]
                        dve.tensor_copy(dst, B.full(dve, i)[:, :]).then_inc(*B.free(i))
                    elif kind == "logit":
                        t, z = j // 2, j % 2
                        dve.wait_ge(*S("sg_exp").taken("dve"))
                        dve.scalar_tensor_tensor(out=g_lg[:, t, z * 512:z * 512 + 512], in0=B[i][:, :], scalar=0.0,
                                                 in1=aexp, op0=ALU.min, op1=ALU.subtract).then_inc(*S("free_a").given())
                        dve.drain().then_inc(*B.free(i))

        uf = uT[:, :, :].rearrange("p k t -> p (k t)")

        def heads(off, n=P):
            return uf[:, off:off + HQ * n].rearrange("p (h t) -> p h t", h=HQ)

        d_s, q_s, k_s, e1_s, sm_s, kt_s = (heads(512 * i) for i in range(6))
        sf_s = uf[:, 3072:4096].rearrange("p (h v) -> p h v", h=HQ)
        st_s = arena_at(21504, 4, 256)
        r_s, last_s, er_s, el_s, elr_s, lr_s = (small[:, 4 * i:4 * i + 4] for i in range(6))

        class GlaScan(Stage):
            steps = [(z, t, n) for z in range(2) for n, t in enumerate([(2, 3, 0, 1), (3, 2, 1, 0)][z])]
            products = sum(7 if n < 3 else 5 for _, _, n in steps)

            def pe(self, pe, B):
                i = 0
                for z, t, n in self.steps:
                    bank = B.empty(pe, i)
                    for h in range(HQ):
                        ins = pe.matmul(bank[:, h * P:h * P + P], g_lg[:, t, z * 512 + h * P:z * 512 + h * P + P],
                                        tri[z], start=True, stop=True)
                    ins.then_inc(full_sem, 1)
                    pe.wait_ge(*S("gla_q").taken("pe"))
                    bank = B.empty(pe, i + 1)
                    for h in range(HQ):
                        ins = pe.matmul(bank[:, h * P:h * P + P], k_s[:, h, :], q_s[:, h, :], start=True, stop=True)
                    ins.then_inc(full_sem, 1)
                    bank = B.empty(pe, i + 2)
                    for h in range(HQ):
                        ins = pe.transpose(bank[:, h * P:h * P + P], k_s[:, h, :], ident)
                    ins.then_inc(full_sem, 1)
                    pe.wait_ge(*S("gla_sm").taken("pe"))
                    if n:
                        pe.wait_ge(*S("gla_sp").taken("pe"))
                    for b in range(2):
                        bank = B.empty(pe, i + 3 + b)
                        for j in range(4):
                            h, v = 2 * b + j // 2, j % 2
                            ins = pe.matmul(bank[:, j * P:j * P + P], g_v[:, t, h * 256 + v * P:h * 256 + v * P + P],
                                            sm_s[:, h, :], start=True, stop=(n == 0))
                            if n:
                                ins = pe.matmul(bank[:, j * P:j * P + P], sf_s[:, h, v * P:v * P + P], q_s[:, h, :],
                                                start=False, stop=True)
                        ins.then_inc(full_sem, 1)
                    if n < 3:
                        B.freed(pe, i + 2)
                        for b in range(2):
                            bank = B.empty(pe, i + 5 + b)
                            for j in range(2):
                                h = 2 * b + j
                                ins = pe.matmul(bank[:, j * 256:j * 256 + 256], kt_s[:, h, :],
                                                g_v[:, t, h * 256:h * 256 + 256], start=True, stop=True)
                            ins.then_inc(full_sem, 1)
                    i += 7 if n < 3 else 5

            def act(self, act, B, ch):
                i = 0
                for z, t, n in self.steps:
                    act.wait_ge(*S("gla_d").taken("act"))
                    act.activation(e1_s, d_s, ACT.Exp, scale=1 / 16).then_inc(*S("gla_e").given())
                    ch.wait(ch(act.drain()))
                    act.activation(d_s, d_s, ACT.Exp, scale=-1 / 16).then_inc(*S("gla_e").given())
                    act.activation(er_s, r_s, ACT.Exp, scale=1 / 16)
                    act.activation(el_s, last_s, ACT.Exp, scale=1 / 16)
                    act.activation(elr_s, lr_s, ACT.Exp, scale=1 / 16).then_inc(*S("gla_el").given())
                    bank = B.full(act, i + 2)
                    act.activation(kt_s, bank[:, :].rearrange("p (h t) -> p h t", h=HQ), ACT.Copy).then_inc(*B.free(i + 2))
                    i += 7 if n < 3 else 5

            def dve(self, dve, B, ch):
                i = 0
                for z, t, n in self.steps:
                    mid, last = (63, 127) if z == 0 else (64, 0)
                    bank = B.full(dve, i)
                    cum = bank[:, :].rearrange("p (h t) -> p h t", h=HQ)
                    dve.tensor_copy(r_s, cum[:, :, mid])
                    dve_link(ch, dve.tensor_copy(last_s, cum[:, :, last]))
                    dve_link(ch, dve.tensor_tensor(lr_s, last_s, r_s, ALU.subtract))
                    dve_link(ch, dve.tensor_tensor(d_s, cum, bc(r_s, P), ALU.subtract))
                    S("gla_d").given()
                    dve.drain().then_inc(S("gla_d").sem, 1)
                    B.release(dve, i)
                    dve.wait_ge(*S("gla_e").taken("dve"))
                    dve.tensor_tensor(q_s, e1_s, g_q[:, :, t * P:t * P + P], ALU.mult)
                    dve.wait_ge(*S("gla_e").taken("dve"))
                    dve.tensor_tensor(k_s, d_s, g_k[:, :, t * P:t * P + P], ALU.mult).then_inc(*S("gla_q").given())
                    dve.wait_ge(*S("gla_el").taken("dve"))
                    if n:
                        dve.tensor_tensor(sf_s, st_s, bc(er_s, 256), ALU.mult).then_inc(*S("gla_sp").given())
                    bank = B.full(dve, i + 1)
                    dve.tensor_tensor(sm_s, bank[:, :].rearrange("p (h t) -> p h t", h=HQ), bcm(tri[z], HQ),
                                      ALU.mult).then_inc(*S("gla_sm").given())
                    B.release(dve, i + 1)
                    for b in range(2):
                        bank = B.full(dve, i + 3 + b)
                        src = bank[:, :].rearrange("p (h t) -> p h t", h=4)
                        dst = g_o[:, 4 * b:4 * b + 4, t * P:t * P + P]
                        if z == 0:
                            dve.tensor_copy(dst, src).then_inc(*B.free(i + 3 + b))
                        else:
                            dve.tensor_tensor(dst, src, dst, ALU.add).then_inc(*B.free(i + 3 + b))
                    if n < 3:
                        if n:
                            dve_link(ch, dve.tensor_tensor(st_s, st_s, bc(el_s, 256), ALU.mult))
                        for b in range(2):
                            bank = B.full(dve, i + 5 + b)
                            for j in range(2):
                                h = 2 * b + j
                                if n:
                                    ins = dve.scalar_tensor_tensor(out=st_s[:, h, :], in0=bank[:, j * 256:j * 256 + 256],
                                                                   scalar=elr_s[:, h:h + 1], in1=st_s[:, h, :],
                                                                   op0=ALU.mult, op1=ALU.add)
                                else:
                                    ins = dve.tensor_scalar(st_s[:, h, :], bank[:, j * 256:j * 256 + 256],
                                                            elr_s[:, h:h + 1], None, ALU.mult)
                            ins.then_inc(*B.free(i + 5 + b))
                        dve_link(ch, dve.drain())
                    i += 7 if n < 3 else 5

        class GlaGate(Stage):
            products = HQ

            def pe(self, pe, B):
                for h in range(HQ):
                    bank = B.empty(pe, h)
                    for v in range(2):
                        pe.wait_ge(*S("squares").taken("pe"))
                        ins = pe.matmul(bank[:, :], one, uT[:, 2 * h + v, :], start=(v == 0), stop=(v == 1))
                    ins.then_inc(full_sem, 1)

            def act(self, act, B, ch):
                for k in range(KD):
                    act.activation(uT[:, k, :], g_o[:, k, :], ACT.Square).then_inc(*S("squares").given())
                for h in range(HQ):
                    rstd_act(act, B, ch, h, h, TOK, 256, RMS_EPS)
                rstd_drop(act, HQ)

            def dve(self, dve, B, ch):
                for h in range(HQ):
                    r = rstd_wait(dve, h, TOK)
                    B.release(dve, h)
                    for v in range(2):
                        k = 2 * h + v
                        dve_link(ch, dve.scalar_tensor_tensor(out=g_o[:, k, :], in0=g_o[:, k, :], scalar=vc("gla_norm", v),
                                                              in1=r, op0=ALU.mult, op1=ALU.mult))
                        dve_link(ch, dve.tensor_tensor(g_o[:, k, :], g_o[:, k, :], g_g[:, k, :], ALU.mult))
                    dve.drain().then_inc(*S("rstd_used").given())

        NG = 8
        s_z = arena_at(0, 16, LAT)
        s_y = arena_at(4096, 16, LAT)
        s_dt = arena_at(8192, 4, 64)
        s_da = arena_at(8448, 4, 64)
        s_cj = arena_at(8704, 4, 64)
        s_t1 = arena_at(8960, 64)
        s_t2 = arena_at(9024, 64)
        PADW = LAT + 4
        s_raw = arena[:, 9088:9088 + 4 * 2 * PADW].rearrange("p (f s t) -> p f s t", f=4, s=2)
        s_acc = arena_at(11168, 2, TOK)
        s_f = arena_at(12192, 3, TOK)
        s_c = arena_at(13728, 2, LAT)
        s_xb = arena_at(14240, 2, 4 * 384)
        s_cb = arena_at(17312, 4, P)
        s_dab = [arena_at(17824 + 2048 * i, 4, P) for i in range(2)]
        s_m = [arena_at(18336 + 2048 * i, 4, P) for i in range(2)]
        s_cx = [arena_at(18848 + 2048 * i, 4, P) for i in range(2)]
        s_xdt = [arena_at(19360 + 2048 * i, 4, 64) for i in range(2)]
        s_xw = [arena_at(19616 + 2048 * i, 4, 64) for i in range(2)]
        s_st = arena_at(21920, 2, 256)
        s_tot = halves[:, 0, :]
        s_el, s_lw = (s_tot[:, 256 * i:256 * i + 256].rearrange("p (t h) -> p t h", t=4) for i in range(2))

        class SsdGates(Stage):
            products = 16 + 4 + 2

            def pe(self, pe, B):
                w_in = I["ssd_w_in"][0]
                for c in range(4):
                    w = W.block(pe, [w_in[:, c * 512:c * 512 + 512]], KD)
                    for j in range(4):
                        feature_major(pe, B, 4 * c + j, w, j * P, uT, KD, 0, LAT)
                    W.used(full_sem, B.base + 4 * c + 4)
                w = W.block(pe, [w_in[:, 6144:6208]], KD)
                for t in range(4):
                    token_major(pe, B, 16 + t, w, 0, 64, uT, KD, t)
                W.used(full_sem, B.base + 20)
                pe.wait_ge(*S("da_done").taken("pe"))
                bank = B.empty(pe, 20)
                for t in range(4):
                    for z in range(2):
                        c = 64 * t + 32 * z
                        ins = pe.matmul(bank[:, c:c + 32], tri[z], s_da[:, t, 32 * z:32 * z + 32], start=True, stop=True)
                ins.then_inc(full_sem, 1)
                bank = B.empty(pe, 21)
                pe.matmul(bank[:, 0:256], one, s_da[:, :, :].rearrange("p t h -> p (t h)"), start=True,
                          stop=True).then_inc(full_sem, 1)

            def act(self, act, B, ch):
                for i in range(16):
                    bank = B.full(act, i)
                    act.activation(s_z[:, i, :], bank[:, 0:LAT], ACT.Silu).then_inc(*B.free(i))
                ch.wait(ch(act.activation(alog[:, :], alog[:, :], ACT.Exp)))
                for t in range(4):
                    act.wait_ge(*S("dti").taken("act"))
                    ch.wait(ch(act.activation(s_t1, s_dt[:, t, :], ACT.Abs)))
                    ch.wait(ch(act.activation(s_t1, s_t1, ACT.Exp, scale=-1.0)))
                    act.activation(s_t2, s_t1, ACT.Ln, bias=1.0).then_inc(*S("dtx").given())
                act.wait_ge(*S("lw").taken("act"))
                act.activation(s_tot, s_tot, ACT.Exp).then_inc(*S("lwx").given())

            def dve(self, dve, B, ch):
                dve_link(ch, dve.memset(arena[:, 9088:9088 + 4 * 2 * PADW], 0.0))
                for t in range(4):
                    bank = B.full(dve, 16 + t)
                    dve.tensor_tensor(s_dt[:, t, :], bank[:, 0:64], dtb[:, :], ALU.add).then_inc(*S("dti").given())
                    B.release(dve, 16 + t)
                    dve.wait_ge(*S("dtx").taken("dve"))
                    dve_link(ch, dve.scalar_tensor_tensor(out=s_dt[:, t, :], in0=s_dt[:, t, :], scalar=0.0, in1=s_t2,
                                                          op0=ALU.max, op1=ALU.add))
                    ins = dve.scalar_tensor_tensor(out=s_da[:, t, :], in0=s_dt[:, t, :], scalar=-1.0, in1=alog[:, :],
                                                   op0=ALU.mult, op1=ALU.mult)
                    dve_link(ch, ins)
                S("da_done").given()
                dve.drain().then_inc(S("da_done").sem, 1)
                bank = B.full(dve, 20)
                dve_link(ch, dve.tensor_copy(s_cj, bank[:, 0:256].rearrange("p (t h) -> p t h", t=4)))
                B.release(dve, 20)
                total = B.full(dve, 21)[:, 0:256].rearrange("p (t h) -> p t h", t=4)
                dve.tensor_copy(s_el, total)
                dve.tensor_tensor(s_lw, total, s_cj, ALU.subtract).then_inc(*S("lw").given())
                B.release(dve, 21)
                dve.wait_ge(*S("lwx").taken("dve"))
                dve_link(ch, dve.tensor_tensor(s_lw, s_lw, s_dt, ALU.mult))

        class SsdGroups(Stage):
            steps = [(0, 2), (1, 3), (0, 3), (1, 2), (0, 0), (1, 1), (0, 1), (1, 0)]

            def __init__(self):
                N, order = 8 * NG, []

                def ahead(g, n):
                    if g >= NG:
                        return []
                    out = [("project", g, n)] if n < 4 else []
                    if 1 <= n < 5:
                        out += [("convolve", g, n - 1)]
                    if n in (5, 6):
                        out += [("turn", g, 2 * (n - 5) + t) for t in range(2)]
                    if n == 6:
                        out += [("overlap", g, 0)]
                    return out
                for n in range(8):
                    order += ahead(0, n)
                order += [("spread", 0, 0), ("spread", 1, 0), ("sums", 0, 0), ("decays", 0, 0)]
                for k in range(N + 1):
                    if k:
                        order += [("state", k - 1, 0)]
                    if k + 1 < N:
                        order += [("sums", k + 1, 0)]
                    if k + 2 < N:
                        order += [("spread", k + 2, 0)]
                    if k < N:
                        order += [("products", k, 0)]
                    if k + 1 < N:
                        order += [("decays", k + 1, 0)]
                    if k < N:
                        order += ahead(k // 8 + 1, k % 8)
                order = [ev for ev in order if ev[0] not in ("spread", "sums") or ev[1] % 8 >= 4]
                self.order, self.index, i = order, {}, 0
                for ev in order:
                    kind, k, _ = ev
                    count = {"project": 1, "turn": 1, "overlap": 1, "sums": 1}.get(kind, 0)
                    if kind == "products":
                        z, t = self.steps[k % 8]
                        count = (t < 2) + (k % 8 < 6)
                    if count:
                        self.index[ev] = i
                        i += count
                self.products = i

            def tile(self, g, j):
                return [2 * g, 2 * g + 1, 16 + g, 24 + g][j]

            def last(self, k):
                z, t = self.steps[k % 8]
                return self.index["products", k, 0] + (t < 2) + (k % 8 < 6) - 1

            def feat(self, g, j):
                return s_f[:, j, :] if j < 3 else s_c[:, g % 2, :]

            def pe(self, pe, B):
                w_in = I["ssd_w_in"][0]
                w = None
                for ev in self.order:
                    kind, k, j = ev
                    i = self.index.get(ev)
                    if kind == "project":
                        if j == 0:
                            w = W.block(pe, [w_in[:, 2048 + k * 256:2048 + k * 256 + 256],
                                             w_in[:, 4096 + k * P:4096 + k * P + P],
                                             w_in[:, 5120 + k * P:5120 + k * P + P]], KD)
                        feature_major(pe, B, i, w, j * P, uT, KD, 0, LAT if j == 3 else TOK)
                        if j == 3:
                            W.used(full_sem, B.base + i + 1)
                    if kind == "turn":
                        if j == 0:
                            pe.wait_ge(*S("feat").taken("pe", 4))
                        bank = B.empty(pe, i)
                        for f in range(3):
                            ins = pe.transpose(bank[:, f * P:f * P + P], s_f[:, f, j * P:j * P + P], ident)
                        ins.then_inc(full_sem, 1)
                    if kind == "overlap":
                        bank = B.empty(pe, i)
                        for t in range(2):
                            ins = pe.matmul(bank[:, t * P:t * P + P], s_f[:, 2, t * P:t * P + P],
                                            s_c[:, k % 2, t * P:t * P + P], start=True, stop=True)
                        ins.then_inc(full_sem, 1)
                    if kind == "sums":
                        z, t = self.steps[k % 8]
                        pe.wait_ge(*S("dab").taken("pe"))
                        bank = B.empty(pe, i)
                        for h in range(4):
                            ins = pe.matmul(bank[:, h * P:h * P + P], s_dab[k % 2][:, h, :], tri[z], start=True, stop=True)
                        ins.then_inc(full_sem, 1)
                    if kind == "products":
                        (z, t), g, n = self.steps[k % 8], k // 8, k % 8
                        pe.wait_ge(*S("xw").taken("pe"))
                        if n >= 2:
                            pe.wait_ge(*S("st").taken("pe"))
                        if t < 2:
                            bank = B.empty(pe, i)
                            for h in range(4):
                                o = bank[64 * (h % 2):64 * (h % 2) + 64, (h // 2) * P:(h // 2) * P + P]
                                pe.matmul(o, s_xdt[k % 2][:, h, :], s_m[k % 2][:, h, :], start=True, stop=False)
                                ins = pe.matmul(o, s_st[:, z, h * 64:h * 64 + 64], s_cx[k % 2][:, h, :], start=False, stop=True)
                            ins.then_inc(full_sem, 1)
                            i += 1
                        if n < 6:
                            bank = B.empty(pe, i)
                            pe.matmul(bank[:, 0:256], s_xb[:, g % 2, t * 384 + 256:t * 384 + 384], s_xw[k % 2][:, :, :],
                                      start=True, stop=True).then_inc(full_sem, 1)

            def act(self, act, B, ch):
                for ev in self.order:
                    kind, k, j = ev
                    i = self.index.get(ev)
                    if kind == "project":
                        bank = B.full(act, i)
                        if k:
                            act.wait_ge(*S("conv").taken("act"))
                        n = 1 if j == 3 else 2
                        act.activation(s_raw[:, j, 0:n, 2:2 + LAT], bank[:, 0:n * LAT].rearrange("p (s t) -> p s t", s=n),
                                       ACT.Copy).then_inc(*B.free(i))
                    if kind == "convolve":
                        T = LAT if j == 3 else TOK
                        act.wait_ge(*S("convd").taken("act"))
                        act.activation(self.feat(k, j)[:, 0:T], s_acc[:, j % 2, 0:T], ACT.Silu,
                                       bias=vc("conv_b", self.tile(k, j))).then_inc(*S("feat").given())
                    if kind == "turn":
                        bank = B.full(act, i)
                        act.activation(s_xb[:, k % 2, j * 384:j * 384 + 384], bank[:, 0:384], ACT.Copy).then_inc(*B.free(i))
                    if kind == "spread":
                        (z, t), g = self.steps[k % 8], k // 8
                        c = 32 * z + 4 * g
                        before = k - 2 if k % 8 >= 6 else k - 6
                        if before >= 0:
                            B.full(act, self.index["sums", before, 0])
                        act.activation(s_dab[k % 2], bc(s_da[:, t, c:c + 4], P), ACT.Copy).then_inc(*S("dab").given())
                    if kind == "sums":
                        bank = B.full(act, i)
                        B.full(act, self.last(k - 2))
                        act.activation(s_cx[k % 2], bank[:, :].rearrange("p (h t) -> p h t", h=4),
                                       ACT.Exp).then_inc(*S("ecx").given())
                    if kind == "decays" and k % 8 >= 4:
                        act.wait_ge(*S("seg").taken("act"))
                        act.activation(s_m[k % 2], s_m[k % 2], ACT.Exp).then_inc(*S("segx").given())

            def dve(self, dve, B, ch):
                for ev in self.order:
                    kind, k, j = ev
                    i = self.index.get(ev)
                    if kind == "convolve":
                        f = self.tile(k, j)
                        n = 1 if j == 3 else 2
                        B.freed(dve, self.index["project", k, j])
                        if j >= 2:
                            dve.wait_ge(*S("feat").taken("dve"))
                        acc = s_acc[:, j % 2, 0:n * LAT].rearrange("p (s t) -> p s t", s=n)
                        dve_link(ch, dve.tensor_scalar(acc, s_raw[:, j, 0:n, 0:LAT], vc("conv_w", f), None, ALU.mult))
                        for tap in range(1, 5):
                            ins = dve.scalar_tensor_tensor(out=acc, in0=s_raw[:, j, 0:n, tap:tap + LAT],
                                                           scalar=vc("conv_w", 32 * tap + f), in1=acc,
                                                           op0=ALU.mult, op1=ALU.add)
                            if tap < 4:
                                dve_link(ch, ins)
                            else:
                                ins.then_inc(*S("convd").given())
                        if k < NG - 1:
                            dve.drain().then_inc(*S("conv").given())
                    if kind == "overlap":
                        dve.wait_ge(*S("feat").taken("dve", 2))
                        bank = B.full(dve, i)
                        for f in range(2):
                            c = 2 * k + f
                            dve.tensor_scalar(s_y[:, c, :], s_f[:, f, 0:LAT], dcol[:, c:c + 1], None, ALU.mult)
                        for z in range(2):
                            dve_link(ch, dve.tensor_tensor(s_cb[:, 2 * z:2 * z + 2, :],
                                                           bank[:, 0:256].rearrange("p (t i) -> p t i", t=2),
                                                           bcm(tri[z], 2), ALU.mult))
                        B.release(dve, i)
                        for t in range(4):
                            B.freed(dve, self.index["turn", k, t])
                    if kind == "sums":
                        (z, t), g = self.steps[k % 8], k // 8
                        c = 32 * z + 4 * g
                        bank = B.full(dve, i)
                        cum = bank[:, :].rearrange("p (h t) -> p h t", h=4)
                        dve.wait_ge(*S("ecx").taken("dve"))
                        B.full(dve, self.last(k - 2))
                        for h in range(4):
                            ins = dve.tensor_scalar(s_m[k % 2][:, h, :], cum[:, h, :], s_cj[:, t, c + h:c + h + 1], 0.0,
                                                    ALU.subtract, ALU.min)
                        ins.then_inc(*S("seg").given())
                        B.release(dve, i)
                    if kind == "decays":
                        (z, t), g = self.steps[k % 8], k // 8
                        c = 32 * z + 4 * g
                        if k >= 2:
                            B.full(dve, self.last(k - 2))
                        x = s_xb[:, g % 2, t * 384:t * 384 + 256].rearrange("p (h d) -> p h d", h=4)
                        if k % 8 < 6:
                            ins = dve.tensor_tensor(s_xw[k % 2], x, bc(s_lw[:, t, c:c + 4], 64), ALU.mult)
                        if t < 2:
                            dve.tensor_tensor(s_xdt[k % 2], x, bc(s_dt[:, t, c:c + 4], 64), ALU.mult)
                            dve.tensor_tensor(s_cx[k % 2], s_cx[k % 2], bcm(s_c[:, g % 2, t * P:t * P + P], 4), ALU.mult)
                            dve.wait_ge(*S("segx").taken("dve"))
                            ins = dve.tensor_tensor(s_m[k % 2], s_m[k % 2], bcm(s_cb[:, 2 * z + t, :], 4), ALU.mult)
                        ins.then_inc(*S("xw").given())
                    if kind == "state":
                        (z, t), g, n = self.steps[k % 8], k // 8, k % 8
                        i = self.index["products", k, 0]
                        if t < 2:
                            bank = B.full(dve, i)
                            y = s_y[:, 2 * g:2 * g + 2, t * P:t * P + P]
                            dve.tensor_tensor(y, bank[:, 0:256].rearrange("p (f i) -> p f i", f=2), y,
                                              ALU.add).then_inc(*B.free(i))
                            i += 1
                        if n < 6:
                            st = s_st[:, z, :]
                            if n >= 2:
                                v = st.rearrange("p (h d) -> p h d", h=4)
                                dve_link(ch, dve.tensor_tensor(v, v, bc(s_el[:, t, 32 * z + 4 * g:32 * z + 4 * g + 4], 64), ALU.mult))
                            bank = B.full(dve, i)
                            if n >= 2:
                                ins = dve.tensor_tensor(st, bank[:, 0:256], st, ALU.add)
                            else:
                                ins = dve.tensor_copy(st, bank[:, 0:256])
                            ins.then_inc(*S("st").given())
                            B.release(dve, i)

        s_sq = arena_at(9088, 16, LAT)

        class SsdGate(Stage):
            products = 1

            def pe(self, pe, B):
                bank = B.empty(pe, 0)
                for k in range(16):
                    pe.wait_ge(*S("squares").taken("pe"))
                    ins = pe.matmul(bank[:, 0:LAT], one, s_sq[:, k, :], start=(k == 0), stop=(k == 15))
                ins.then_inc(full_sem, 1)

            def act(self, act, B, ch):
                for k in range(16):
                    act.wait_ge(*S("normed").taken("act"))
                    act.activation(s_sq[:, k, :], s_y[:, k, :], ACT.Square).then_inc(*S("squares").given())
                rstd_act(act, B, ch, 0, 0, LAT, 2048, RMS_EPS)

            def dve(self, dve, B, ch):
                for k in range(16):
                    dve.tensor_tensor(s_y[:, k, :], s_y[:, k, :], s_z[:, k, :], ALU.mult).then_inc(*S("normed").given())
                dve_link(ch, dve.drain())
                r = rstd_wait(dve, 0, LAT)
                B.release(dve, 0)
                for k in range(16):
                    dve.scalar_tensor_tensor(out=s_y[:, k, :], in0=s_y[:, k, :], scalar=vc("ssd_norm", k), in1=r,
                                             op0=ALU.mult, op1=ALU.mult)

        class LoadCtx(Stage):
            products = KD

            def act(self, act, B, ch):
                act.dma_start(xrow[:, 0:2, :], I["ctx_2"].rearrange("o (t p) d -> p (o t) d", p=P))\
                   .then_inc(S("bias_loads").sem, 16)

            def pe(self, pe, B):
                pe.wait_ge(S("bias_loads").sem, 16)
                for k in range(KD):
                    bank = B.empty(pe, k)
                    for t in range(2):
                        ins = pe.transpose(bank[:, t * P:t * P + P], xrow[:, t, k * P:k * P + P], ident)
                    ins.then_inc(full_sem, 1)

            def dve(self, dve, B, ch):
                for k in range(KD):
                    bank = B.full(dve, k)
                    dve.tensor_copy(hT[:, k, LAT:TOK], bank[:, 0:CTX]).then_inc(*B.free(k))

        m_y = arena_at(0, KD, TOK)
        m_q = arena_at(4096, 8, TOK)
        m_k = arena_at(8192, 6, TOK)
        m_v = arena_at(11264, 4, 640)
        m_g = arena_at(13824, 4, TOK)
        m_bias = arena_at(13824, 8, 6, GRID)
        m_pad = arena_at(15872, 4, 2 * (LAT + 2))
        m_gc = arena_at(6144, 4, TOK)
        m_s = [[uT[:, 2 * i + j, :] for j in range(2)] for i in range(2)]
        m_pt = [uT[:, 4 + i, :] for i in range(2)]
        sinks = sb("sinks", [P, 8])

        class EvenProject(Stage):
            products = 24

            def pe(self, pe, B):
                w_in = I["ev_w_in_2"][0]
                for c in range(6):
                    w = W.block(pe, [w_in[:, c * 512:c * 512 + 512]], KD)
                    for j in range(4):
                        if c == 5:
                            token_major(pe, B, 4 * c + j, w, 0, 512, uT, KD, j)
                        else:
                            feature_major(pe, B, 4 * c + j, w, j * P, uT, KD, 0, TOK)
                    W.used(full_sem, B.base + 4 * c + 4)

            def act(self, act, B, ch):
                for i in range(8):
                    bank = B.full(act, i)
                    act.activation((m_g if i < 4 else m_gc)[:, i % 4, :], bank[:, :], ACT.Copy).then_inc(*B.free(i))
                for i in range(12, 24, 2):
                    bank = B.full(act, i)
                    act.activation(self.dst(i), bank[:, :], ACT.Copy).then_inc(*B.free(i))

            def dst(self, i):
                return [m_q, m_k, m_v][(i - 12) // 4][:, i % 4, 0:512]

            def dve(self, dve, B, ch):
                dve_link(ch, dve.memset(arena[:, 15872:15872 + 8 * (LAT + 2)], 0.0))
                for j in range(4):
                    pad = m_pad[:, j, :].rearrange("p (s t) -> p s t", s=2)
                    acc = m_y[:, j, :].rearrange("p (s t) -> p s t", s=2)
                    bank = B.full(dve, 8 + j)
                    B.freed(dve, 4 + j)
                    dve.tensor_tensor(pad[:, :, 1:1 + LAT], bank[:, :].rearrange("p (s t) -> p s t", s=2),
                                      m_gc[:, j, :].rearrange("p (s t) -> p s t", s=2), ALU.mult).then_inc(*B.free(8 + j))
                    B.freed(dve, 8 + j)
                    dve_link(ch, dve.tensor_scalar(acc, pad[:, :, 0:LAT], vc("ev_conv", j), None, ALU.mult))
                    for tap in (1, 2):
                        dve_link(ch, dve.scalar_tensor_tensor(out=acc, in0=pad[:, :, tap:tap + LAT],
                                                              scalar=vc("ev_conv", 4 * tap + j), in1=acc,
                                                              op0=ALU.mult, op1=ALU.add))
                    dve_link(ch, dve.tensor_tensor(m_y[:, j, :], m_y[:, j, :], m_g[:, j, :], ALU.mult))
                for i in range(13, 24, 2):
                    bank = B.full(dve, i)
                    dve.tensor_copy(self.dst(i), bank[:, :]).then_inc(*B.free(i))

        m_braw = arena_at(16896, 8, 6, GRID)

        class BiasLoad(Stage):
            products = 6

            def act(self, act, B, ch):
                t = I["ev_rpb_2"]
                for b in range(2):
                    for h in range(8):
                        src = bass.AP(tensor=t.tensor, offset=h * 15 * 31 + (5 - b) * 31 + 15 - 63,
                                      ap=[[1, GRID], [31, 6], [1, GRID]])
                        act.dma_start(m_braw[64 * b:64 * b + 64, h, :, :], src).then_inc(S("moe_loads").sem, 16)

            def pe(self, pe, B):
                pe.wait_ge(S("moe_loads").sem, 16 * 16)
                raw = m_braw.rearrange("p h m c -> p (h m c)")
                for i in range(6):
                    bank = B.empty(pe, i)
                    pe.matmul(bank[:, :], const[:, C_FLIP:C_FLIP + P], raw[:, i * 512:i * 512 + 512], start=True,
                              stop=True).then_inc(full_sem, 1)

            def dve(self, dve, B, ch):
                v = m_bias.rearrange("p h m c -> p (h m) c")
                for i in range(6):
                    bank = B.full(dve, i)
                    dve.tensor_tensor(v[:, 8 * i:8 * i + 8, :], bank[:, :].rearrange("p (a c) -> p a c", a=8),
                                      bcm(const[:, C_COL:C_COL + GRID], 8), ALU.add).then_inc(*B.free(i))

        class HeadNorm(Stage):

            def __init__(self, tiles, rope):
                self.tiles, self.rope = tiles, rope
                self.products = len(tiles) * (2 if rope else 1)
                self.sq = [rl[0], rl[1]]

            def pe(self, pe, B):
                n = len(self.tiles)
                for i, (x, gain, T) in enumerate(self.tiles):
                    pe.wait_ge(*S("squares").taken("pe"))
                    bank = B.empty(pe, i)
                    pe.matmul(bank[:, 0:T], half, self.sq[i % 2][:, 0:T], start=True, stop=True).then_inc(full_sem, 1)
                if self.rope:
                    for i, (x, gain, T) in enumerate(self.tiles):
                        pe.wait_ge(*S("rope_in").taken("pe"))
                        bank = B.empty(pe, n + i)
                        pe.matmul(bank[:, 0:LAT], rot, x[:, 0:LAT], start=True, stop=True).then_inc(full_sem, 1)

            def act(self, act, B, ch):
                for i, (x, gain, T) in enumerate(self.tiles):
                    if i >= 2:
                        B.full(act, i - 2)
                    act.activation(self.sq[i % 2][:, 0:T], x, ACT.Square).then_inc(*S("squares").given())
                    if i >= 1:
                        rstd_act(act, B, ch, i - 1, i - 1, self.tiles[i - 1][2], 64, RMS_EPS)
                n = len(self.tiles)
                rstd_act(act, B, ch, n - 1, n - 1, self.tiles[-1][2], 64, RMS_EPS)
                rstd_drop(act, n)

            def dve(self, dve, B, ch):
                n = len(self.tiles)
                for i, (x, gain, T) in enumerate(self.tiles):
                    r = rstd_wait(dve, i, T)
                    B.release(dve, i)
                    ins = dve.scalar_tensor_tensor(out=x, in0=x, scalar=vc(gain), in1=r, op0=ALU.mult, op1=ALU.mult)
                    if self.rope:
                        ins.then_inc(*S("rope_in").given())
                        dve.wait_ge(S("rope_in").sem, S("rope_in").made)
                    else:
                        dve_link(ch, ins)
                    dve.drain().then_inc(*S("rstd_used").given())
                if self.rope:
                    cos, sin = const[:, C_COS:C_COS + LAT], const[:, C_SIN:C_SIN + LAT]
                    for i, (x, gain, T) in enumerate(self.tiles):
                        bank = B.full(dve, n + i)
                        dve_link(ch, dve.tensor_tensor(rl[0][:, 0:LAT], bank[:, 0:LAT], sin, ALU.mult))
                        dve_link(ch, dve.tensor_tensor(x[:, 0:LAT], x[:, 0:LAT], cos, ALU.mult))
                        dve_link(ch, dve.tensor_tensor(x[:, 0:LAT], x[:, 0:LAT], rl[0][:, 0:LAT], ALU.add))
                        B.release(dve, n + i)

        class Attention(Stage):

            def __init__(self, items, lam=None):
                self.items, self.lam = items, lam
                self.ns = len(items[0]["q"])
                order = []
                for n in range(-2, len(items) + 1):
                    order += [("s", n + 2, j) for j in range(self.ns)]
                    order += [("t", n, 0), ("o", n - 1, 0)]
                order = [key for key in order if 0 <= key[1] < len(items)]
                self.order = {key: i for i, key in enumerate(order)}
                self.products = len(order)

            def pe(self, pe, B):
                for (kind, n, j), i in self.order.items():
                    it = self.items[n]
                    nk = it["nk"]
                    if kind == "s":
                        bank = B.empty(pe, i)
                        pe.matmul(bank[:, 0:nk], it["q"][j], it["k"][j], start=True, stop=True).then_inc(full_sem, 1)
                    elif kind == "t":
                        pe.wait_ge(*S("pn").taken("pe"))
                        bank = B.empty(pe, i)
                        for t in range(nk // P):
                            ins = pe.transpose(bank[:, t * P:t * P + P], m_s[n % 2][0][:, t * P:t * P + P], ident)
                        ins.then_inc(full_sem, 1)
                    else:
                        B.freed(pe, self.order["t", n, 0])
                        bank = B.empty(pe, i)
                        r0, m = it["rows"]
                        for t, v in enumerate(it["v"]):
                            ins = pe.matmul(bank[r0:r0 + m, 0:P], v, m_pt[n % 2][:, t * P:t * P + P], start=(t == 0),
                                            stop=(t == len(it["v"]) - 1))
                        ins.then_inc(full_sem, 1)

            def stats(self, n, j):
                o = 24 * (n % 2) + 12 * j
                return [small[:, o + x:o + x + 1] for x in range(5)]

            def act(self, act, B, ch):
                def exps(n):
                    it = self.items[n]
                    for j in range(self.ns):
                        mx, nm, den, es, rc = self.stats(n, j)
                        act.wait_ge(*S("nm").taken("act"))
                        s = m_s[n % 2][j][:, 0:it["nk"]]
                        if it["sink"] is not None:
                            act.activation(es, it["sink"], ACT.Exp, bias=nm)
                        act.activation(s, s, ACT.Exp, bias=nm, accum_out=den)
                        act.drain().then_inc(*S("pr").given())
                for n in range(-1, len(self.items)):
                    if n + 1 < len(self.items):
                        exps(n + 1)
                    if n >= 0:
                        i, nk = self.order["t", n, 0], self.items[n]["nk"]
                        if n >= 2:
                            B.full(act, self.order["o", n - 2, 0])
                        bank = B.full(act, i)
                        act.activation(m_pt[n % 2][:, 0:nk], bank[:, 0:nk], ACT.Copy).then_inc(*B.free(i))

            def dve(self, dve, B, ch):
                def scores(n):
                    it = self.items[n]
                    nk = it["nk"]
                    for j in range(self.ns):
                        mx, nm, den, es, rc = self.stats(n, j)
                        i = self.order["s", n, j]
                        bank = B.full(dve, i)
                        if n >= 2 and j == 0:
                            B.full(dve, self.order["t", n - 2, 0])
                        s = m_s[n % 2][j]
                        b = 0
                        if it["bias"] is not None:
                            b = LAT
                            dve.scalar_tensor_tensor(out=s[:, 0:b], in0=bank[:, 0:b], scalar=0.125, in1=it["bias"],
                                                     op0=ALU.mult, op1=ALU.add)
                        dve_link(ch, dve.tensor_scalar(s[:, b:nk], bank[:, b:nk], 0.125, None, ALU.mult))
                        B.release(dve, i)
                        dve_link(ch, dve.tensor_reduce(mx, s[:, 0:nk], AX.X, ALU.max))
                        if it["sink"] is not None:
                            dve_link(ch, dve.tensor_tensor(mx, mx, it["sink"], ALU.max))
                        dve.tensor_scalar(nm, mx, -1.0, None, ALU.mult).then_inc(*S("nm").given())

                def output(n):
                    i = self.order["o", n, 0]
                    bank = B.full(dve, i)
                    r0, m = self.items[n]["rows"]
                    dve.tensor_copy(self.items[n]["o"], bank[r0:r0 + m, 0:P]).then_inc(*B.free(i))

                def normalise(n):
                    it = self.items[n]
                    for j in range(self.ns):
                        mx, nm, den, es, rc = self.stats(n, j)
                        dve.wait_ge(*S("pr").taken("dve"))
                        if it["sink"] is not None:
                            dve_link(ch, dve.tensor_tensor(den, den, es, ALU.add))
                        dve_link(ch, dve.reciprocal(rc, den))
                    s0 = m_s[n % 2][0][:, 0:it["nk"]]
                    r0 = self.stats(n, 0)[4]
                    if self.ns == 1:
                        dve.tensor_scalar(s0, s0, r0, None, ALU.mult).then_inc(*S("pn").given())
                    else:
                        s1, r1 = m_s[n % 2][1][:, 0:it["nk"]], self.stats(n, 1)[4]
                        dve_link(ch, dve.tensor_scalar(s1, s1, r1, self.lam, ALU.mult, ALU.mult))
                        dve.scalar_tensor_tensor(out=s0, in0=s0, scalar=r0, in1=s1, op0=ALU.mult,
                                                 op1=ALU.add).then_inc(*S("pn").given())
                for n in range(-1, len(self.items)):
                    if n + 1 < len(self.items):
                        scores(n + 1)
                    if n >= 0:
                        normalise(n)
                    if n >= 1:
                        output(n - 1)
                output(len(self.items) - 1)

        def even_items():
            items = []
            for h in range(8):
                r, f = 64 * (h % 2), h // 2
                for t in range(4):
                    lat = t < 2
                    ks = 0 if lat else LAT
                    items.append(dict(
                        q=[m_q[r:r + 64, f, t * P:t * P + P]], k=[m_k[r:r + 64, f, ks:TOK]], nk=TOK - ks,
                        bias=m_bias[:, h, 2 - 2 * t:6 - 2 * t, :].rearrange("p m c -> p (m c)") if lat else None, sink=None,
                        v=[m_v[:, j, h * 64:h * 64 + 64] for j in range(ks // P, 4)], rows=(r, 64),
                        o=m_y[r:r + 64, 4 + f, t * P:t * P + P]))
            return items

        def window_items():
            items = []
            for h in range(8):
                r, f = 64 * (h % 2), h // 2
                for t in range(2):
                    items.append(dict(
                        q=[m_q[r:r + 64, f, t * P:t * P + P]], k=[m_k[r:r + 64, h // 4, :]], nk=TOK,
                        bias=const[:, C_SWA + t * LAT:C_SWA + t * LAT + LAT], sink=sinks[:, h:h + 1],
                        v=[m_v[:, j, 64 * (h // 4):64 * (h // 4) + 64] for j in range(4)], rows=(r, 64),
                        o=m_y[r:r + 64, f, t * P:t * P + P]))
            return items

        def diff_items():
            return [dict(q=[m_q[64 * i:64 * i + 64, 4 + h, t * P:t * P + P] for i in range(2)],
                         k=[m_k[64 * i:64 * i + 64, 2 + h, :] for i in range(2)], nk=TOK, bias=None, sink=None,
                         v=[m_v[:, j, P + h * P:P + h * P + P] for j in range(4)], rows=(0, P),
                         o=m_y[:, 4 + h, t * P:t * P + P])
                    for h in range(4) for t in range(2)]

        class HiddenSwiglu(Stage):

            def __init__(self, w1, w3, T, guest=None):
                self.guest = guest
                self.places = {f: range(32 * f // (w1.shape[1] // P), 32 * (f + 1) // (w1.shape[1] // P))
                               for f in range(w1.shape[1] // P)}
                self.nf, self.T = w1.shape[1] // P, T
                self.hid = arena_at(0, self.nf, T)
                self.products = 2 * self.nf
                self.w = (w1, w3)

            def pe(self, pe, B):
                for c in range(0, self.nf, 4):
                    n = min(4, self.nf - c)
                    a, b = (W.block(pe, [w[:, c * P:(c + n) * P]], KD) for w in self.w)
                    for j in range(n):
                        feature_major(pe, B, 2 * (c + j), a, j * P, uT, KD, 0, self.T)
                        feature_major(pe, B, 2 * (c + j) + 1, b, j * P, uT, KD, 0, self.T)
                        for p in self.places[c + j] if self.guest else ():
                            self.guest.pe(pe, p)
                    W.used(full_sem, B.base + 2 * (c + n))
                    W.used(full_sem, B.base + 2 * (c + n))

            def act(self, act, B, ch):
                for f in range(self.nf):
                    bank = B.full(act, 2 * f)
                    if f >= 2:
                        act.wait_ge(*S("free_a").taken("act"))
                    act.activation(rl[f % 2][:, 0:self.T], bank[:, 0:self.T], ACT.Silu).then_inc(*B.free(2 * f))
                    for p in self.places[f] if self.guest else ():
                        self.guest.act(act, p)
                for f in range(2):
                    act.wait_ge(*S("free_a").taken("act"))

            def dve(self, dve, B, ch):
                for f in range(self.nf):
                    B.freed(dve, 2 * f)
                    bank = B.full(dve, 2 * f + 1)
                    h = self.hid[:, f, :]
                    dve.tensor_tensor(h, bank[:, 0:self.T], rl[f % 2][:, 0:self.T], ALU.mult).then_inc(*S("free_a").given())
                    B.release(dve, 2 * f + 1)
                    if self.guest:
                        self.guest.sums(dve, ch, self.places[f])
                if self.guest:
                    self.guest.dve(dve, ch)

        class OddProject(Stage):
            products = 4 + 4 + 1 + 4 + 4 + 4

            cuts = ((0, 512), (512, 1024), (1024, 1280), (1280, 1792), (1792, 2304))

            def pe(self, pe, B):
                i = 0
                for c, (c0, c1) in enumerate(self.cuts):
                    w = W.block(pe, [I["od_w_in_2"][0][:, c0:c1]], KD)
                    if c == 2:
                        feature_major(pe, B, i, w, 0, uT, KD, 0, TOK)
                        i += 1
                    for j in range(4):
                        if c == 2:
                            token_major(pe, B, i, w, P, 2 * P, uT, KD, j)
                        elif c == 4:
                            token_major(pe, B, i, w, 0, 512, uT, KD, j)
                        else:
                            feature_major(pe, B, i, w, j * P, uT, KD, 0, LAT if c < 2 else TOK)
                        i += 1
                    W.used(full_sem, B.base + i)

            def dst(self, i):
                if i < 8:
                    return m_q[:, i, 0:LAT]
                if i == 8:
                    return m_k[:, 0, :]
                if i < 13:
                    return m_v[:, i - 9, 0:P]
                if i < 17:
                    return m_k[:, 2 + i - 13, :]
                return m_v[:, i - 17, P:P + 512]

            def act(self, act, B, ch):
                for i in range(0, 21, 2):
                    bank, d = B.full(act, i), self.dst(i)
                    act.activation(d, bank[:, 0:d.shape[1]], ACT.Copy).then_inc(*B.free(i))

            def dve(self, dve, B, ch):
                for i in range(1, 21, 2):
                    bank, d = B.full(dve, i), self.dst(i)
                    dve.tensor_copy(d, bank[:, 0:d.shape[1]]).then_inc(*B.free(i))

        LAM_INIT = 0.8 - 0.6 * math.exp(-0.3)
        lam_t = small[:, 60:61]

        class KeysAndLambda(Stage):
            products = 3

            def pe(self, pe, B):
                for g in range(2):
                    bank = B.empty(pe, g)
                    pe.matmul(bank[:, :], const[:, C_DUP + g * P:C_DUP + g * P + P], m_k[:, 0, :], start=True,
                              stop=True).then_inc(full_sem, 1)
                pe.wait_ge(*S("lam").taken("pe"))
                bank = B.empty(pe, 2)
                pe.matmul(bank[:, 0:2], one[0:64, :], small[0:64, 56:58], start=True, stop=True).then_inc(full_sem, 1)

            def act(self, act, B, ch):
                act.dma_start(sinks[:, :], flat(I["od_sink_2"]).partition_broadcast(P)).then_inc(S("bias_loads").sem, 16)
                act.wait_ge(S("bias_loads").sem, 32)
                bank = B.full(act, 2)
                act.activation(small[:, 58:60], bank[:, 0:2], ACT.Exp).then_inc(*B.free(2))

            def dve(self, dve, B, ch):
                dve.tensor_tensor(small[0:64, 56:57], lamv[0:64, 0:1], lamv[0:64, 1:2], ALU.mult)
                dve.tensor_tensor(small[0:64, 57:58], lamv[0:64, 2:3], lamv[0:64, 3:4], ALU.mult).then_inc(*S("lam").given())
                for g in range(2):
                    B.full(dve, 1)
                    bank = B.full(dve, g)
                    dve.tensor_copy(m_k[:, g, :], bank[:, :]).then_inc(*B.free(g))
                B.freed(dve, 2)
                dve_link(ch, dve.tensor_tensor(lam_t, small[:, 59:60], small[:, 58:59], ALU.subtract))
                dve_link(ch, dve.tensor_scalar(lam_t, lam_t, -LAM_INIT, None, ALU.add))

        class SubNorm(Stage):
            products = 4

            def pe(self, pe, B):
                for h in range(4):
                    pe.wait_ge(*S("squares").taken("pe"))
                    bank = B.empty(pe, h)
                    pe.matmul(bank[:, 0:LAT], one, uT[:, h, 0:LAT], start=True, stop=True).then_inc(full_sem, 1)

            def act(self, act, B, ch):
                for h in range(4):
                    act.activation(uT[:, h, 0:LAT], m_y[:, 4 + h, 0:LAT], ACT.Square).then_inc(*S("squares").given())
                for h in range(4):
                    rstd_act(act, B, ch, h, h, LAT, P, RMS_EPS)
                rstd_drop(act, 4)

            def dve(self, dve, B, ch):
                dve_link(ch, dve.tensor_scalar(small[:, 61:62], vc("subln"), 1.0 - LAM_INIT, None, ALU.mult))
                for h in range(4):
                    r = rstd_wait(dve, h, LAT)
                    B.release(dve, h)
                    y = m_y[:, 4 + h, 0:LAT]
                    dve_link(ch, dve.scalar_tensor_tensor(out=y, in0=y, scalar=small[:, 61:62], in1=r,
                                                          op0=ALU.mult, op1=ALU.mult))
                    dve.drain().then_inc(*S("rstd_used").given())

        NE = 8
        lg = arena[:, 6144:6240].rearrange("p (t i e) -> p t i e", t=2, i=6)
        routing = sb("routing", [P, 7, NE])
        overflow = ctx.enter_context(nc.sbuf_tensor("overflow", [1, 1], mybir.dt.int32))

        class Router(Stage):
            products = 2 + 1

            def pe(self, pe, B):
                w = W.block(pe, [I["moe_router_2"][0]], KD)
                for t in range(2):
                    token_major(pe, B, t, w, 0, NE, uT, KD, t)
                W.used(full_sem, B.base + 2)
                pe.wait_ge(*S("picked").taken("pe"))
                bank = B.empty(pe, 2)
                pe.matmul(bank[:, 0:NE], tri[0], routing[:, 0, :], start=True, stop=True)
                for c, m in ((1, tri[0]), (2, one)):
                    pe.matmul(bank[:, c * NE:c * NE + NE], one, routing[:, 0, :], start=True, stop=False)
                    ins = pe.matmul(bank[:, c * NE:c * NE + NE], m, routing[:, 1, :], start=False, stop=True)
                ins.then_inc(full_sem, 1)

            def act(self, act, B, ch):
                for t in range(2):
                    act.wait_ge(*S("dti").taken("act"))
                    act.activation(lg[:, t, 2, :], lg[:, t, 0, :], ACT.Exp, bias=small[:, 62:63]).then_inc(*S("dtx").given())

            def dve(self, dve, B, ch):
                for t in range(2):
                    l, mx, e, gt, eq, run_ = (lg[:, t, i, :] for i in range(6))
                    bank = B.full(dve, t)
                    dve_link(ch, dve.tensor_copy(l, bank[:, 0:NE]))
                    B.release(dve, t)
                    dve_link(ch, dve.max(mx, l))
                    dve.tensor_scalar(small[:, 62:63], mx[:, 0:1], -1.0, None, ALU.mult).then_inc(*S("dti").given())
                    dve.tensor_scalar(gt, l, mx[:, 1:2], None, ALU.is_gt)
                    dve_link(ch, dve.tensor_scalar(eq, l, mx[:, 1:2], None, ALU.is_equal))
                    dve.tensor_tensor_scan(run_, one[:, 0:NE], eq, 0.0, ALU.mult, ALU.add)
                    dve_link(ch, dve.tensor_reduce(small[:, 63:64], gt, AX.X, ALU.add))
                    dve_link(ch, dve.tensor_scalar(run_, run_, small[:, 63:64], None, ALU.add))
                    dve_link(ch, dve.scalar_tensor_tensor(out=eq, in0=run_, scalar=2.0, in1=eq, op0=ALU.is_le, op1=ALU.mult))
                    dve.wait_ge(*S("dtx").taken("dve"))
                    dve_link(ch, dve.tensor_tensor(routing[:, t, :], gt, eq, ALU.add))
                    dve_link(ch, dve.tensor_tensor(l, routing[:, t, :], e, ALU.mult))
                    dve_link(ch, dve.tensor_reduce(small[:, 63:64], l, AX.X, ALU.add))
                    dve_link(ch, dve.reciprocal(small[:, 63:64], small[:, 63:64]))
                    dve_link(ch, dve.tensor_scalar(routing[:, 4 + t, :], l, small[:, 63:64], None, ALU.mult))
                S("picked").given()
                dve.drain().then_inc(S("picked").sem, 1)
                bank = B.full(dve, 2)
                place = routing[:, 2:4, :].rearrange("p t e -> p (t e)")
                dve_link(ch, dve.tensor_tensor(place, bank[:, 0:2 * NE], routing[:, 0:2, :].rearrange("p t e -> p (t e)"),
                                               ALU.mult))
                dve_link(ch, dve.tensor_scalar(place, place, -1.0, None, ALU.add))
                dve_link(ch, dve.tensor_reduce(small[0:1, 63:64], bank[0:1, 2 * NE:3 * NE], AX.X, ALU.max))
                B.release(dve, 2)
                dve_link(ch, dve.tensor_scalar(small[0:1, 62:63], small[0:1, 63:64], float(P), None, ALU.is_gt))
                dve.tensor_copy(overflow[:, :], small[0:1, 62:63]).then_inc(*S("overflow_known").given())

        NFE = I["moe_w1_2"].shape[3] // P
        m_xt = arena_at(0, 2, D)
        m_sel = arena_at(2048, 2, NE * P)
        m_selg = arena_at(4096, 2, NE * P)
        m_slot = arena_at(6144, NE, LAT)
        m_x = arena_at(8192, KD, NE * P)
        m_hid = [arena_at(16384 + i * NFE * P, NFE, P) for i in range(2)]
        m_yt = [arena_at(16384 + 2 * NFE * P + i * D, D) for i in range(2)]
        place = routing[:, 2:4, :]

        class Experts(Stage):
            XT, ST, GA = 0, 4, 8
            NH = (NFE + 1) // 2
            FIRST = 24
            products = 24 + NE * (NH + 4 + 4)

            def __init__(self, n):
                self.n = n

            def hidden(self, e):
                return self.FIRST + e * (self.NH + 8) - (4 if e else 0)

            def scatter(self, e):
                return self.hidden(e + 1) + self.NH if e < NE - 1 else self.products - 4

            def output(self, e):
                return self.hidden(e) + self.NH + (4 if e else 0)

            def tiles(self, i):
                return range(2 * i, min(2 * i + 2, NFE))

            def pe(self, pe, B):
                if self.n == 1:
                    W.second_pass = len(W.plan)
                for i in range(4):
                    t, c = i // 2, i % 2
                    bank = B.empty(pe, self.XT + i)
                    for j in range(4):
                        ins = pe.transpose(bank[:, j * P:j * P + P], uT[:, 4 * c + j, t * P:t * P + P], ident)
                    ins.then_inc(full_sem, 1)
                pe.wait_ge(*S("gate_cols").taken("pe"))
                for i in range(4):
                    bank = B.empty(pe, self.ST + i)
                    for j in range(2):
                        for t in range(2):
                            c = (2 * i + j) * P
                            ins = pe.transpose(bank[:, j * LAT + t * P:j * LAT + t * P + P], m_selg[:, t, c:c + P], ident)
                    ins.then_inc(full_sem, 1)
                for i in range(4):
                    B.freed(pe, self.XT + i)
                for i in range(16):
                    c, k = i // KD, i % KD
                    bank = B.empty(pe, self.GA + i)
                    for t in range(2):
                        ins = pe.matmul(bank[:, :], m_xt[:, t, k * P:k * P + P], m_sel[:, t, c * 512:c * 512 + 512],
                                        start=(t == 0), stop=(t == 1))
                    ins.then_inc(full_sem, 1)
                for e in range(NE):
                    if e in (0, 4):
                        for k in range(2, KD):
                            B.freed(pe, self.GA + 2 * e + k)
                    h0 = self.hidden(e)
                    for c in range(0, NFE, 4):
                        n = min(4, NFE - c)
                        w1, w3 = (W.block(pe, [I[nm][0, e][:, c * P:(c + n) * P]], KD) for nm in ("moe_w1_2", "moe_w3_2"))
                        for i in range(c // 2, (c + n + 1) // 2):
                            bank = B.empty(pe, h0 + i)
                            for f in self.tiles(i):
                                for half_, w in enumerate((w1, w3)):
                                    o = half_ * 256 + (f % 2) * P
                                    for k in range(KD):
                                        ins = pe.matmul(bank[:, o:o + P], w[:, k, (f - c) * P:(f - c) * P + P],
                                                        m_x[:, k, e * P:e * P + P], start=(k == 0), stop=(k == KD - 1))
                            ins.then_inc(full_sem, 1)
                        for _ in range(2):
                            W.used(full_sem, B.base + h0 + (c + n + 1) // 2)
                    if e:
                        self.scatter_pe(pe, B, e - 1)
                    for i in range(self.NH):
                        B.freed(pe, h0 + i)
                    hid = m_hid[e % 2]
                    for i in range(4):
                        w = W.block(pe, [I["moe_w2_2"][0, e][:, i * 256:i * 256 + 256]], NFE)
                        bank = B.empty(pe, self.output(e) + i)
                        for k in range(NFE):
                            ins = pe.matmul(bank[:, 0:256], hid[:, k, :], w[:, k, :], start=(k == 0), stop=(k == NFE - 1))
                        ins.then_inc(full_sem, 1)
                        W.used(full_sem, B.base + self.output(e) + i + 1)
                self.scatter_pe(pe, B, NE - 1)

            def scatter_pe(self, pe, B, e):
                for i in range(4):
                    B.freed(pe, self.output(e) + i)
                for i in range(4):
                    bank = B.empty(pe, self.scatter(e) + i)
                    for j in range(2):
                        f = 2 * i + j
                        ins = pe.matmul(bank[:, j * LAT:j * LAT + LAT], m_yt[e % 2][:, f * P:f * P + P], m_slot[:, e, :],
                                        start=True, stop=True)
                    ins.then_inc(full_sem, 1)

            def act(self, act, B, ch):
                for i in range(4):
                    t, c = i // 2, i % 2
                    bank = B.full(act, self.XT + i)
                    act.activation(m_xt[:, t, c * 512:c * 512 + 512], bank[:, :], ACT.Copy).then_inc(*B.free(self.XT + i))
                for i in range(0, 16, 2):
                    c, k = i // KD, i % KD
                    bank = B.full(act, self.GA + i)
                    act.activation(m_x[:, k, c * 512:c * 512 + 512], bank[:, :], ACT.Copy).then_inc(*B.free(self.GA + i))
                n = 0
                for e in range(NE):
                    for i in range(self.NH):
                        bank = B.full(act, self.hidden(e) + i)
                        w = P * len(self.tiles(i))
                        if n >= 2:
                            act.wait_ge(*S("moe_rl").taken("act"))
                        act.activation(rl[n % 2][:, 0:w], bank[:, 0:w], ACT.Silu).then_inc(*S("hid").given())
                        n += 1
                    if e >= 2:
                        B.full(act, self.scatter(e - 2) + 3)
                    for i in range(4):
                        bank = B.full(act, self.output(e) + i)
                        act.activation(m_yt[e % 2][:, i * 256:i * 256 + 256], bank[:, 0:256], ACT.Copy)\
                           .then_inc(*B.free(self.output(e) + i))
                act.wait_ge(*S("moe_rl").taken("act", 2))

            def dve(self, dve, B, ch):
                if self.n == 1:
                    dve_link(ch, dve.tensor_scalar(place, place, -float(P), None, ALU.add))
                iota = const[:, C_IOTA:C_IOTA + P]
                for t in range(2):
                    for e in range(NE):
                        v, g = place[:, t, e:e + 1], routing[:, 4 + t, e:e + 1]
                        dve.tensor_scalar(m_sel[:, t, e * P:e * P + P], iota, v, None, ALU.is_equal)
                        dve.tensor_scalar(m_selg[:, t, e * P:e * P + P], iota, v, g, ALU.is_equal, ALU.mult)
                S("gate_cols").given()
                dve.drain().then_inc(S("gate_cols").sem, 1)
                for i in range(4):
                    bank = B.full(dve, self.ST + i)
                    dve.tensor_copy(m_slot[:, 2 * i:2 * i + 2, :], bank[:, :].rearrange("p (e t) -> p e t", e=2))\
                       .then_inc(*B.free(self.ST + i))
                for i in range(1, 16, 2):
                    c, k = i // KD, i % KD
                    bank = B.full(dve, self.GA + i)
                    dve.tensor_copy(m_x[:, k, c * 512:c * 512 + 512], bank[:, :]).then_inc(*B.free(self.GA + i))
                n = 0
                for e in range(NE + 1):
                    for i in range(self.NH if e < NE else 0):
                        w = P * len(self.tiles(i))
                        f = 2 * i
                        if i == 0 and e >= 2:
                            B.full(dve, self.output(e - 2) + 3)
                        dve.wait_ge(*S("hid").taken("dve"))
                        bank = B[self.hidden(e) + i]
                        dst = m_hid[e % 2][:, f:f + w // P, :].rearrange("p f t -> p (f t)")
                        dve.tensor_tensor(dst, bank[:, 256:256 + w], rl[n % 2][:, 0:w], ALU.mult)\
                           .then_inc(*S("moe_rl").given())
                        B.release(dve, self.hidden(e) + i)
                        n += 1
                    if e:
                        dve_link(ch, dve.drain())
                        for i in range(4):
                            bank = B.full(dve, self.scatter(e - 1) + i)
                            for j in range(2):
                                f = 2 * i + j
                                ins = dve.scalar_tensor_tensor(out=hT[:, f, 0:LAT], in0=bank[:, j * LAT:j * LAT + LAT],
                                                               scalar=mods[3][:, 40 + f, 0:1], in1=hT[:, f, 0:LAT],
                                                               op0=ALU.mult, op1=ALU.add)
                            ins.then_inc(*B.free(self.scatter(e - 1) + i))

        class Store(Stage):
            products = 4
            orow = arena_at(0, 2, D)

            def pe(self, pe, B):
                for i in range(4):
                    t, c = i // 2, i % 2
                    bank = B.empty(pe, i)
                    for j in range(4):
                        ins = pe.transpose(bank[:, j * P:j * P + P], hT[:, 4 * c + j, t * P:t * P + P], ident)
                    ins.then_inc(B.full_sem, 1)

            def dve(self, dve, B, ch):
                for i in range(4):
                    bank = B.full(dve, i)
                    dve.tensor_copy(self.orow[:, i // 2, 512 * (i % 2):512 * (i % 2) + 512], bank[:, :]).then_inc(*B.free(i))

            def act(self, act, B, ch):
                for t in range(2):
                    for c in range(2):
                        B.freed(act, 2 * t + c)
                    act.dma_start(out[0, t * P:t * P + P, :], self.orow[:, t, :]).then_inc(S("stored").sem, 16)
                act.wait_ge(S("stored").sem, 32)

        M = mods
        y8 = g_o
        stages = [Setup(), Ada(0, 0)]
        stages += [Modulate(M[0], 0, True, True), GlaProject(), GlaScan(), GlaGate(),
                   Residual(I["gla_w_out"][0], y8, KD, M[0], 2, TOK, True), LayerNorm(0, 0, TOK),
                   Modulate(M[0], 3, True, False)]
        hid = HiddenRelu2(I["ffn_w1"][0], TOK, AdaGuest(0, 1))
        stages += [hid, Residual(I["ffn_w2"][0], hid.hid, 32, M[0], 5, TOK, False, AdaGuest(1, 0)), LayerNorm(0, 1, TOK)]
        mark = {"b1l0": len(stages)}
        stages += [Modulate(M[1], 0, True, True), SsdGates()] + [SsdGroups()]
        stages += [SsdGate(), Residual(I["ssd_w_out"][0], s_y, 16, M[1], 2, LAT, True), LayerNorm(1, 0, LAT)]
        mark["b1l1m"] = len(stages)
        stages += [Modulate(M[1], 3, False, False)]
        hid = HiddenRelu2(I["ffn_w1"][1], LAT)
        stages += [hid, Residual(I["ffn_w2"][1], hid.hid, 32, M[1], 5, LAT, False), LayerNorm(1, 1, LAT)]
        mark["b1"] = len(stages)
        stages += [LoadCtx(), RmsNorm(M[2], 0, TOK), EvenProject(), BiasLoad(),
                   HeadNorm([(m_q[:, i, :], "ev_q_g_2", TOK) for i in range(4)]
                            + [(m_k[:, i, :], "ev_k_g_2", TOK) for i in range(4)], False),
                   Attention(even_items()), Residual(I["ev_w_out_2"][0], m_y, KD, M[2], 2, TOK, False)]
        mark["b2l0m"] = len(stages)
        stages += [RmsNorm(M[2], 3, TOK)]
        hid = HiddenSwiglu(I["ffn_w1_2"][0], I["ffn_w3_2"][0], TOK, AdaGuest(1, 1))
        stages += [hid, Residual(I["ffn_w2_2"][0], hid.hid, 22, M[2], 5, TOK, False)]
        mark["b2l0"] = len(stages)
        stages += [RmsNorm(M[3], 0, TOK), OddProject(),
                   HeadNorm([(m_q[:, i, 0:LAT], "od_cq_g_2" if i < 4 else "od_dq_g_2", LAT) for i in range(8)]
                            + [(m_k[:, 0, :], "od_ck_g_2", TOK)]
                            + [(m_k[:, 2 + i, :], "od_dk_g_2", TOK) for i in range(4)], True),
                   KeysAndLambda(), Attention(window_items()), Attention(diff_items(), lam_t), SubNorm(),
                   Residual(I["od_w_out_2"][0], m_y, KD, M[3], 2, LAT, False)]
        mark["b2l1m"] = len(stages)
        stages += [RmsNorm(M[3], 3, LAT), Router()]
        loop_at = len(stages) + 1
        stages += [Experts(0), Experts(1)]
        if stop is not None:
            stages, loop_at = stages[:mark[stop]], None
        stored_full, stored_free = sem("store_products"), [sem(f"store_bank_free{i}") for i in range(NBANK)]
        experts_done = {e: sem(f"experts_done_{e}") for e in ENG}
        block = ctx.enter_context(nc.Block())

        def part(name, st, eng, B, ch):
            if name == "pe":
                st.pe(eng, B)
            elif name == "act":
                st.act(eng, B, ch)
            else:
                st.dve(eng, B, ch)

        def run(name, eng, ch):
            B = Banks(banks_t, full_sem, free_sem)

            def stage(n, st):
                if n:
                    for other in ENG:
                        if other != name:
                            eng.wait_ge(stage_done[other], n)
                if st.guest:
                    st.guest.stage = n
                part(name, st, eng, B, ch)
                eng.drain().then_inc(stage_done[name], 1)
                B.base += st.products
            for n, st in enumerate(stages):
                if n == loop_at:
                    again = eng.value_load(overflow[0:1, 0:1], min_val=0, max_val=1)
                    with eng.If(again > 0):
                        stage(n, st)
                else:
                    stage(n, st)
            eng.drain().then_inc(experts_done[name], 1)
            for other in ENG:
                if other != name:
                    eng.wait_ge(experts_done[other], 1)
            part(name, Store(), eng, Banks(banks_t, stored_full, stored_free), None)

        @block.tensor
        def _(pe):
            run("pe", pe, None)

        @block.scalar
        def _(act):
            run("act", act, Chain(act, chain_sem["act"]))

        @block.vector
        def _(dve):
            run("dve", dve, Chain(dve, chain_sem["dve"]))

        @block.sync
        def _(sync):
            def stream(blocks):
                for n in blocks:
                    for before, guest, k in W.loads:
                        if before == n:
                            guest.load(sync, k)
                    pieces, kt = W.plan[n]
                    if n >= SLOTS:
                        sync.wait_ge(*W.done[n - SLOTS])
                    v = W.view(n)
                    at = 0
                    for piece in pieces:
                        c = piece.shape[1]
                        sync.dma_start(v[:, :, at:at + c], piece.rearrange("(k p) c -> p k c", p=P))\
                            .then_inc(W.landed[n % SLOTS], 16)
                        at += c
            stream(range(W.second_pass or len(W.plan)))
            if loop_at is not None:
                sync.wait_ge(*S("overflow_known").taken("sync"))
                again = sync.value_load(overflow[0:1, 0:1], min_val=0, max_val=1)
                with sync.If(again > 0):
                    stream(range(W.second_pass, len(W.plan)))


_OUTS = [((1, 256, 1024), "float32")]
_STOP = None


def kernel(**inputs):
    import concourse.bacc as _bacc
    from concourse.bass_utils import run_bass_kernel_spmd as _run

    nc = _bacc.Bacc("TRN2", target_bir_lowering=False, num_devices=1)
    arrays, aps = {}, {}
    for name, a in list(inputs.items()) + [("const", constants())]:
        a = np.ascontiguousarray(a)
        if a.size == 0 or name.startswith("hy_"):
            continue
        arrays[f"in_{name}"] = a
        aps[name] = nc.dram_tensor(f"in_{name}", a.shape, mybir.dt.from_np(a.dtype), kind="ExternalInput").ap()
    o = nc.dram_tensor("out_0", _OUTS[0][0], F32, kind="ExternalOutput").ap()
    build(nc, aps, o, _STOP)
    r = _run(nc, [arrays], core_ids=[0])
    return r.results[0]["out_0"]
```
